# Optimizing a Trainium2 kernel written in Bass

```python
import jax
import jax.numpy as jnp
from jax import lax
import numpy as np

D_MODEL = 1024
BATCH = 1
SEQ = 1024
DEPTH = 2
DEC_BATCH = 8
DEC_SEQ = 8
PAST_LEN = 2048
PAGE_SIZE = 128

N_MIXERS = 2
N_A = (DEPTH + 1) // 2
N_B = DEPTH // 2
MIX_WIDTH = 3 * D_MODEL // 4
MEM_WIDTH = D_MODEL - MIX_WIDTH
CHUNK = 128
GM_GROUP_DIM = 128
GM_GROUPS = MIX_WIDTH // GM_GROUP_DIM
SB_HEAD_DIM = 64
SB_HEADS = MIX_WIDTH // SB_HEAD_DIM
SB_BLOCK = 128
SB_BIAS_INIT = -5.0
MEM_TOKENS = 256
MEM_HEADS = 4
MEM_HEAD_DIM = MEM_WIDTH // MEM_HEADS
D_FF = 128 * ((8 * D_MODEL // 3 + 127) // 128)
CONV_W = 3
EPS = 1e-6

kernel_name = 'hybrid_gmlp_stickbreak_memxattn_convffn_step'

def rms_norm(x, gain):
    x32 = x.astype(jnp.float32)
    y = x32 * lax.rsqrt(jnp.mean(x32 * x32, axis=-1, keepdims=True) + EPS)
    return (y * gain.astype(jnp.float32)).astype(x.dtype)

def gmlp_mixer(h, w_in, v_gain, ws, bs):
    B, T, _ = h.shape
    proj = h @ w_in
    u = jax.nn.gelu(proj[..., :MIX_WIDTH])
    v = rms_norm(jax.nn.gelu(proj[..., MIX_WIDTH:2 * MIX_WIDTH]), v_gain)
    mq = proj[..., 2 * MIX_WIDTH:].reshape(B, T, MEM_HEADS, MEM_HEAD_DIM)
    n_chunks = -(-T // CHUNK)
    vc = jnp.pad(v, ((0, 0), (0, n_chunks * CHUNK - T), (0, 0)))
    vc = vc.reshape(B, n_chunks, CHUNK, GM_GROUPS, GM_GROUP_DIM)
    causal = jnp.tril(jnp.ones((CHUNK, CHUNK), dtype=bool))
    w = jnp.where(causal, ws, jnp.zeros_like(ws))
    mixed = jnp.einsum('gts,bcsge->bctge', w, vc) + bs.T[None, None, :, :, None]
    mixed = mixed.reshape(B, n_chunks * CHUNK, MIX_WIDTH)[:, :T]
    return u * mixed, mq, v

def stick_breaking(q, k, v, bias, q_pos, k_pos):
    z = jnp.einsum('bqhd,bkhd->bhqk', q, k, preferred_element_type=jnp.float32) * (SB_HEAD_DIM ** -0.5)
    z = z + bias.astype(jnp.float32)[None, :, None, None]
    mask = k_pos[None, :] < q_pos[:, None]
    log_keep = jnp.where(mask, jax.nn.log_sigmoid(-z), 0.0)
    log_after = lax.cumsum(log_keep, axis=3, reverse=True) - log_keep
    a = jnp.where(mask, jnp.exp(jax.nn.log_sigmoid(z) + log_after), 0.0)
    return jnp.einsum('bhqk,bkhd->bqhd', a.astype(v.dtype), v)

def sb_project(h, w_in):
    B, T, _ = h.shape
    p = h @ w_in
    q = p[..., :MIX_WIDTH].reshape(B, T, SB_HEADS, SB_HEAD_DIM)
    k = p[..., MIX_WIDTH:2 * MIX_WIDTH].reshape(B, T, SB_HEADS, SB_HEAD_DIM)
    v = p[..., 2 * MIX_WIDTH:3 * MIX_WIDTH].reshape(B, T, SB_HEADS, SB_HEAD_DIM)
    mq = p[..., 3 * MIX_WIDTH:].reshape(B, T, MEM_HEADS, MEM_HEAD_DIM)
    return q, k, v, mq

def sb_prompt(q, k, v, bias):
    B, T, H, Dh = q.shape
    nb = T // SB_BLOCK
    qb = jnp.moveaxis(q.reshape(B, nb, SB_BLOCK, H, Dh), 1, 0)
    k_pos = jnp.arange(T)

    def block(args):
        q_blk, start = args
        return stick_breaking(q_blk, k, v, bias, start + jnp.arange(SB_BLOCK), k_pos)

    out = lax.map(block, (qb, jnp.arange(nb) * SB_BLOCK))
    return jnp.moveaxis(out, 0, 1).reshape(B, T, H * Dh)

def sb_sample(q, k, v, bias, past_k, past_v):
    Bd, Tn, H, Dh = q.shape
    past_len = past_k.shape[1] * past_k.shape[2]
    k_all = jnp.concatenate([past_k.reshape(Bd, past_len, H, Dh), k], axis=1)
    v_all = jnp.concatenate([past_v.reshape(Bd, past_len, H, Dh), v], axis=1)
    q_pos = past_len + jnp.arange(Tn)
    k_pos = jnp.arange(past_len + Tn)
    return stick_breaking(q, k_all, v_all, bias, q_pos, k_pos).reshape(Bd, Tn, H * Dh)

def mem_kv(mem, gain, w_kv, k_gain):
    B, M, _ = mem.shape
    m = rms_norm(mem, gain) @ w_kv
    k = rms_norm(m[..., :MEM_WIDTH].reshape(B, M, MEM_HEADS, MEM_HEAD_DIM), k_gain)
    v = m[..., MEM_WIDTH:].reshape(B, M, MEM_HEADS, MEM_HEAD_DIM)
    return k, v

def mem_attend(q, mk, mv, q_gain):
    B, T = q.shape[0], q.shape[1]
    q = rms_norm(q, q_gain)
    s = jnp.einsum('bqhd,bmhd->bhqm', q, mk, preferred_element_type=jnp.float32) * (MEM_HEAD_DIM ** -0.5)
    p = jax.nn.softmax(s, axis=-1)
    return jnp.einsum('bhqm,bmhd->bqhd', p.astype(mv.dtype), mv).reshape(B, T, MEM_WIDTH)

def conv_ffn(x, gain, w_up, cw, cb, w_down, past_rows):
    T = x.shape[1]
    up = rms_norm(x, gain) @ w_up
    ext = jnp.concatenate([past_rows, up], axis=1)
    conv = cb + sum(cw[j] * ext[:, j:j + T] for j in range(CONV_W))
    out = (jax.nn.silu(conv[..., :D_FF]) * conv[..., D_FF:]) @ w_down
    return out, ext[:, ext.shape[1] - (CONV_W - 1):]

def setup_inputs(seed: int = 0) -> dict:
    key = jax.random.key(seed)
    k = jax.random.split(key, 32)
    f32 = jnp.float32

    def nrm(i, shape, scale):
        return jax.random.normal(k[i], shape, f32) * scale

    n_pages = PAST_LEN // PAGE_SIZE
    n_used = DEC_BATCH * n_pages
    n_pool = n_used + max(1, n_used // 4)
    page_table = jax.random.permutation(k[0], n_pool)[:n_used].reshape(DEC_BATCH, n_pages).astype(jnp.int32)
    d_in_a = 2 * MIX_WIDTH + MEM_WIDTH
    d_in_b = 3 * MIX_WIDTH + MEM_WIDTH
    return {
        'x_prompt': nrm(1, (BATCH, SEQ, D_MODEL), 1.0),
        'x_sample': nrm(2, (DEC_BATCH, DEC_SEQ, D_MODEL), 1.0),
        'cache_mem_k': nrm(3, (DEPTH, DEC_BATCH, MEM_TOKENS, MEM_HEADS, MEM_HEAD_DIM), 1.0),
        'cache_mem_v': nrm(4, (DEPTH, DEC_BATCH, MEM_TOKENS, MEM_HEADS, MEM_HEAD_DIM), 1.0),
        'cache_sb_k': nrm(5, (N_B, n_pool, PAGE_SIZE, SB_HEADS, SB_HEAD_DIM), 1.0),
        'cache_sb_v': nrm(6, (N_B, n_pool, PAGE_SIZE, SB_HEADS, SB_HEAD_DIM), 1.0),
        'state_ffn_conv': nrm(7, (DEPTH, DEC_BATCH, CONV_W - 1, 2 * D_FF), 1.0),
        'page_table': page_table,
        'mem_prompt': nrm(8, (BATCH, MEM_TOKENS, D_MODEL), 1.0),
        'norm_mix': 1.0 + nrm(9, (DEPTH, D_MODEL), 0.05),
        'norm_ffn': 1.0 + nrm(10, (DEPTH, D_MODEL), 0.05),
        'norm_mem': 1.0 + nrm(11, (DEPTH, D_MODEL), 0.05),
        'w_in_a': nrm(12, (N_A, D_MODEL, d_in_a), D_MODEL ** -0.5),
        'gm_v_norm': 1.0 + nrm(13, (N_A, MIX_WIDTH), 0.05),
        'gm_ws': nrm(14, (N_A, GM_GROUPS, CHUNK, CHUNK), CHUNK ** -0.5),
        'gm_bs': 1.0 + nrm(15, (N_A, GM_GROUPS, CHUNK), 0.1),
        'w_in_b': nrm(16, (N_B, D_MODEL, d_in_b), D_MODEL ** -0.5),
        'sb_bias': SB_BIAS_INIT + nrm(25, (N_B, SB_HEADS), 0.1),
        'w_mem_kv': nrm(17, (DEPTH, D_MODEL, 2 * MEM_WIDTH), D_MODEL ** -0.5),
        'mem_q_norm': 1.0 + nrm(18, (DEPTH, MEM_HEAD_DIM), 0.05),
        'mem_k_norm': 1.0 + nrm(19, (DEPTH, MEM_HEAD_DIM), 0.05),
        'w_out': nrm(20, (DEPTH, D_MODEL, D_MODEL), D_MODEL ** -0.5),
        'w_up': nrm(21, (DEPTH, D_MODEL, 2 * D_FF), D_MODEL ** -0.5),
        'conv_w': nrm(22, (DEPTH, CONV_W, 2 * D_FF), CONV_W ** -0.5),
        'conv_b': nrm(23, (DEPTH, 2 * D_FF), 0.01),
        'w_down': nrm(24, (DEPTH, D_FF, D_MODEL), D_FF ** -0.5),
    }

def reference(x_prompt, x_sample, cache_mem_k, cache_mem_v, cache_sb_k, cache_sb_v, state_ffn_conv, page_table, mem_prompt, norm_mix, norm_ffn, norm_mem, w_in_a, gm_v_norm, gm_ws, gm_bs, w_in_b, sb_bias, w_mem_kv, mem_q_norm, mem_k_norm, w_out, w_up, conv_w, conv_b, w_down):
    xp, xs = x_prompt, x_sample
    mem_k_p, mem_v_p = [], []
    sb_k_p, sb_v_p, sb_k_s, sb_v_s = [], [], [], []
    gm_v_s = []
    conv_p, conv_s = [], []
    for i in range(DEPTH):
        hp = rms_norm(xp, norm_mix[i])
        hs = rms_norm(xs, norm_mix[i])
        mkp, mvp = mem_kv(mem_prompt, norm_mem[i], w_mem_kv[i], mem_k_norm[i])
        mem_k_p.append(mkp)
        mem_v_p.append(mvp)
        if i % N_MIXERS == 0:
            a = i // N_MIXERS
            mix_p, mq_p, _ = gmlp_mixer(hp, w_in_a[a], gm_v_norm[a], gm_ws[a], gm_bs[a])
            mix_s, mq_s, v_new = gmlp_mixer(hs, w_in_a[a], gm_v_norm[a], gm_ws[a], gm_bs[a])
            gm_v_s.append(v_new)
        else:
            b = i // N_MIXERS
            qp, kp, vp, mq_p = sb_project(hp, w_in_b[b])
            qs, ks, vs, mq_s = sb_project(hs, w_in_b[b])
            mix_p = sb_prompt(qp, kp, vp, sb_bias[b])
            past_k = cache_sb_k[b][page_table]
            past_v = cache_sb_v[b][page_table]
            mix_s = sb_sample(qs, ks, vs, sb_bias[b], past_k, past_v)
            sb_k_p.append(kp)
            sb_v_p.append(vp)
            sb_k_s.append(ks)
            sb_v_s.append(vs)
        mem_out_p = mem_attend(mq_p, mkp, mvp, mem_q_norm[i])
        mem_out_s = mem_attend(mq_s, cache_mem_k[i], cache_mem_v[i], mem_q_norm[i])
        xp = xp + jnp.concatenate([mix_p, mem_out_p], axis=-1) @ w_out[i]
        xs = xs + jnp.concatenate([mix_s, mem_out_s], axis=-1) @ w_out[i]
        zero_rows = jnp.zeros((xp.shape[0], CONV_W - 1, 2 * D_FF), xp.dtype)
        fp, cp = conv_ffn(xp, norm_ffn[i], w_up[i], conv_w[i], conv_b[i], w_down[i], zero_rows)
        fs, cs = conv_ffn(xs, norm_ffn[i], w_up[i], conv_w[i], conv_b[i], w_down[i], state_ffn_conv[i])
        xp = xp + fp
        xs = xs + fs
        conv_p.append(cp)
        conv_s.append(cs)
    return (xp, xs, jnp.stack(mem_k_p), jnp.stack(mem_v_p), jnp.stack(sb_k_p), jnp.stack(sb_v_p), jnp.stack(sb_k_s), jnp.stack(sb_v_s), jnp.stack(gm_v_s), jnp.stack(conv_p), jnp.stack(conv_s))


_drawn_inputs = setup_inputs


def setup_inputs(seed=0):
    import zlib

    import numpy as np

    out = dict(_drawn_inputs(seed))
    spreads = {}
    factors = {'sb_bias': 52.72, 'mem_q_norm': 8.0, 'conv_b': 6.148, 'cache_sb_v': 8.0}
    for name, (base, spread) in spreads.items():
        noise = np.random.default_rng([zlib.crc32(name.encode()), seed]).standard_normal(out[name].shape)
        drawn = base * np.exp(spread * noise) if base else spread * noise
        out[name] = jnp.asarray(drawn.astype(out[name].dtype))
    for name, factor in factors.items():
        out[name] = (out[name] * factor).astype(out[name].dtype)
    return out
```

```python
from contextlib import ExitStack

import concourse.bass as bass
from concourse import mybir

F32 = mybir.dt.float32
F32R = mybir.dt.float32r
I32 = mybir.dt.int32
ALU = mybir.AluOpType
ACT = mybir.ActivationFunctionType
AX_X = mybir.AxisListType.X

P = 128
D = 1024
KT = D // P
SEQ = 1024
NPT = SEQ // P
NB, NQ = 8, 8
NS = NB * NQ
NT = NPT + 1
MIX = 768
MEMW = 256
MH, HD = 4, 64
M = 256
SH = 12
NPAIR = SH // 2
DFF = 2816
NFT = DFF // P
PAGES = 16
EPS = 1e-6
SM_CAP = 30.0
NEG = -1e30
UW = 256
NTOK = SEQ + NS
EXT = NQ + 2
SAMP0 = 2 + SEQ
FW = 1110
TG = FW // 3
CB = 3

ROWS = [P] * NPT + [NS]


class Counts:

    def __init__(self):
        self.turn = 0
        self.xn = 0
        self.norm = 0
        self.ssq = 0
        self.kv = 0


def build(nc, A, O, scratch):
    es = ExitStack()
    with es:
        place = [16512]
        top = nc.sbuf_usable_end // 32 * 32 - 576

        def sb_at(name, shape, off, dt=F32):
            return nc.alloc_sbuf_tensor_at(name, shape, dt, offset=off)

        def size(shape):
            n = 4
            for s in shape[1:]:
                n *= s
            return (n + 31) // 32 * 32

        def sb(name, shape, dt=F32):
            t = sb_at(name, shape, place[0], dt)
            place[0] += size(shape)
            return t

        class Region:

            def __init__(self, at):
                self.at = at

            def __call__(self, name, shape, dt=F32):
                t = sb_at(name, shape, self.at, dt)
                self.at += size(shape)
                assert self.at <= top, (name, self.at, top)
                return t

        x = sb("x", [P, NT, D])
        act_hi = sb("act_hi", [P, KT, FW], F32R)
        act_lo = sb("act_lo", [P, KT, FW], F32R)
        w_hi = sb("w_hi", [P, 2, KT, UW], F32R)
        w_lo = sb("w_lo", [P, 2, KT, UW], F32R)
        w_raw = sb("w_raw", [P, KT, UW])
        ident = sb("ident", [P, P])
        gains = sb("gains", [P, 48])
        cwb = sb("cwb", [P, 2, 4, 2 * NFT])
        qk_gain = sb("qk_gain", [P, 4, HD])
        ssq = sb("ssq", [P, NT])
        root = sb("root", [P, NT])
        inv = sb("inv", [P, NT])
        head_of = sb("head_of", [P, MH])
        query_of = sb("query_of", [P, NQ])
        batch_of = sb("batch_of", [P, 4])
        rep8 = sb("rep8", [NQ, NB, NQ])
        phase0 = place[0]

        r = Region(phase0)
        gains_raw = r("gains_raw", [48, P])
        conv_raw = r("conv_raw", [2 * NFT, 2, 4, P])
        slot16 = r("slot16", [P, 16])

        r = Region(phase0)
        mk_bd = r("mk_bd", [P, 2, 2 * M])
        mv_pad = r("mv_pad", [P, 2, MH, P])
        keep = r.at
        xn = r("xn", [P, 4, D])
        mem_hi = r("mem_hi", [P, KT, M], F32R)
        mem_lo = r("mem_lo", [P, KT, M], F32R)
        mem_raw = r("mem_raw", [P, 2, D])
        mkv = r("mkv", [P, 2, 2 * MEMW])
        kv_sq = r("kv_sq", [P, 2, MEMW])
        kv_stat = r("kv_stat", [P, 3, 8])
        stage = sb_at("stage", [P, 2, NT, UW], keep)

        r = Region(keep)
        v_all = r("v_all", [P, NT, MIX])
        gm_cat = r("gm_cat", [P, 4, MIX])
        w_t = r("w_t", [P, 6, P])
        ws_raw = sb_at("ws_raw", [P, 6, P], r.at)
        gm_gain = sb_at("gm_gain", [P, MIX], r.at)
        r.at += size([P, MIX])
        w_s = r("w_s", [NS, 6, NS])
        bias_raw = r("bias_raw", [6, P])
        bias_t = r("bias_t", [P, 6])
        bias_s = r("bias_s", [NS, 6])
        same_batch = r("same_batch", [NS, NS])
        gm_junk = r("gm_junk", [P, MIX])

        r = Region(keep)
        tri_neg = r("tri_neg", [P, P])
        ones_neg = r("ones_neg", [P, P])
        bias12 = r("bias12", [P, SH])
        new01 = r("new01", [NQ, SH, NQ])
        new_neg = r("new_neg", [NQ, SH, NQ])
        head12 = r("head12", [96, SH])
        mid = r.at
        sbq_raw = r("sbq_raw", [P, NPT, P])
        sbk_raw = r("sbk_raw", [P, NPT, P])
        sbv_raw = r("sbv_raw", [P, NPT, P])
        sb_v = r("sb_v", [P, NPT, P])
        sb_q = r("sb_q", [65, 2, SEQ])
        sb_k = r("sb_k", [65, 2, SEQ])
        stick = r("stick", [P, 3, 512])
        later = r("later", [P, 512])
        brk = r("brk", [P, 2, 512])
        tri01 = r("tri01", [P, P])
        diag_neg = r("diag_neg", [P, 512])
        r = Region(mid)
        pk_raw = r("pk_raw", [P, 2, MIX])
        pv_raw = r("pv_raw", [P, 2, 4, MIX])
        pk_t = r("pk_t", [P, 2, NPAIR, P])
        q_s = r("q_s", [P, NPAIR, NS])
        q_bd = r("q_bd", [P, NPAIR * 112])
        s_stick = r("s_stick", [P, 2, 4, 96])
        s_arg = r("s_arg", [P, 4, 96])
        s_out = sb_at("s_out", [96, MIX], mid + size([P, 2, MIX]) + size([P, 2, 4, MIX]))
        s_later = r("s_later", [P, 4, 96])
        s_zb = r("s_zb", [P, 4, 96])

        r = Region(keep)
        mq = r("mq", [P, NT, MEMW])
        mq_sq = sb_at("mq_sq", [P, NT, MEMW], r.at)
        r.at += size([P, NT, MEMW])
        mq_n = r("mq_n", [P, 2, MEMW])
        mq_t = r("mq_t", [P, 2, 2, P])
        mq_stat = r("mq_stat", [P, 3, NT * MH])
        sm_max = r("sm_max", [P, 2, MH])
        sm_sum = r("sm_sum", [P, 2, MH])
        sm_inv = r("sm_inv", [P, 2, MH])
        mid = r.at
        prob = r("prob", [P, 2, MH, M])
        prob_t = r("prob_t", [P, 2, 2, MH, P])
        r = Region(mid)
        mkc = r("mkc", [P, 4, 2, MEMW])
        mvc = r("mvc", [P, 4, 2, MEMW])
        mkc_t = sb_at("mkc_t", [P, 4, 2, M], keep + size([P, NT, MEMW]))
        mq_bd = r("mq_bd", [P, 4 * 288])
        prob_s = r("prob_s", [P, M])
        prob_st = r("prob_st", [P, 2, P])
        ms_out = r("ms_out", [P, MEMW])
        pick = r("pick", [P, 4, NQ])

        r = Region(phase0)
        up_u = r("up_u", [P, FW])
        up_g = r("up_g", [P, FW])
        cv_u = r("cv_u", [P, FW])
        cv_g = r("cv_g", [P, FW])
        d_hi = r("d_hi", [P, D], F32R)
        d_lo = r("d_lo", [P, D], F32R)
        d_raw = r("d_raw", [P, D])
        g_hi = r("g_hi", [P, 2, NTOK], F32R)
        g_lo = r("g_lo", [P, 2, NTOK], F32R)
        past_t = r("past_t", [P, NB, 2, 2 * NFT])
        tail_p = r("tail_p", [P, 2, 2 * NFT])
        tail_s = r("tail_s", [P, NB, 2, 2 * NFT])
        rows_st = r("rows_st", [P, 2, P])

        ps = es.enter_context(nc.psum_tensor("ps", [P, 8, 512], F32))

        def sem(name):
            return es.enter_context(nc.semaphore(name))

        filled, masked, set_ld, set_mm, set_ev = (sem(n) for n in ("filled", "masked", "set_ld", "set_mm", "set_ev"))
        x_ld, mem_ld = sem("x_ld"), sem("mem_ld")
        wr_ld, wh_ok, w_ok, w_used = (sem(n) for n in ("wr_ld", "wh_ok", "w_ok", "w_used"))
        ssq_ok, root_ok, inv_ok, xn_ok = (sem(n) for n in ("ssq_ok", "root_ok", "inv_ok", "xn_ok"))
        turned, turn_hi, turn_lo = (sem(n) for n in ("turned", "turn_hi", "turn_lo"))
        kv_mm, kv_ev, kv_st, kv_root, kv_tr, kv_ok, kv_out = (
            sem(n) for n in ("kv_mm", "kv_ev", "kv_st", "kv_root", "kv_tr", "kv_ok", "kv_out"))
        in_mm, in_ev, in_st, stage_free = (sem(n) for n in ("in_mm", "in_ev", "in_st", "stage_free"))
        out_mm, out_ev = sem("out_mm"), sem("out_ev")
        gm_ld, gm_gelu, gm_ssq, gm_root, gm_inv, gm_v, gm_set, gm_setmm, gm_mix, gm_ug, gm_cat_ok, gm_out = (
            sem(n) for n in ("gm_ld", "gm_gelu", "gm_ssq", "gm_root", "gm_inv", "gm_v", "gm_set", "gm_setmm",
                             "gm_mix", "gm_ug", "gm_cat_ok", "gm_out"))
        mq_ld, mq_step, mq_root, mq_tr, mq_tc, mq_s, mq_mx, mq_ex, mq_pr, mq_pt, mq_pc, mq_av, mq_hi, mq_lo = (
            sem(n) for n in ("mq_ld", "mq_step", "mq_root", "mq_tr", "mq_tc", "mq_s", "mq_mx", "mq_ex", "mq_pr",
                             "mq_pt", "mq_pc", "mq_av", "mq_hi", "mq_lo"))
        ms_ld, ms_tr, ms_tc, ms_q, ms_s, ms_step, ms_ex, ms_pt, ms_pc, ms_av, ms_ok, ms_mt, ms_hi, ms_lo = (
            sem(n) for n in ("ms_ld", "ms_tr", "ms_tc", "ms_q", "ms_s", "ms_step", "ms_ex", "ms_pt", "ms_pc",
                             "ms_av", "ms_ok", "ms_mt", "ms_hi", "ms_lo"))
        bp_ld, bp_free, bp_tr, bp_q, bp_k, bp_b, bp_z, bp_m, bp_e, bp_l, bp_L, bp_r, bp_s, bp_adj, bp_a, bp_av, bp_hi, \
            bp_lo, bp_set = (sem("bp_" + n) for n in ("ld", "free", "tr", "q", "k", "b", "z", "m", "e", "l", "L", "r",
                                                      "s", "adj", "a", "av", "hi", "lo", "set"))
        bs_q, bs_n, bs_tr, bs_tc, bs_bd, bs_z, bs_m, bs_e, bs_l, bs_L, bs_r, bs_s, bs_adj, bs_a, bs_av, \
            bs_o, bs_mt, bs_hi, bs_lo, bs_set = (sem("bs_" + n) for n in (
                "q", "n", "tr", "tc", "bd", "z", "m", "e", "l", "L", "r", "s", "adj", "a", "av", "o", "mt",
                "hi", "lo", "set"))
        up_mm, up_ev, past_in, cv_ok, silu_ok, gate_ok, gh_ok, g_ok, dr_ld, dh_ok, d_ok, dn_mm, dn_ev = (
            sem(n) for n in ("up_mm", "up_ev", "past_in", "cv_ok", "silu_ok", "gate_ok", "gh_ok", "g_ok", "dr_ld",
                             "dh_ok", "d_ok", "dn_mm", "dn_ev"))
        gm_u = [sem(f"gm_u{n}") for n in range(4)]
        bs_k, bs_v = [sem("bs_k0"), sem("bs_k1")], [sem("bs_v0"), sem("bs_v1")]
        st_ld, tl_out = [sem("st_ld0"), sem("st_ld1")], [sem("tl_out0"), sem("tl_out1")]
        pe_held, bs_half, bp_one, bs_zero = sem("pe_held"), sem("bs_half"), sem("bp_one"), sem("bs_zero")
        tap_ok, bp_tri, bs_tri, mq_nm = sem("tap_ok"), sem("bp_tri"), sem("bs_tri"), sem("mq_nm")
        st_mm, st_ev, tl_mm, tl_ev = (sem(n) for n in ("st_mm", "st_ev", "tl_mm", "tl_ev"))
        pad_ok, copied, y_out, mem_pad = sem("pad_ok"), sem("copied"), sem("y_out"), sem("mem_pad")

        proj = scratch

        KV_U, OUT_U, FFN_U = 2, 4, NFT
        IN_U = [7, 10]
        LU = [KV_U + IN_U[0] + OUT_U + FFN_U, KV_U + IN_U[1] + OUT_U + FFN_U]
        kv0 = [0, LU[0]]
        in0 = [kv0[l] + KV_U for l in (0, 1)]
        out0 = [in0[l] + IN_U[l] for l in (0, 1)]
        ffn0 = [out0[l] + OUT_U for l in (0, 1)]
        N_UNITS = sum(LU)
        win = [A["w_in_a"][0], A["w_in_b"][0]]

        def tok_cols(t):
            return slice(t * P, t * P + ROWS[t])

        def samp_ffn(tile, k):
            return tile[:, k, SAMP0:SAMP0 + NB * EXT].rearrange("p (b t) -> p b t", t=EXT)[:, :, 2:EXT]

        def load_unit(sp, n, src_a, src_b, dst_a, dst_b):
            if not (isinstance(n, int) and n == 0):
                sp.wait_ge(w_ok, n)
            sp.dma_start(dst_a, src_a).then_inc(wr_ld, 16)
            sp.dma_start(dst_b, src_b).then_inc(wr_ld, 16)

        def load_cols(sp, n, w, c0):
            v = w[:, bass.ds(c0, UW)].rearrange("(k p) f -> p k f", p=P)
            load_unit(sp, n, v[:, 0:4, :], v[:, 4:8, :], w_raw[:, 0:4, :], w_raw[:, 4:8, :])

        def split_hi(act, n, par):
            act.wait_ge(wr_ld, 32 * n + 32)
            if not (isinstance(n, int) and n < 2):
                act.wait_ge(w_used, n - 1)
            act.activation(w_hi[:, par], w_raw[:, :, :], ACT.Copy).then_inc(wh_ok, 1)

        def split_lo(dve, n, par):
            dve.wait_ge(wh_ok, n + 1)
            dve.tensor_tensor(w_lo[:, par], w_raw[:, :, :], w_hi[:, par].bitcast(F32), ALU.subtract).then_inc(w_ok, 1)

        def mm3(pe, out, ahi, alo, bhi, blo, first, last, **kw):
            pe.matmul(out, ahi, bhi, start=first, stop=False, **kw)
            pe.matmul(out, ahi, blo, start=False, stop=False, **kw)
            return pe.matmul(out, alo, bhi, start=False, stop=last, **kw)

        def pool_masks(pool, fills, selects):
            f0 = pool_masks.filled
            m0 = pool_masks.masked
            for t, v in fills:
                pool.memset(t, v).then_inc(filled, 1)
            pool_masks.filled += len(fills)
            pool.wait_ge(filled, f0 + len(fills))
            for n, (t, cmp, fill, base, pattern, mult) in enumerate(selects):
                if n:
                    pool.wait_ge(masked, m0 + n)
                pool.affine_select(out=t, in_=t, compare_op=cmp, fill=fill, base=base, pattern=pattern,
                                   channel_multiplier=mult).then_inc(masked, 1)
            pool_masks.masked += len(selects)

        pool_masks.filled = 0
        pool_masks.masked = 0

        SET_MASKS = 5

        def pool_setup(pool):
            for n, name in enumerate(("norm_mix", "norm_ffn", "norm_mem")):
                pool.dma_start(gains_raw[16 * n:16 * n + 16, :],
                               A[name].rearrange("l (k p) -> (l k) p", p=P)).then_inc(set_ld, 16)
            for l in (0, 1):
                pool.dma_start(conv_raw[:, l, 0:3, :],
                               A["conv_w"][l].rearrange("j (t f) -> t j f", f=P)).then_inc(set_ld, 16)
                pool.dma_start(conv_raw[:, l, 3, :],
                               A["conv_b"][l].rearrange("(t f) -> t f", f=P)).then_inc(set_ld, 16)
            for n, name in enumerate(("mem_q_norm", "mem_k_norm")):
                pool.dma_start(qk_gain[:, 2 * n:2 * n + 2, :].rearrange("p l d -> p (l d)"),
                               A[name].rearrange("l d -> (l d)").partition_broadcast(P)).then_inc(set_ld, 16)
            pool_masks(pool, [(ident[:, :], 0.0), (slot16[:, :], 1.0), (batch_of[:, :], 1.0)], [
                (ident[:, :], ALU.not_equal, 1.0, 0, [[-1, P]], 1),
                (slot16[:, :], ALU.is_ge, 0.0, 0, [[-8, 16]], 1),
                (slot16[:, :], ALU.is_ge, 0.0, 7, [[8, 16]], -1),
                (batch_of[:, :], ALU.is_ge, 0.0, 0, [[-32, 4]], 1),
                (batch_of[:, :], ALU.is_ge, 0.0, 31, [[32, 4]], -1),
            ])

        def pe_setup(pe):
            pe.wait_ge(set_ld, 16 * 9)
            pe.wait_ge(masked, SET_MASKS)
            pe.transpose(ps[:, 0, 0:48], gains_raw[:, :], ident[0:48, 0:48]).then_inc(set_mm, 1)
            for l in (0, 1):
                for j in range(4):
                    at = (l * 4 + j) * 2 * NFT
                    last = pe.transpose(ps[:, 1, at:at + 2 * NFT], conv_raw[:, l, j, :], ident[0:2 * NFT, 0:2 * NFT])
            last.then_inc(set_mm, 1)

        def dve_setup(dve):
            dve.memset(ssq[:, :], 1.0).then_inc(set_ev, 1)
            dve.wait_ge(masked, SET_MASKS)
            dve.tensor_reduce(head_of[:, :], slot16[:, :].rearrange("p (b h) -> p h b", h=MH), AX_X, ALU.add).then_inc(set_ev, 1)
            dve.tensor_reduce(query_of[:, :], ident[:, :].rearrange("p (j q) -> p q j", q=NQ), AX_X, ALU.add).then_inc(set_ev, 1)
            dve.tensor_copy(rep8[:, :, :], ident[0:NQ, 0:NQ].unsqueeze(1).broadcast_to([NQ, NB, NQ])).then_inc(set_ev, 1)
            dve.wait_ge(set_mm, 2)
            dve.tensor_copy(gains[:, :], ps[:, 0, 0:48]).then_inc(set_ev, 1)
            dve.tensor_copy(cwb[:, :, :, :].rearrange("p l j t -> p (l j t)"), ps[:, 1, 0:8 * 2 * NFT]).then_inc(set_ev, 1)

        SET_EV = 6

        def act_norm(act, c, src, tiles, wait_src):
            for t in tiles:
                wait_src(act, t)
                if c.ssq:
                    act.wait_ge(ssq_ok, c.ssq)
                act.activation(ps[0:ROWS[t], 6:8, :].rearrange("p a b -> p (a b)"), src(t), ACT.Square,
                               accum_out=ssq[0:ROWS[t], t:t + 1]).then_inc(ssq_ok, 1)
                c.ssq += 1
            act.wait_ge(ssq_ok, c.ssq)
            n = len(tiles)
            act.activation(root[:, 0:n], ssq[:, 0:n], ACT.Sqrt, scale=1.0 / D, bias=eps_ap[:, 0:1]).then_inc(root_ok, 1)

        def dve_inv(dve, c, n):
            c.norm += 1
            dve.wait_ge(root_ok, c.norm)
            dve.reciprocal(inv[:, 0:n], root[:, 0:n]).then_inc(inv_ok, 1)
            dve.wait_ge(inv_ok, c.norm)

        def dve_normed(dve, c, src, t):
            dve.tensor_scalar(xn[0:ROWS[t], t % 4, :], src(t), inv[0:ROWS[t], t:t + 1], None, ALU.mult).then_inc(xn_ok, 1)
            c.xn += 1

        def pe_turn(pe, c, src, group, ktiles, wait_src):
            wait_src(pe)
            for k in range(ktiles):
                bank = c.turn % 4
                if c.turn >= 4:
                    pe.wait_ge(turn_lo, c.turn - 3)
                for j, t in enumerate(group):
                    last = pe.transpose(ps[:, bank, j * P:j * P + ROWS[t]], src(t, k), ident[0:ROWS[t], 0:ROWS[t]])
                last.then_inc(turned, 1)
                c.turn += 1

        def turn_dst(dst, k, group, ffn):
            if group[0] == NPT:
                if ffn:
                    return samp_ffn(dst, k)
                return dst[:, k, SEQ:NTOK].rearrange("p (b t) -> p b t", t=NQ)
            a = group[0] * P + (2 if ffn else 0)
            return dst[:, k, a:a + P * len(group)]

        def turn_src(bank, group):
            if group[0] == NPT:
                return ps[:, bank, 0:NS].rearrange("p (b t) -> p b t", t=NQ)
            return ps[:, bank, 0:P * len(group)]

        def act_turn(act, c, dst, group, ktiles, gain0, ffn):
            for k in range(ktiles):
                bank = c.turn % 4
                act.wait_ge(turned, c.turn + 1)
                scale = 1.0 if gain0 is None else gains[:, gain0 + k:gain0 + k + 1]
                act.activation(turn_dst(dst, k, group, ffn), turn_src(bank, group), ACT.Copy, scale=scale).then_inc(turn_hi, 1)
                c.turn += 1

        def dve_turn(dve, c, hi, lo, group, ktiles, gain0, ffn):
            for k in range(ktiles):
                bank = c.turn % 4
                dve.wait_ge(turn_hi, c.turn + 1)
                scale = 1.0 if gain0 is None else gains[:, gain0 + k:gain0 + k + 1]
                dve.scalar_tensor_tensor(out=turn_dst(lo, k, group, ffn), in0=turn_src(bank, group), scalar=scale,
                                         in1=turn_dst(hi, k, group, ffn).bitcast(F32), op0=ALU.mult,
                                         op1=ALU.subtract).then_inc(turn_lo, 1)
                c.turn += 1

        GROUPS = [[0, 1, 2, 3], [4, 5, 6, 7], [8]]
        eps_ap = sb_at("eps_ap", [P, 1], top)

        def xt(t):
            return x[0:ROWS[t], t, :]

        def mt(t):
            return mem_raw[:, t, :]

        def xn_k(t, k):
            return xn[0:ROWS[t], t % 4, k * P:(k + 1) * P]

        def dve_norm_x(dve, c, gain0, ffn):
            dve_inv(dve, c, NT)
            for group in GROUPS:
                if group[0]:
                    dve.wait_ge(turned, c.turn)
                for t in group:
                    dve_normed(dve, c, xt, t)
                dve_turn(dve, c, act_hi, act_lo, group, KT, gain0, ffn)

        def pe_norm_x(pe, c):
            for group in GROUPS:
                c.xn += len(group)
                pe_turn(pe, c, xn_k, group, KT, lambda e: e.wait_ge(xn_ok, c.xn))

        def act_norm_x(act, c, gain0, ffn, wait_src):
            act_norm(act, c, xt, range(NT), wait_src)
            for group in GROUPS:
                act_turn(act, c, act_hi, group, KT, gain0, ffn)

        def pool_mem(pool, l):
            if l:
                pool.wait_ge(dn_ev, 2 + 18 * NFT)
                pool.wait_ge(tl_out[0], 16 * 4)
                pool.wait_ge(tl_out[1], 16 * 3)
            pool.dma_start(mem_raw[:, :, :], A["mem_prompt"][0].rearrange("(t p) d -> p t d", p=P)).then_inc(mem_ld, 16)

        def act_mem(act, c, l):
            act_norm(act, c, mt, range(2), lambda e, t: e.wait_ge(mem_ld, 16 * (l + 1)))
            act_turn(act, c, mem_hi, [0, 1], KT, 32 + 8 * l, False)

        def dve_mem(dve, c, l):
            dve_inv(dve, c, 2)
            for t in range(2):
                dve_normed(dve, c, mt, t)
            dve_turn(dve, c, mem_hi, mem_lo, [0, 1], KT, 32 + 8 * l, False)

        def pe_mem(pe, c, l):
            c.xn += 2
            pe_turn(pe, c, xn_k, [0, 1], KT, lambda e: e.wait_ge(xn_ok, c.xn))

        def pe_kv(pe, c, l):
            pe.wait_ge(turn_lo, c.turn)
            for u in range(2):
                n = kv0[l] + u
                pe.wait_ge(w_ok, n + 1)
                for t in range(2):
                    for k in range(KT):
                        last = mm3(pe, ps[:, 4 + 2 * u + t, 0:UW], mem_hi[:, k, t * P:(t + 1) * P],
                                   mem_lo[:, k, t * P:(t + 1) * P], w_hi[:, n % 2, k, :], w_lo[:, n % 2, k, :],
                                   k == 0, k == KT - 1)
                    last.then_inc(w_used if t else kv_mm, 1)

        def act_kv(act, c, l):
            for u in range(2):
                n = kv0[l] + u
                split_hi(act, n + 1, (n + 1) % 2)
                for t in range(2):
                    if t:
                        act.wait_ge(w_used, n + 1)
                    else:
                        act.wait_ge(kv_mm, 2 * l + u + 1)
                    act.activation(mkv[:, t, u * UW:(u + 1) * UW], ps[:, 4 + 2 * u + t, 0:UW], ACT.Copy).then_inc(kv_ev, 1)
            act.wait_ge(kv_st, 7 * l + 2)
            act.activation(kv_stat[:, 1, :], kv_stat[:, 0, :], ACT.Sqrt, scale=1.0 / HD, bias=eps_ap[:, 0:1]).then_inc(kv_root, 1)

        def dve_kv(dve, c, l):
            for u in range(2):
                split_lo(dve, kv0[l] + u + 1, (kv0[l] + u + 1) % 2)
            dve.memset(mk_bd[:, :, :], 0.0).then_inc(kv_ok, 1)
            dve.memset(mv_pad[:, :, :, :], 0.0).then_inc(kv_ok, 1)
            dve.wait_ge(kv_ev, 4 * l + 4)
            keys = mkv[:, :, 0:MEMW].rearrange("p t (h d) -> p t h d", d=HD)
            dve.tensor_tensor(kv_sq[:, :, :], mkv[:, :, 0:MEMW], mkv[:, :, 0:MEMW], ALU.mult).then_inc(kv_st, 1)
            dve.wait_ge(kv_st, 7 * l + 1)
            dve.tensor_reduce(kv_stat[:, 0, :].rearrange("p (t h) -> p t h", h=MH),
                              kv_sq[:, :, :].rearrange("p t (h d) -> p t h d", d=HD), AX_X, ALU.add).then_inc(kv_st, 1)
            dve.wait_ge(kv_root, l + 1)
            dve.reciprocal(kv_stat[:, 2, :], kv_stat[:, 1, :]).then_inc(kv_st, 1)
            dve.wait_ge(kv_st, 7 * l + 3)
            for t in range(2):
                dve.tensor_tensor(keys[:, t], keys[:, t],
                                  kv_stat[:, 2, 4 * t:4 * t + 4].unsqueeze(2).broadcast_to([P, MH, HD]),
                                  ALU.mult).then_inc(kv_st, 1)
            dve.wait_ge(kv_st, 7 * l + 5)
            for t in range(2):
                dve.tensor_tensor(keys[:, t], keys[:, t], qk_gain[:, 2 + l, :].unsqueeze(1).broadcast_to([P, MH, HD]),
                                  ALU.mult).then_inc(kv_st, 1)
            dve.wait_ge(kv_ok, 8 * l + 2)
            for hh in range(2):
                dve.tensor_copy(mv_pad[:, :, :, :].rearrange("p t (a b) c -> p t a b c", b=2)[:, :, :, hh, hh * HD:(hh + 1) * HD],
                                mkv[:, :, MEMW:].rearrange("p t (a b d) -> p t a b d", b=2, d=HD)[:, :, :, hh, :]).then_inc(kv_ok, 1)

        def dve_kv_turn(dve, l):
            for a in range(2):
                dve.wait_ge(kv_tr, 2 * l + a + 1)
                for hh in range(2):
                    dve.tensor_copy(mk_bd[hh * HD:(hh + 1) * HD, a, hh * M:(hh + 1) * M],
                                    ps[hh * HD:(hh + 1) * HD, 4 + a, 0:M]).then_inc(kv_ok, 1)

        def pe_kv_turn(pe, c, l):
            pe.wait_ge(kv_st, 7 * l + 7)
            for a in range(2):
                for t in range(2):
                    last = pe.transpose(ps[:, 4 + a, t * P:(t + 1) * P], mkv[:, t, a * P:(a + 1) * P], ident[:, :])
                last.then_inc(kv_tr, 1)
            pe.wait_ge(kv_ok, 8 * (l + 1))

        def pool_kv(pool, l):
            pool.wait_ge(kv_st, 7 * l + 7)
            pool.wait_ge(kv_ev, 4 * l + 4)
            for half, name in enumerate(("mem_k", "mem_v")):
                pool.dma_start(O[name][l, 0].rearrange("(t p) h d -> p t (h d)", p=P),
                               mkv[:, :, half * MEMW:(half + 1) * MEMW]).then_inc(kv_out, 16)

        def pe_in_unit(pe, l, u, n, par, t0):
            pe.wait_ge(w_ok, n + 1)
            for t in range(NT):
                pe.wait_ge(in_ev, t0 + t + 1)
                for k in range(KT):
                    last = mm3(pe, ps[0:ROWS[t], t % CB, 0:UW], act_hi[:, k, tok_cols(t)], act_lo[:, k, tok_cols(t)],
                               w_hi[:, par, k, :], w_lo[:, par, k, :], k == 0, k == KT - 1)
                last.then_inc(w_used if t == NT - 1 else in_mm, 1)

        def act_in_unit(act, l, u, n, par, t0, un):
            split_hi(act, n + 1, 1 - par)
            act.wait_ge(stage_free, un + 1)
            for t in range(NT):
                if t == NT - 1:
                    act.wait_ge(w_used, n + 1)
                else:
                    act.wait_ge(in_mm, 8 * un + t + 1)
                act.activation(stage[0:ROWS[t], par, t, :], ps[0:ROWS[t], t % CB, 0:UW], ACT.Copy).then_inc(in_ev, 1)

        def pool_in_unit(pool, l, u, par, un):
            pool.wait_ge(in_ev, CB + 9 * un + 9)
            pool.dma_start(proj[0:SEQ, bass.ds(u * UW, UW)].rearrange("(t p) f -> p t f", p=P),
                           stage[:, par, 0:NPT, :]).then_inc(in_st, 16)
            pool.dma_start(proj[SEQ:NTOK, bass.ds(u * UW, UW)], stage[0:NS, par, NPT, :]).then_inc(in_st, 16)
            pool.wait_ge(in_st, 32 * un + 32)
            pool.sem_inc(stage_free, 1)

        def in_units(eng, l, body):
            un0 = 0 if l == 0 else IN_U[0]
            with eng.Fori(0, IN_U[l] // 2) as i:
                for h in range(2):
                    body(i * 2 + h, i * 2 + (in0[l] + h), (in0[l] + h) % 2, i * 2 + (un0 + h))
            if IN_U[l] % 2:
                u = IN_U[l] - 1
                body(u, in0[l] + u, (in0[l] + u) % 2, un0 + u)

        IN_ST = [32 * IN_U[0], 32 * (IN_U[0] + IN_U[1])]

        def pool_gm_load(pool):
            pool.wait_ge(in_st, IN_ST[0])
            pool.wait_ge(kv_out, 32)
            pool.wait_ge(kv_tr, 2)
            pool_masks(pool, [(same_batch[:, :], 1.0)], [
                (same_batch[:, :].rearrange("p (b t) -> p b t", t=NQ), ALU.is_ge, 0.0, 0, [[-8, NB], [0, NQ]], 1),
                (same_batch[:, :].rearrange("p (b t) -> p b t", t=NQ), ALU.is_ge, 0.0, 7, [[8, NB], [0, NQ]], -1)])
            pool.dma_start(ws_raw[:, :, :], A["gm_ws"][0].rearrange("g t s -> t g s")).then_inc(gm_set, 16)
            pool.dma_start(bias_raw[:, :], A["gm_bs"][0]).then_inc(gm_set, 16)
            pool.dma_start(v_all[:, 0:NPT, :], proj[0:SEQ, MIX:2 * MIX].rearrange("(t p) f -> p t f", p=P)).then_inc(gm_ld, 16)
            pool.dma_start(v_all[0:NS, NPT, :], proj[SEQ:NTOK, MIX:2 * MIX]).then_inc(gm_ld, 16)
            pool.wait_ge(gm_set, 32)
            pool.affine_select(out=ws_raw[:, :, :], in_=ws_raw[:, :, :], compare_op=ALU.is_ge, fill=0.0, base=0,
                               pattern=[[0, 6], [-1, P]], channel_multiplier=1).then_inc(masked, 1)
            pool_masks.masked += 1
            GM["masked"] = pool_masks.masked
            pool.wait_ge(gm_setmm, 2)
            pool.dma_start(gm_gain[:, :], A["gm_v_norm"][0].partition_broadcast(P)).then_inc(gm_set, 16)
            for t in range(NT):
                if t >= 4:
                    pool.wait_ge(turned, TURN["gm"] + 6 * (t // 4))
                src = proj[t * P:t * P + ROWS[t], 0:MIX]
                pool.dma_start(gm_cat[0:ROWS[t], t % 4, :], src).then_inc(gm_u[t % 4], 16)
            pool.wait_ge(gm_v, NT)
            pool.dma_start(O["gm_v"][0].rearrange("b t f -> (b t) f"), v_all[0:NS, NPT, :]).then_inc(gm_out, 16)

        GM = {"masked": 0}
        TURN = {"gm": KT + 3 * KT}
        GM_MASKED = SET_MASKS + 2 + 1

        def pe_gm(pe, c):
            pe.wait_ge(masked, GM_MASKED)
            for g in range(6):
                last = pe.transpose(ps[:, 4 + g // 4, (g % 4) * P:(g % 4) * P + P], ws_raw[:, g, :], ident[:, :])
            last.then_inc(gm_setmm, 1)
            pe.transpose(ps[:, 6, 0:6], bias_raw[:, :], ident[0:6, 0:6]).then_inc(gm_setmm, 1)
            pe.wait_ge(gm_gelu, 3)
            rep = rep8[:, :, :].rearrange("p b q -> p (b q)")
            pe.matmul(ps[0:NS, 7, 0:6 * NQ], rep, w_t[0:NQ, :, 0:NQ], start=True, stop=True).then_inc(gm_setmm, 1)
            pe.matmul(ps[0:NS, 6, 8:14], rep, bias_t[0:NQ, :], start=True, stop=True).then_inc(gm_setmm, 1)
            pe.wait_ge(gm_gelu, 5)
            for group in GROUPS:
                for t in group:
                    pe.wait_ge(gm_v, t + 1)
                    if t >= 2:
                        pe.wait_ge(gm_cat_ok, 6 * (t - 1))
                    lhs = w_t if t < NPT else w_s
                    b = 4 + 2 * (t % 2)
                    for g in range(6):
                        last = pe.matmul(ps[0:ROWS[t], b + g // 4, (g % 4) * P:(g % 4) * P + P], lhs[0:ROWS[t], g, :],
                                         v_all[0:ROWS[t], t, g * P:(g + 1) * P], start=(g % 4 == 0), stop=True,
                                         skip_group_check=True)
                    last.then_inc(gm_mix, 1)
                pe_turn(pe, c, lambda t, k: gm_cat[0:ROWS[t], t % 4, k * P:(k + 1) * P], group, 6,
                        lambda e: e.wait_ge(gm_cat_ok, 6 * (group[-1] + 1)))

        def act_gm(act, c):
            act.wait_ge(gm_ld, 32)
            for t in range(NT):
                act.activation(v_all[0:ROWS[t], t, :], v_all[0:ROWS[t], t, :], ACT.Gelu_apprx_tanh).then_inc(gm_ssq, 1)
            for t in range(NT):
                act.wait_ge(gm_ssq, t + 1)
                act.wait_ge(ssq_ok, c.ssq)
                act.activation(gm_junk[0:ROWS[t], :], v_all[0:ROWS[t], t, :], ACT.Square,
                               accum_out=ssq[0:ROWS[t], t:t + 1]).then_inc(ssq_ok, 1)
                c.ssq += 1
            act.wait_ge(ssq_ok, c.ssq)
            act.activation(root[:, :], ssq[:, :], ACT.Sqrt, scale=1.0 / MIX, bias=eps_ap[:, 0:1]).then_inc(root_ok, 1)
            for group in GROUPS:
                for t in group:
                    act.wait_ge(gm_u[t % 4], 16 * (t // 4 + 1))
                    s = gm_cat[0:ROWS[t], t % 4, :]
                    act.activation(s, s, ACT.Gelu_apprx_tanh).then_inc(gm_ug, 1)
                act_turn(act, c, act_hi, group, 6, None, False)

        def dve_gm(dve, c):
            dve.wait_ge(gm_setmm, 2)
            dve.tensor_copy(w_t[:, 0:4, :].rearrange("p g t -> p (g t)"), ps[:, 4, :]).then_inc(gm_gelu, 1)
            dve.tensor_copy(w_t[:, 4:6, :].rearrange("p g t -> p (g t)"), ps[:, 5, 0:2 * P]).then_inc(gm_gelu, 1)
            dve.tensor_copy(bias_t[:, :], ps[:, 6, 0:6]).then_inc(gm_gelu, 1)
            dve.wait_ge(gm_setmm, 4)
            dve.tensor_tensor(w_s[:, :, :].rearrange("p g (b t) -> p g b t", t=NQ),
                              ps[0:NS, 7, 0:6 * NQ].rearrange("p (g t) -> p g t", t=NQ).unsqueeze(2).broadcast_to([NS, 6, NB, NQ]),
                              same_batch[:, :].rearrange("p (b t) -> p b t", t=NQ).unsqueeze(1).broadcast_to([NS, 6, NB, NQ]),
                              ALU.mult).then_inc(gm_gelu, 1)
            dve.tensor_copy(bias_s[:, :], ps[0:NS, 6, 8:14]).then_inc(gm_gelu, 1)
            dve_inv(dve, c, NT)
            dve.wait_ge(gm_set, 48)
            for group in GROUPS:
                for t in group:
                    v = v_all[0:ROWS[t], t, :]
                    dve.scalar_tensor_tensor(out=v, in0=v, scalar=inv[0:ROWS[t], t:t + 1], in1=gm_gain[0:ROWS[t], :],
                                             op0=ALU.mult, op1=ALU.mult).then_inc(gm_v, 1)
            for group in GROUPS:
                for t in group:
                    dve.wait_ge(gm_mix, t + 1)
                    dve.wait_ge(gm_ug, t + 1)
                    b = 4 + 2 * (t % 2)
                    bias = bias_t if t < NPT else bias_s
                    for g in range(6):
                        u = gm_cat[0:ROWS[t], t % 4, g * P:(g + 1) * P]
                        dve.scalar_tensor_tensor(out=u, in0=ps[0:ROWS[t], b + g // 4, (g % 4) * P:(g % 4) * P + P],
                                                 scalar=bias[0:ROWS[t], g:g + 1], in1=u, op0=ALU.add,
                                                 op1=ALU.mult).then_inc(gm_cat_ok, 1)
                dve_turn(dve, c, act_hi, act_lo, group, 6, None, False)

        UNITS = []
        for hh in range(2):
            for g in range(2):
                for kb in range(4 * g + 3, -1, -1):
                    UNITS.append((hh, g, kb, max(0, kb - 4 * g) * P, kb >= 4 * g, kb == 4 * g + 3))
        NU = len(UNITS)
        DIAG = [sum(u[4] for u in UNITS[:s]) for s in range(NU + 1)]

        def pool_bp(pool):
            pool.wait_ge(in_st, IN_ST[1])
            pool.wait_ge(kv_out, 64)
            pool.wait_ge(kv_tr, 4)
            for name, c0 in (("sb_k", MIX), ("sb_v", 2 * MIX)):
                pool.dma_start(O[name + "_p"][0, 0].rearrange("t h d -> t (h d)"), proj[0:SEQ, c0:c0 + MIX]).then_inc(copied, 16)
                pool.dma_start(O[name + "_s"][0].rearrange("b t h d -> (b t) (h d)"), proj[SEQ:NTOK, c0:c0 + MIX]).then_inc(copied, 16)
            pool.dma_start(bias12[:, :], A["sb_bias"][0].partition_broadcast(P)).then_inc(bp_set, 16)
            pool_masks(pool, [(tri_neg[:, :], -1.0), (ones_neg[:, :], -1.0), (tri01[:, :], 1.0), (diag_neg[:, :], 0.0),
                              (new01[:, :, :], 1.0), (new_neg[:, :, :], 0.0), (head12[:, :], 1.0)], [
                (tri_neg[:, :], ALU.is_ge, 0.0, 0, [[-1, P]], 1),
                (tri01[:, :], ALU.is_gt, 0.0, 0, [[1, P]], -1),
                (diag_neg[:, 0:P], ALU.is_gt, NEG, 0, [[1, P]], -1),
                (new01[:, :, :], ALU.is_gt, 0.0, 0, [[0, SH], [1, NQ]], -1),
                (new_neg[:, :, :], ALU.is_gt, NEG, 0, [[0, SH], [1, NQ]], -1),
                (head12[:, :], ALU.is_ge, 0.0, 0, [[-8, SH]], 1),
                (head12[:, :], ALU.is_ge, 0.0, 7, [[8, SH]], -1)])
            with pool.Fori(0, NPAIR) as i:
                pool.wait_ge(bp_free, i + 1)
                for dst, c0 in ((sbq_raw, 0), (sbk_raw, MIX), (sbv_raw, 2 * MIX)):
                    pool.dma_start(dst[:, :, :], proj[0:SEQ, bass.ds(i * P + c0, P)].rearrange("(t p) f -> p t f", p=P)).then_inc(bp_ld, 16)

        BP_MASKED = GM_MASKED + 7

        def pe_bp(pe):
            pe.wait_ge(masked, BP_MASKED)
            with pe.Fori(0, NPAIR) as i:
                pe.wait_ge(bp_ld, i * 48 + 48)
                for hh in range(2):
                    for n, raw in enumerate((sbq_raw, sbk_raw)):
                        for half in range(2):
                            if n == 1:
                                pe.wait_ge(bp_q, i * 4 + (2 * hh + half + 1))
                            elif hh == 1:
                                pe.wait_ge(bp_k, i * 4 + (half + 1))
                            pe.sem_inc(pe_held, 1)
                            for j in range(4):
                                last = pe.transpose(ps[0:HD, 4 + half, j * P:(j + 1) * P],
                                                    raw[:, 4 * half + j, hh * HD:(hh + 1) * HD], ident[:, :])
                            last.then_inc(bp_tr, 1)
                pe.wait_ge(bp_q, i * 4 + 4)
                pe.wait_ge(bp_b, i * 3 + 3)
                for s in range(NU + 2):
                    if s < NU:
                        hh, g, kb, c0, _, _ = UNITS[s]
                        pe.matmul(ps[:, s % 4, c0:512], sb_k[0:65, hh, kb * P:(kb + 1) * P],
                                  sb_q[0:65, hh, g * 512 + c0:(g + 1) * 512], start=True, stop=False,
                                  skip_group_check=True).then_inc(bp_z, 1)
                    if 1 <= s <= NU:
                        hh, g, kb, c0, diag, first = UNITS[s - 1]
                        pe.wait_ge(bp_L, i * NU + s)
                        if diag:
                            pe.wait_ge(bp_s, i * DIAG[NU] + DIAG[s])
                        mm = pe.matmul(ps[:, (s - 1) % 4, c0:512], tri_neg[:, :], stick[:, (s - 1) % 3, c0:512],
                                       start=False, stop=first, skip_group_check=True)
                        if not first:
                            cp = UNITS[s - 2][3]
                            pe.wait_ge(bp_r, i * NU + s)
                            mm = pe.matmul(ps[:, (s - 1) % 4, cp:512], ones_neg[:, :], later[:, cp:512], start=False,
                                           stop=True, skip_group_check=True)
                        mm.then_inc(bp_tri, 1)
                    if s >= 2:
                        hh, g, kb, c0, _, first = UNITS[s - 2]
                        pe.wait_ge(bp_a, i * NU + (s - 1))
                        if first:
                            pe.wait_ge(bp_lo, i * 4 + (2 * hh + g + 1))
                        pe.matmul(ps[0:HD, 6 + g, c0:512], sb_v[:, kb, hh * HD:(hh + 1) * HD], brk[:, s % 2, c0:512],
                                  start=first, stop=(kb == 0), skip_group_check=True).then_inc(bp_av, 1)

        def act_bp(act):
            with act.Fori(0, NPAIR) as i:
                for hh in range(2):
                    for half in range(2):
                        act.wait_ge(bp_tr, i * 8 + (4 * hh + half + 1))
                        act.activation(sb_q[0:HD, hh, half * 512:(half + 1) * 512], ps[0:HD, 4 + half, :], ACT.Copy,
                                       scale=HD ** -0.5).then_inc(bp_q, 1)

                def weights(s):
                    hh, g, kb, c0, diag, first = UNITS[s]
                    act.wait_ge(bp_av, i * NU + (s + 1))
                    if diag:
                        act.wait_ge(bp_adj, i * DIAG[NU] + DIAG[s + 1])
                        act.activation(brk[:, s % 2, c0:512], brk[:, s % 2, c0:512], ACT.Exp).then_inc(bp_a, 1)
                    else:
                        act.wait_ge(bp_tri, i * NU + (s + 1))
                        act.activation(brk[:, s % 2, c0:512], ps[:, s % 4, c0:512], ACT.Exp).then_inc(bp_a, 1)
                    if kb == 0:
                        evac(s)

                def evac(s):
                    hh, g, kb, c0, diag, first = UNITS[s]
                    act.wait_ge(bp_av, i * NU + (s + 3))
                    act.activation(act_hi[hh * HD:(hh + 1) * HD, bass.ds(i, 1), g * 512:(g + 1) * 512].rearrange("p a c -> p (a c)"),
                                   ps[0:HD, 6 + g, :], ACT.Copy).then_inc(bp_hi, 1)

                for s in range(NU + 1):
                    if s < NU:
                        c0 = UNITS[s][3]
                        b = stick[:, s % 3, c0:512]
                        act.wait_ge(bp_m, i * NU + (s + 1))
                        act.activation(b, b, ACT.Exp).then_inc(bp_e, 1)
                        act.wait_ge(bp_e, i * NU + (s + 1))
                        act.activation(b, b, ACT.Ln, bias=1.0).then_inc(bp_l, 1)
                    if s >= 1:
                        weights(s - 1)

        def dve_bp(dve):
            dve.memset(sb_k[HD:HD + 1, :, :], 1.0).then_inc(bp_one, 1)
            dve.wait_ge(bp_one, 1)
            dve.wait_ge(bp_set, 16)
            dve.wait_ge(masked, BP_MASKED)
            with dve.Fori(0, NPAIR) as i:
                for hh in range(2):
                    for half in range(2):
                        dve.wait_ge(bp_tr, i * 8 + (4 * hh + 2 + half + 1))
                        dve.tensor_copy(sb_k[0:HD, hh, half * 512:(half + 1) * 512], ps[0:HD, 4 + half, :]).then_inc(bp_k, 1)
                dve.wait_ge(bp_ld, i * 48 + 48)
                for hh in range(2):
                    dve.tensor_scalar(sb_q[HD:HD + 1, hh, :], sb_k[HD:HD + 1, hh, :], bias12[HD:HD + 1, bass.ds(i * 2 + hh, 1)],
                                      None, ALU.mult).then_inc(bp_b, 1)
                dve.tensor_copy(sb_v[:, :, :], sbv_raw[:, :, :]).then_inc(bp_b, 1)
                dve.wait_ge(bp_b, i * 3 + 3)
                dve.sem_inc(bp_free, 1)

                def stick_of(s):
                    hh, g, kb, c0, diag, first = UNITS[s]
                    b = stick[:, s % 3, c0:512]
                    z = ps[:, s % 4, c0:512]
                    dve.wait_ge(bp_z, i * NU + (s + 1))
                    dve.tensor_scalar(b, z, SM_CAP, None, ALU.min).then_inc(bp_m, 1)
                    dve.wait_ge(bp_l, i * NU + (s + 1))
                    dve.tensor_tensor(b, b, z, ALU.max).then_inc(bp_L, 1)
                    if diag:
                        dve.wait_ge(bp_L, i * NU + (s + 1))
                        d = stick[:, s % 3, c0:c0 + P]
                        dve.tensor_tensor(d, d, tri01[:, :], ALU.mult).then_inc(bp_s, 1)
                    if s:
                        dve.wait_ge(bp_tri, i * NU + s)
                    if first:
                        dve.memset(later[:, :], 0.0).then_inc(bp_r, 1)
                    else:
                        cp = UNITS[s - 1][3]
                        if UNITS[s - 1][4]:
                            dve.wait_ge(bp_s, i * DIAG[NU] + DIAG[s])
                        dve.wait_ge(bp_r, i * NU + s)
                        dve.tensor_tensor(later[:, cp:512], later[:, cp:512], stick[:, (s - 1) % 3, cp:512], ALU.add).then_inc(bp_r, 1)

                def adjust(s):
                    hh, g, kb, c0, diag, first = UNITS[s]
                    if diag:
                        dve.wait_ge(bp_tri, i * NU + (s + 1))
                        dve.wait_ge(bp_av, i * NU + (s + 1))
                        dve.scalar_tensor_tensor(out=brk[:, s % 2, c0:512], in0=ps[:, s % 4, c0:512], scalar=0.0,
                                                 in1=diag_neg[:, 0:512 - c0], op0=ALU.min, op1=ALU.add).then_inc(bp_adj, 1)
                    if kb == 0:
                        j = 2 * hh + g
                        dve.wait_ge(bp_hi, i * 4 + (j + 1))
                        dve.tensor_tensor(act_lo[hh * HD:(hh + 1) * HD, bass.ds(i, 1), g * 512:(g + 1) * 512].rearrange("p a c -> p (a c)"),
                                          ps[0:HD, 6 + g, :],
                                          act_hi[hh * HD:(hh + 1) * HD, bass.ds(i, 1), g * 512:(g + 1) * 512].rearrange("p a c -> p (a c)").bitcast(F32),
                                          ALU.subtract).then_inc(bp_lo, 1)

                for s in range(NU + 1):
                    if s >= 1 and UNITS[s - 1][2] != 0:
                        adjust(s - 1)
                    if s < NU:
                        stick_of(s)
                    if s >= 1 and UNITS[s - 1][2] == 0:
                        adjust(s - 1)

        HQ = SH * NQ
        page_t = sb_at("page_t", [1, NB * PAGES], top + 64, I32)

        def pool_bs(pool):
            pool.dma_start(page_t[:, :], A["page_table"].rearrange("b p -> (b p)").unsqueeze(0)).then_inc(bs_set, 16)
            pool.wait_ge(bp_lo, 2 + 4 * NPAIR)
            pool.dma_start(pk_raw[0:NS, 0, :], proj[SEQ:NTOK, 0:MIX]).then_inc(bs_q, 16)
            pool.wait_ge(bs_set, 16)
            with pool.Fori(0, NB) as b:
                pool.wait_ge(bs_tr, b * 17 + 1)
                pool.dma_start(pk_raw[0:NQ, 0, :], proj[bass.ds(b * NQ + SEQ, NQ), MIX:2 * MIX]).then_inc(bs_k[0], 16)
                for n in range(1, PAGES + 1):
                    if n >= 2:
                        pool.wait_ge(bs_tr, b * 17 + n)
                    page = pool.value_load(page_t[0:1, bass.ds(b * PAGES + (PAGES - n), 1)])
                    pool.dma_start(pk_raw[:, n % 2, :],
                                   A["cache_sb_k"][0, bass.ds(page, 1)].rearrange("a t h d -> t (a h d)")).then_inc(bs_k[n % 2], 16)

        def sp_bs(sp):
            sp.wait_ge(bs_set, 16)
            sp.wait_ge(bp_lo, 2 + 4 * NPAIR)
            with sp.Fori(0, NB) as b:
                sp.wait_ge(bs_av, b * 5 + 5)
                sp.dma_start(pv_raw[0:NQ, 0, 0, :], proj[bass.ds(b * NQ + SEQ, NQ), 2 * MIX:3 * MIX]).then_inc(bs_n, 16)
                for g in range(1, 5):
                    if g >= 2:
                        sp.wait_ge(bs_av, b * 5 + (4 + g))
                    for j in range(4):
                        page = sp.value_load(page_t[0:1, bass.ds(b * PAGES + (PAGES - 1 - 4 * (g - 1) - j), 1)])
                        sp.dma_start(pv_raw[:, g % 2, j, :],
                                     A["cache_sb_v"][0, bass.ds(page, 1)].rearrange("a t h d -> t (a h d)")).then_inc(bs_v[g % 2], 16)

        def pe_bs(pe):
            pe.wait_ge(bs_q, 16)
            for a in range(NPAIR):
                last = pe.transpose(ps[:, 0, a * NS:(a + 1) * NS], pk_raw[0:NS, 0, a * P:(a + 1) * P], ident[0:NS, 0:NS])
            last.then_inc(bs_tr, 1)
            with pe.Fori(0, NB) as b:

                def turn(n):
                    rows = P if n else NQ
                    pe.wait_ge(bs_k[n % 2], b * (16 * (9 - n % 2)) + 16 * (n // 2 + 1))
                    pe.wait_ge(bs_tc, b * 17 + max(n, 1))
                    if n == 0:
                        pe.sem_inc(pe_held, 1)
                    for a in range(NPAIR):
                        last = pe.transpose(ps[:, 2 * (n % 2) + a // 3, (a % 3) * P:(a % 3) * P + rows],
                                            pk_raw[0:rows, n % 2, a * P:(a + 1) * P], ident[0:rows, 0:rows])
                    last.then_inc(bs_tr, 1)

                def score(n):
                    rows = P if n else NQ
                    g = (n + 3) // 4
                    j = (n - 1) % 4 if n else 0
                    pe.wait_ge(bs_tc, b * 17 + n + 2)
                    if n == 0:
                        pe.sem_inc(pe_held, 1)
                    for a in range(NPAIR):
                        last = pe.matmul(ps[0:rows, 4 + g % 2, j * 96:(j + 1) * 96], pk_t[:, n % 2, a, 0:rows],
                                         q_bd[:, a * 96:(a + 1) * 96], start=(a == 0 and j == 0), stop=False,
                                         skip_group_check=True)
                    if n == 0 or j == 3:
                        last.then_inc(bs_z, 1)

                def carry(g):
                    pe.wait_ge(bs_L, b * 5 + g + 1)
                    rows, n = (P, 384) if g else (NQ, 96)
                    if g == 0:
                        pe.wait_ge(bs_s, b + 1)
                        pe.sem_inc(pe_held, 1)
                    mm = pe.matmul(ps[0:rows, 4 + g % 2, 0:n], tri_neg[0:rows, 0:rows],
                                   s_stick[0:rows, g % 2].rearrange("p j c -> p (j c)")[:, 0:n], start=False,
                                   stop=(g == 0), skip_group_check=True)
                    if g:
                        pe.wait_ge(bs_r, b * 17 + (1 + 4 * g))
                        mm = pe.matmul(ps[:, 4 + g % 2, 0:n], ones_neg[:, :],
                                       s_later[:, :, :].rearrange("p j c -> p (j c)"), start=False, stop=True,
                                       skip_group_check=True)
                    mm.then_inc(bs_tri, 1)

                def use(g):
                    pe.wait_ge(bs_a, b * 5 + g + 1)
                    if g == 0:
                        pe.wait_ge(bs_n, b * 16 + 16)
                    else:
                        pe.wait_ge(bs_v[g % 2], b * 128 + 64 * ((g + 1) // 2))
                    for j in range(4 if g else 1):
                        for c in range(2):
                            v = pv_raw[:, g % 2, j, c * 384:(c + 1) * 384] if g else pv_raw[0:NQ, 0, 0, c * 384:(c + 1) * 384]
                            rows = P if g else NQ
                            last = pe.matmul(ps[0:96, 6 + c, 0:384], s_arg[0:rows, j, :], v, start=(g == 0),
                                             stop=(g == 4 and j == 3))
                    last.then_inc(bs_av, 1)

                pe.wait_ge(bs_bd, b * 2 + 2)
                turn(0)
                turn(1)
                score(0)
                for g in range(5):
                    ns = range(4 * g + 1, 4 * g + 5) if g < 4 else []
                    for n in ns[:2]:
                        if n < PAGES:
                            turn(n + 1)
                        score(n)
                    carry(g)
                    for n in ns[2:]:
                        if n < PAGES:
                            turn(n + 1)
                        score(n)
                    use(g)
                pe.wait_ge(bs_o, b + 1)
                for a in range(NPAIR):
                    last = pe.matmul(ps[:, 5, a * NQ:(a + 1) * NQ], s_out[:, a * P:(a + 1) * P], query_of[0:96, :],
                                     start=True, stop=True, skip_group_check=True)
                last.then_inc(bs_mt, 1)
                pe.wait_ge(bs_lo, b + 1)

        def act_bs(act):
            act.wait_ge(bs_tr, 1)
            act.activation(q_s[:, :, :].rearrange("p a c -> p (a c)"), ps[:, 0, 0:NPAIR * NS], ACT.Copy,
                           scale=HD ** -0.5).then_inc(bs_tc, 1)
            with act.Fori(0, NB) as b:

                def keys(n):
                    rows = P if n else NQ
                    act.wait_ge(bs_tr, b * 17 + n + 2)
                    k = 2 * (n % 2)
                    act.activation(pk_t[:, n % 2, :, 0:rows].rearrange("p (u v) c -> p u v c", u=2),
                                   ps[:, k:k + 2, 0:384].rearrange("p u (v c) -> p u v c", c=P)[:, :, :, 0:rows],
                                   ACT.Copy).then_inc(bs_tc, 1)

                def sticks(g):
                    rows, n = (P, 4) if g else (NQ, 1)
                    s = s_stick[0:rows, g % 2, 0:n, :]
                    act.wait_ge(bs_m, b * 10 + 2 * g + 2)
                    act.activation(s, s, ACT.Exp).then_inc(bs_e, 1)
                    act.wait_ge(bs_e, b * 5 + g + 1)
                    act.activation(s, s, ACT.Ln, bias=1.0).then_inc(bs_l, 1)

                def weights(g):
                    rows, n = (P, 4) if g else (NQ, 1)
                    a = s_arg[0:rows, 0:n, :]
                    act.wait_ge(bs_adj, b * 6 + g + 2)
                    act.activation(a, a, ACT.Exp).then_inc(bs_a, 1)

                keys(0)
                keys(1)
                sticks(0)
                for g in range(5):
                    ns = range(4 * g + 1, 4 * g + 5) if g < 4 else []
                    for n in ns[:2]:
                        if n < PAGES:
                            keys(n + 1)
                    if g < 4:
                        weights(g)
                    for n in ns[2:]:
                        if n < PAGES:
                            keys(n + 1)
                    if g < 4:
                        sticks(g + 1)
                    else:
                        weights(g)
                act.wait_ge(bs_mt, b + 1)
                act.activation(act_hi[:, 0:NPAIR, bass.ds(b * NQ + SEQ, NQ)],
                               ps[:, 5, 0:NPAIR * NQ].rearrange("p (a q) -> p a q", q=NQ), ACT.Copy).then_inc(bs_hi, 1)

        def dve_bs(dve):
            dve.wait_ge(bp_lo, 2 + 4 * NPAIR)
            dve.memset(q_bd[:, :], 0.0).then_inc(bs_zero, 1)
            dve.wait_ge(bs_tc, 1)
            dve.wait_ge(bs_zero, 1)
            with dve.Fori(0, NB) as b:

                def bias(n, rows):
                    v = bias12[0:rows, :].unsqueeze(2).broadcast_to([rows, SH, NQ])
                    return v.unsqueeze(1).broadcast_to([rows, n, SH, NQ])

                def split(t, n):
                    return t.rearrange("p j (h q) -> p j h q", q=NQ)

                def sticks(g):
                    rows, n = (P, 4) if g else (NQ, 1)
                    z = ps[0:rows, 4 + g % 2, 0:96 * n].rearrange("p (j h q) -> p j h q", h=SH, q=NQ)
                    zb = s_zb[0:rows, 0:n, :]
                    s = s_stick[0:rows, g % 2, 0:n, :]
                    dve.wait_ge(bs_z, b * 5 + g + 1)
                    dve.tensor_tensor(split(zb, n), z, bias(n, rows), ALU.add).then_inc(bs_m, 1)
                    dve.wait_ge(bs_m, b * 10 + 2 * g + 1)
                    dve.tensor_scalar(s, zb, SM_CAP, None, ALU.min).then_inc(bs_m, 1)
                    dve.wait_ge(bs_l, b * 5 + g + 1)
                    dve.tensor_tensor(s, s, zb, ALU.max).then_inc(bs_L, 1)
                    dve.wait_ge(bs_L, b * 5 + g + 1)
                    if g == 0:
                        dve.tensor_tensor(s, s, new01[:, :, :].rearrange("p h q -> p (h q)").unsqueeze(1), ALU.mult).then_inc(bs_s, 1)
                    else:
                        dve.wait_ge(bs_tri, b * 5 + g)
                        r0 = b * 17 + (0 if g == 1 else 1 + 4 * (g - 1))
                        if g == 1:
                            dve.wait_ge(bs_s, b + 1)
                            dve.memset(s_later[:, 0, :], 0.0).then_inc(bs_r, 1)
                            dve.wait_ge(bs_r, r0 + 1)
                            dve.tensor_copy(s_later[0:NQ, 0, :], s_stick[0:NQ, 0, 0, :]).then_inc(bs_r, 1)
                            r0 = r0 + 1
                        else:
                            dve.tensor_tensor(s_later[:, 0, :], s_later[:, 3, :], s_stick[:, (g - 1) % 2, 3, :],
                                              ALU.add).then_inc(bs_r, 1)
                        for j in range(1, 4):
                            dve.wait_ge(bs_r, r0 + j)
                            dve.tensor_tensor(s_later[:, j, :], s_later[:, j - 1, :], s_stick[:, g % 2, j - 1, :],
                                              ALU.add).then_inc(bs_r, 1)

                def adjust(g):
                    rows, n = (P, 4) if g else (NQ, 1)
                    z = ps[0:rows, 4 + g % 2, 0:96 * n].rearrange("p (j h q) -> p j h q", h=SH, q=NQ)
                    a = s_arg[0:rows, 0:n, :]
                    dve.wait_ge(bs_tri, b * 5 + g + 1)
                    dve.wait_ge(bs_av, b * 5 + g + 5)
                    dve.tensor_tensor(split(a, n), z, bias(n, rows), ALU.add).then_inc(bs_adj, 1)
                    if g == 0:
                        dve.wait_ge(bs_adj, b * 6 + 1)
                        dve.scalar_tensor_tensor(out=a[:, 0, :], in0=a[:, 0, :], scalar=0.0,
                                                 in1=new_neg[:, :, :].rearrange("p h q -> p (h q)"), op0=ALU.min,
                                                 op1=ALU.add).then_inc(bs_adj, 1)

                for hh in range(2):
                    rows = slice(hh * HD, (hh + 1) * HD)
                    dve.tensor_copy(q_bd[rows, :].rearrange("p (a c) -> p a c", c=112)[:, :, hh * NQ:(hh + 1) * NQ],
                                    q_s[rows, :, bass.ds(b * NQ, NQ)]).then_inc(bs_bd, 1)
                sticks(0)
                for g in range(5):
                    adjust(g)
                    if g < 4:
                        sticks(g + 1)
                dve.wait_ge(bs_av, b * 5 + 10)
                for c in range(2):
                    dve.tensor_tensor(s_out[:, c * 384:(c + 1) * 384].rearrange("p (h d) -> p h d", d=HD),
                                      ps[0:96, 6 + c, 0:384].rearrange("p (h d) -> p h d", d=HD),
                                      head12[:, 6 * c:6 * c + 6].unsqueeze(2).broadcast_to([96, 6, HD]), ALU.mult).then_inc(bs_half if c == 0 else bs_o, 1)
                dve.wait_ge(bs_hi, b + 1)
                cols = bass.ds(b * NQ + SEQ, NQ)
                dve.tensor_tensor(act_lo[:, 0:NPAIR, cols], ps[:, 5, 0:NPAIR * NQ].rearrange("p (a q) -> p a q", q=NQ),
                                  act_hi[:, 0:NPAIR, cols].bitcast(F32), ALU.subtract).then_inc(bs_lo, 1)


        def wait_attended(eng, l):
            if l == 0:
                eng.wait_ge(turn_lo, TURN["gm"] + 18)
                eng.wait_ge(gm_out, 16)
            else:
                eng.wait_ge(bs_lo, NB)

        MQC = [2304, 1024]

        def pool_mq(pool, l):
            wait_attended(pool, l)
            q0 = (2 * MIX, 3 * MIX)[l]
            pool.wait_ge(mem_pad, l + 1)
            pool.dma_start(mq[:, 0:NPT, :], proj[0:SEQ, q0:q0 + MEMW].rearrange("(t p) f -> p t f", p=P)).then_inc(mq_ld, 16)
            pool.dma_start(mq[0:NS, NPT, :], proj[SEQ:NTOK, q0:q0 + MEMW]).then_inc(mq_ld, 16)

        def dve_mq(dve, l):
            wait_attended(dve, l)
            dve.memset(mq[HD:P, NPT, :], 1.0).then_inc(mem_pad, 1)
            dve.wait_ge(mq_ld, 32 * l + 32)
            s0 = 4 * l
            heads = mq[:, :, :].rearrange("p t (h d) -> p (t h) d", d=HD)
            dve.tensor_tensor(mq_sq[:, :, :], mq[:, :, :], mq[:, :, :], ALU.mult).then_inc(mq_step, 1)
            dve.wait_ge(mq_step, s0 + 1)
            dve.tensor_reduce(mq_stat[:, 0, :], mq_sq[:, :, :].rearrange("p t (h d) -> p (t h) d", d=HD), AX_X,
                              ALU.add).then_inc(mq_step, 1)
            dve.wait_ge(mq_root, l + 1)
            dve.reciprocal(mq_stat[:, 2, :], mq_stat[:, 1, :]).then_inc(mq_step, 1)
            dve.wait_ge(mq_step, s0 + 3)
            dve.tensor_tensor(heads, heads, mq_stat[:, 2, :].unsqueeze(2).broadcast_to([P, NT * MH, HD]),
                              ALU.mult).then_inc(mq_step, 1)
            dve.wait_ge(mq_step, s0 + 4)
            gain = qk_gain[:, l, :].unsqueeze(1).broadcast_to([P, MH, HD])
            T0 = 8 * l
            with dve.Fori(0, NPT // 2) as i:
                for h in range(2):
                    dve.tensor_tensor(mq_n[:, h, :].rearrange("p (h d) -> p h d", d=HD),
                                      mq[:, bass.ds(i * 2 + h, 1), :].rearrange("p a (h d) -> p (a h) d", d=HD), gain,
                                      ALU.mult).then_inc(mq_nm, 1)
                for h in range(2):
                    t = i * 2 + (T0 + h)
                    b = 2 + 2 * h
                    dve.wait_ge(mq_s, t + 1)
                    dve.tensor_reduce(sm_max[:, h, :], ps[:, b:b + 2, :].rearrange("p a (h m) -> p (a h) m", m=M), AX_X,
                                      ALU.max).then_inc(mq_mx, 1)
                    dve.wait_ge(mq_mx, t * 2 + 1)
                    dve.tensor_scalar(sm_max[:, h, :], sm_max[:, h, :], -HD ** -0.5, None, ALU.mult).then_inc(mq_mx, 1)
                for h in range(2):
                    t = i * 2 + (T0 + h)
                    dve.wait_ge(mq_ex, t * 4 + 4)
                    dve.reciprocal(sm_inv[:, h, :], sm_sum[:, h, :]).then_inc(mq_pr, 1)
                    dve.wait_ge(mq_pr, t * 2 + 1)
                    dve.tensor_tensor(prob[:, h, :, :], prob[:, h, :, :],
                                      sm_inv[:, h, :].unsqueeze(2).broadcast_to([P, MH, M]), ALU.mult).then_inc(mq_pr, 1)
                for h in range(2):
                    t = i * 2 + (T0 + h)
                    cols = bass.ds(i * (2 * P) + h * P, P)
                    dve.wait_ge(mq_hi, t + 1)
                    dve.tensor_tensor(act_lo[:, NPAIR:KT, cols], ps[:, 6 + h, 0:2 * P].rearrange("p (a c) -> p a c", c=P),
                                      act_hi[:, NPAIR:KT, cols].bitcast(F32), ALU.subtract).then_inc(mq_lo, 1)

        def act_mq(act, l):
            act.wait_ge(mq_step, 4 * l + 2)
            act.activation(mq_stat[:, 1, :], mq_stat[:, 0, :], ACT.Sqrt, scale=1.0 / HD, bias=eps_ap[:, 0:1]).then_inc(mq_root, 1)
            T0 = 8 * l
            with act.Fori(0, NPT // 2) as i:
                for h in range(2):
                    t = i * 2 + (T0 + h)
                    act.wait_ge(mq_tr, t + (l + 1))
                    act.activation(mq_t[:, h, :, :].rearrange("p a c -> p (a c)"), ps[:, h, 0:2 * P], ACT.Copy).then_inc(mq_tc, 1)
                for h in range(2):
                    t = i * 2 + (T0 + h)
                    act.wait_ge(mq_mx, t * 2 + 2)
                    for hd in range(MH):
                        act.activation(prob[:, h, hd, :], ps[:, 2 + 2 * h + hd // 2, (hd % 2) * M:(hd % 2 + 1) * M], ACT.Exp,
                                       bias=sm_max[:, h, hd:hd + 1], scale=HD ** -0.5,
                                       accum_out=sm_sum[:, h, hd:hd + 1]).then_inc(mq_ex, 1)
                for h in range(2):
                    t = i * 2 + (T0 + h)
                    act.wait_ge(mq_pt, t + 1)
                    act.activation(prob_t[:, h].rearrange("p a h c -> p a (h c)"), ps[:, 2 * h:2 * h + 2, :], ACT.Copy).then_inc(mq_pc, 1)
                for h in range(2):
                    t = i * 2 + (T0 + h)
                    cols = bass.ds(i * (2 * P) + h * P, P)
                    act.wait_ge(mq_av, t + 1)
                    act.activation(act_hi[:, NPAIR:KT, cols], ps[:, 6 + h, 0:2 * P].rearrange("p (a c) -> p a c", c=P),
                                   ACT.Copy).then_inc(mq_hi, 1)

        def pe_mq(pe, l):
            T0 = 8 * l
            with pe.Fori(0, NPT // 2) as i:
                for h in range(2):
                    t = i * 2 + (T0 + h)
                    pe.wait_ge(mq_nm, t + (l + 1))
                    for a in range(2):
                        last = pe.transpose(ps[:, h, a * P:(a + 1) * P], mq_n[:, h, a * P:(a + 1) * P], ident[:, :])
                    last.then_inc(mq_tr, 1)
                    pe.wait_ge(mq_tc, t + (l + 1))
                    for a in range(2):
                        last = pe.matmul(ps[:, 2 + 2 * h + a, :], mq_t[:, h, a, :], mk_bd[:, a, :], start=True, stop=True)
                    last.then_inc(mq_s, 1)
                for h in range(2):
                    t = i * 2 + (T0 + h)
                    pe.wait_ge(mq_pr, t * 2 + 2)
                    for m in range(2):
                        for hd in range(MH):
                            last = pe.transpose(ps[:, 2 * h + m, hd * P:(hd + 1) * P], prob[:, h, hd, m * P:(m + 1) * P], ident[:, :])
                    last.then_inc(mq_pt, 1)
                    pe.wait_ge(mq_pc, t + 1)
                    pe.wait_ge(mq_lo, t + 1)
                    for a in range(2):
                        for n in range(4):
                            hd, m = 2 * a + n // 2, n % 2
                            last = pe.matmul(ps[:, 6 + h, a * P:(a + 1) * P], mv_pad[:, m, hd, :], prob_t[:, h, m, hd, :],
                                             start=(n == 0), stop=(n == 3), skip_group_check=True)
                    last.then_inc(mq_av, 1)

        def sp_ms(sp, l):
            sp.wait_ge(mq_lo, 2 + 8 * (l + 1))
            for gr in range(2):
                G = 2 * l + gr
                if gr:
                    sp.wait_ge(ms_tr, 4 * G)
                    sp.wait_ge(ms_av, G)
                for b in range(4):
                    for dst, name in ((mkc, "cache_mem_k"), (mvc, "cache_mem_v")):
                        sp.dma_start(dst[:, b], A[name][l, 4 * gr + b].rearrange("(t p) h d -> p t (h d)", p=P)).then_inc(ms_ld, 16)

        def dve_ms(dve, l):
            gain = qk_gain[0:NS, l, :].unsqueeze(1).broadcast_to([NS, MH, HD])
            dve.tensor_tensor(mq_n[0:NS, 0, :].rearrange("p (h d) -> p h d", d=HD),
                              mq[0:NS, NPT, :].rearrange("p (h d) -> p h d", d=HD), gain, ALU.mult).then_inc(mq_nm, 1)
            dve.memset(mq_bd[:, :], 0.0).then_inc(ms_q, 1)
            dve.tensor_tensor(pick[:, :, :], batch_of[:, :].unsqueeze(2).broadcast_to([P, 4, NQ]),
                              query_of[:, :].unsqueeze(1).broadcast_to([P, 4, NQ]), ALU.mult).then_inc(ms_q, 1)
            dve.wait_ge(mq_tc, 9 * l + 9)
            for gr in range(2):
                G = 2 * l + gr
                if gr:
                    dve.wait_ge(ms_s, G)
                dve.wait_ge(ms_q, 10 * l + 2 + 4 * gr)
                for a in range(2):
                    for hh in range(2):
                        rows = slice(hh * HD, (hh + 1) * HD)
                        c = a * P + (2 * a + hh) * NQ
                        dve.tensor_copy(mq_bd[rows, :].rearrange("p (b c) -> p b c", c=288)[:, :, c:c + NQ],
                                        mq_t[rows, 0, a, gr * 32:gr * 32 + 32].rearrange("p (b q) -> p b q", q=NQ)).then_inc(ms_q, 1)
                s0 = 4 * G
                dve.wait_ge(ms_s, G + 1)
                dve.tensor_reduce(sm_max[:, 0, 0:1], ps[:, 4, 0:M], AX_X, ALU.max).then_inc(ms_step, 1)
                dve.wait_ge(ms_step, s0 + 1)
                dve.tensor_scalar(sm_max[:, 0, 0:1], sm_max[:, 0, 0:1], -HD ** -0.5, None, ALU.mult).then_inc(ms_step, 1)
                dve.wait_ge(ms_ex, G + 1)
                dve.reciprocal(sm_inv[:, 0, 0:1], sm_sum[:, 0, 0:1]).then_inc(ms_step, 1)
                dve.wait_ge(ms_step, s0 + 3)
                dve.tensor_scalar(prob_s[:, :], prob_s[:, :], sm_inv[:, 0, 0:1], None, ALU.mult).then_inc(ms_step, 1)
                dve.wait_ge(ms_av, G + 1)
                dve.tensor_tensor(ms_out[:, :].rearrange("p (h d) -> p h d", d=HD),
                                  ps[:, 6, 0:MEMW].rearrange("p (h d) -> p h d", d=HD),
                                  head_of[:, :].unsqueeze(2).broadcast_to([P, MH, HD]), ALU.mult).then_inc(ms_ok, 1)
                dve.wait_ge(ms_hi, G + 1)
                cols = slice(SEQ + 32 * gr, SEQ + 32 * gr + 32)
                dve.tensor_tensor(act_lo[:, NPAIR:KT, cols], ps[:, 7, 0:64].rearrange("p (a c) -> p a c", c=32),
                                  act_hi[:, NPAIR:KT, cols].bitcast(F32), ALU.subtract).then_inc(ms_lo, 1)

        def act_ms(act, l):
            act.wait_ge(mq_tr, 9 * l + 9)
            act.activation(mq_t[:, 0, :, 0:NS], ps[:, 0, 0:2 * NS].rearrange("p (a c) -> p a c", c=NS), ACT.Copy).then_inc(mq_tc, 1)
            for gr in range(2):
                G = 2 * l + gr
                if gr:
                    act.wait_ge(ms_s, G)
                for b in range(4):
                    act.wait_ge(ms_tr, 4 * G + b + 1)
                    act.activation(mkc_t[:, b, :, :].rearrange("p a m -> p (a m)"), ps[:, b, :], ACT.Copy).then_inc(ms_tc, 1)
                act.wait_ge(ms_step, 4 * G + 2)
                act.activation(prob_s[:, :], ps[:, 4, 0:M], ACT.Exp, bias=sm_max[:, 0, 0:1], scale=HD ** -0.5,
                               accum_out=sm_sum[:, 0, 0:1]).then_inc(ms_ex, 1)
                act.wait_ge(ms_pt, G + 1)
                act.activation(prob_st[:, :, :].rearrange("p a c -> p (a c)"), ps[:, 5, 0:2 * P], ACT.Copy).then_inc(ms_pc, 1)
                act.wait_ge(ms_mt, G + 1)
                cols = slice(SEQ + 32 * gr, SEQ + 32 * gr + 32)
                act.activation(act_hi[:, NPAIR:KT, cols], ps[:, 7, 0:64].rearrange("p (a c) -> p a c", c=32), ACT.Copy).then_inc(ms_hi, 1)

        def pe_ms(pe, l):
            pe.wait_ge(mq_nm, 9 * l + 9)
            for a in range(2):
                last = pe.transpose(ps[:, 0, a * NS:(a + 1) * NS], mq_n[0:NS, 0, a * P:(a + 1) * P], ident[0:NS, 0:NS])
            last.then_inc(mq_tr, 1)
            pe.wait_ge(mq_tc, 9 * l + 9)
            for gr in range(2):
                G = 2 * l + gr
                pe.wait_ge(ms_ld, 128 * (G + 1))
                for b in range(4):
                    if gr:
                        pe.wait_ge(ms_tc, 4 * (G - 1) + b + 1)
                    for a in range(2):
                        for m in range(2):
                            last = pe.transpose(ps[:, b, (2 * a + m) * P:(2 * a + m + 1) * P], mkc[:, b, m, a * P:(a + 1) * P], ident[:, :])
                    last.then_inc(ms_tr, 1)
                pe.wait_ge(ms_q, 10 * l + 6 + 4 * gr)
                pe.wait_ge(ms_tc, 4 * G + 4)
                for b in range(4):
                    for a in range(2):
                        n = 2 * b + a
                        last = pe.matmul(ps[:, 4, 0:M], mq_bd[:, n * P:(n + 1) * P], mkc_t[:, b, a, :], start=(n == 0), stop=(n == 7))
                last.then_inc(ms_s, 1)
                pe.wait_ge(ms_step, 4 * G + 4)
                for m in range(2):
                    last = pe.transpose(ps[:, 5, m * P:(m + 1) * P], prob_s[:, m * P:(m + 1) * P], ident[:, :])
                last.then_inc(ms_pt, 1)
                pe.wait_ge(ms_pc, G + 1)
                for b in range(4):
                    for m in range(2):
                        last = pe.matmul(ps[32 * b:32 * b + 32, 6, 0:MEMW], prob_st[:, m, 32 * b:32 * b + 32], mvc[:, b, m, :],
                                         start=(m == 0), stop=(m == 1))
                last.then_inc(ms_av, 1)
                pe.wait_ge(ms_ok, G + 1)
                for a in range(2):
                    last = pe.matmul(ps[:, 7, a * 32:(a + 1) * 32], ms_out[:, a * P:(a + 1) * P],
                                     pick[:, :, :].rearrange("p b q -> p (b q)"), start=True, stop=True, skip_group_check=True)
                last.then_inc(ms_mt, 1)

        def out_units(eng, l, body):
            with eng.Fori(0, OUT_U // 2) as i:
                for h in range(2):
                    body(i * 2 + h, i * 2 + (out0[l] + h), (out0[l] + h) % 2, i * 2 + (OUT_U * l + h))

        def pe_out_unit(pe, u, n, par, un):
            pe.wait_ge(w_ok, n + 1)
            for t in range(NT):
                pe.wait_ge(out_ev, un * 9 + (t + 1))
                for k in range(KT):
                    last = mm3(pe, ps[0:ROWS[t], t % CB, 0:UW], act_hi[:, k, tok_cols(t)], act_lo[:, k, tok_cols(t)],
                               w_hi[:, par, k, :], w_lo[:, par, k, :], k == 0, k == KT - 1)
                last.then_inc(w_used if t == NT - 1 else out_mm, 1)

        def dve_out_unit(dve, u, n, par, un):
            split_lo(dve, n + 1, 1 - par)
            for t in range(NT):
                if t == NT - 1:
                    dve.wait_ge(w_used, n + 1)
                else:
                    dve.wait_ge(out_mm, un * 8 + (t + 1))
                xs = x[0:ROWS[t], t, bass.ds(u * UW, UW)]
                dve.tensor_tensor(xs, xs, ps[0:ROWS[t], t % CB, 0:UW], ALU.add).then_inc(out_ev, 1)

        ROWCH = [(c * P, min(P, 16 * 2 * NFT - c * P)) for c in range(6)]

        def pool_past(pool, l):
            pool.wait_ge(ms_lo, 2 * (l + 1))
            v = A["state"][l].rearrange("b j (t f) -> (b j t) f", f=P)
            for c, (r0, nr) in enumerate(ROWCH):
                if c >= 2:
                    pool.wait_ge(st_mm, 6 * l + c - 1)
                pool.dma_start(rows_st[0:nr, c % 2, :], v[r0:r0 + nr, :]).then_inc(st_ld[c % 2], 16)

        def pe_past(pe, l):
            for c, (r0, nr) in enumerate(ROWCH):
                pe.wait_ge(st_ld[c % 2], 16 * (3 * l + c // 2 + 1))
                if c >= 2:
                    pe.wait_ge(st_ev, 6 * l + c - 1)
                pe.transpose(ps[:, 4 + c % 2, 0:nr], rows_st[0:nr, c % 2, :], ident[0:nr, 0:nr]).then_inc(st_mm, 1)

        def dve_past(dve, l):
            for c, (r0, nr) in enumerate(ROWCH):
                dve.wait_ge(st_mm, 6 * l + c + 1)
                dve.tensor_copy(past_t[:, :, :, :].rearrange("p b j t -> p (b j t)")[:, r0:r0 + nr], ps[:, 4 + c % 2, 0:nr]).then_inc(st_ev, 1)
            for t in (act_hi, act_lo):
                dve.memset(t[:, :, 0:2].bitcast(F32), 0.0).then_inc(pad_ok, 1)
                for k in range(KT):
                    dve.memset(t[:, k, SAMP0:SAMP0 + NB * EXT].rearrange("p (b t) -> p b t", t=EXT)[:, :, 0:2].bitcast(F32),
                               0.0).then_inc(pad_ok, 1)
                dve.memset(t[:, :, SAMP0 + NB * EXT:FW].bitcast(F32), 0.0).then_inc(pad_ok, 1)

        def ffn_units(eng, l, first, body):
            first()
            with eng.Fori(0, (NFT - 2) // 2) as i:
                for h in range(2):
                    body(i * 2 + (1 + h), (1 + h) % 2)
            body(NFT - 1, (NFT - 1) % 2)

        def wpar(l, par):
            return (ffn0[l] + par) % 2

        def pe_up(pe, l, u, par):
            n = u + ffn0[l]
            U = u + NFT * l
            pe.wait_ge(w_ok, n + 1)
            w = wpar(l, par)
            for h in range(2):
                if not (isinstance(u, int) and u == 0):
                    pe.wait_ge(up_ev, U * 2 + (h - 1))
                for g in range(3):
                    for k in range(KT):
                        last = mm3(pe, ps[:, 3 * h + g, 0:TG], w_hi[:, w, k, h * P:(h + 1) * P],
                                   w_lo[:, w, k, h * P:(h + 1) * P], act_hi[:, k, g * TG:(g + 1) * TG],
                                   act_lo[:, k, g * TG:(g + 1) * TG], k == 0, k == KT - 1)
                last.then_inc(w_used if h else up_mm, 1)

        def pe_down(pe, l, v, par):
            V = v + NFT * l
            pe.wait_ge(g_ok, V * 2 + 2)
            pe.wait_ge(d_ok, V + 1)
            for t in range(NT):
                for c in range(2):
                    pe.wait_ge(dn_ev, V * 18 + (2 * t + c + 1))
                    last = mm3(pe, ps[0:ROWS[t], 6 + c, :], g_hi[:, par, tok_cols(t)], g_lo[:, par, tok_cols(t)],
                               d_hi[:, c * 512:(c + 1) * 512], d_lo[:, c * 512:(c + 1) * 512], True, True)
                    last.then_inc(dn_mm, 1)

        def pe_ffn(pe, l):
            pe.wait_ge(pad_ok, 2 * (KT + 2) * (l + 1))
            def body(u, par):
                pe_up(pe, l, u, par)
                pe_down(pe, l, u - 1, 1 - par)
            ffn_units(pe, l, lambda: pe_up(pe, l, 0, 0), body)
            pe_down(pe, l, NFT - 1, (NFT - 1) % 2)

        def split_d_hi(act, l, v):
            V = v + NFT * l
            act.wait_ge(dr_ld, V * 16 + 16)
            if not (isinstance(v, int) and v == 0):
                act.wait_ge(dn_ev, V * 18 + 2)
            act.activation(d_hi[:, :], d_raw[:, :], ACT.Copy).then_inc(dh_ok, 1)

        def split_d_lo(dve, l, v):
            V = v + NFT * l
            dve.wait_ge(dh_ok, V + 1)
            dve.tensor_tensor(d_lo[:, :], d_raw[:, :], d_hi[:, :].bitcast(F32), ALU.subtract).then_inc(d_ok, 1)

        def coef(l, j, u, h):
            return cwb[:, l, j, bass.ds(u + NFT * h, 1)]

        def act_unit(act, l, u, par, first):
            U = u + NFT * l
            n = u + ffn0[l]
            if not first:
                split_d_hi(act, l, u - 1)
            if not (isinstance(n, int) and n + 1 >= N_UNITS):
                split_hi(act, n + 1, 1 - wpar(l, par))
            for h, (up, cv) in enumerate(((up_u, cv_u), (up_g, cv_g))):
                if h:
                    act.wait_ge(w_used, n + 1)
                else:
                    act.wait_ge(up_mm, U + 1)
                if not first:
                    act.wait_ge(tap_ok, U * 2 + (h - 1))
                    act.wait_ge(gate_ok if h else g_ok, U if h else U * 2)
                src = ps[:, 3 * h:3 * h + 3, 0:TG]
                act.activation(up[:, :].rearrange("p (g c) -> p g c", c=TG), src, ACT.Copy).then_inc(past_in, 1)
                act.activation(cv[:, :].rearrange("p (g c) -> p g c", c=TG), src, ACT.Identity, scale=coef(l, 2, u, h),
                               bias=coef(l, 3, u, h)).then_inc(up_ev, 1)
            act.wait_ge(cv_ok, U * 4 + 2)
            act.activation(cv_u[:, 2:FW], cv_u[:, 2:FW], ACT.Silu).then_inc(silu_ok, 1)
            act.wait_ge(gate_ok, U + 1)
            if not first:
                act.wait_ge(dn_ev, U * 18 + (2 - 18))
            act.activation(g_hi[:, par, 0:SEQ], cv_u[:, 2:2 + SEQ], ACT.Copy).then_inc(gh_ok, 1)
            act.activation(g_hi[:, par, SEQ:NTOK].rearrange("p (b t) -> p b t", t=NQ), samp_cv(cv_u), ACT.Copy).then_inc(gh_ok, 1)

        def samp_cv(t):
            return t[:, SAMP0:SAMP0 + NB * EXT].rearrange("p (b t) -> p b t", t=EXT)[:, :, 2:EXT]

        def dve_taps(dve, l, u, h, first):
            U = u + NFT * l
            up, cv = ((up_u, cv_u), (up_g, cv_g))[h]
            ft = bass.ds(u + NFT * h, 1)
            ext = up[:, SAMP0:SAMP0 + NB * EXT].rearrange("p (b t) -> p b t", t=EXT)
            dve.wait_ge(up_ev, U * 2 + (h + 1))
            dve.tensor_copy(ext[:, :, 0:2], past_t[:, :, :, ft].rearrange("p b j a -> p b (j a)")).then_inc(ins_ok, 1)
            dve.tensor_copy(tail_p[:, :, ft].rearrange("p j a -> p (j a)"), up[:, SEQ:SEQ + 2]).then_inc(tail_ok, 1)
            dve.tensor_copy(tail_s[:, :, :, ft].rearrange("p b j a -> p b (j a)"), ext[:, :, EXT - 2:EXT]).then_inc(tail_ok, 1)
            dve.wait_ge(ins_ok, U * 2 + (h + 1))
            dve.scalar_tensor_tensor(out=cv[:, 2:FW], in0=up[:, 1:FW - 1], scalar=coef(l, 1, u, h), in1=cv[:, 2:FW],
                                     op0=ALU.mult, op1=ALU.add).then_inc(cv_ok, 1)
            dve.wait_ge(cv_ok, U * 4 + (2 * h + 1))
            dve.scalar_tensor_tensor(out=cv[:, 2:FW], in0=up[:, 0:FW - 2], scalar=coef(l, 0, u, h), in1=cv[:, 2:FW],
                                     op0=ALU.mult, op1=ALU.add).then_inc(cv_ok, 1)
            dve.wait_ge(cv_ok, U * 4 + (2 * h + 2))
            dve.sem_inc(tap_ok, 1)

        ins_ok, tail_ok = sem("ins_ok"), sem("tail_ok")

        def dve_adds(dve, l, v):
            V = v + NFT * l
            for t in range(NT):
                for c in range(2):
                    dve.wait_ge(dn_mm, V * 18 + (2 * t + c + 1))
                    xs = x[0:ROWS[t], t, c * 512:(c + 1) * 512]
                    dve.tensor_tensor(xs, xs, ps[0:ROWS[t], 6 + c, :], ALU.add).then_inc(dn_ev, 1)

        def dve_unit(dve, l, u, par, first):
            U = u + NFT * l
            n = u + ffn0[l]
            if not first:
                split_d_lo(dve, l, u - 1)
            if not (isinstance(n, int) and n + 1 >= N_UNITS):
                split_lo(dve, n + 1, 1 - wpar(l, par))
            dve_taps(dve, l, u, 0, first)
            if not first:
                dve_adds(dve, l, u - 1)
            dve_taps(dve, l, u, 1, first)
            dve.wait_ge(silu_ok, U + 1)
            dve.tensor_tensor(cv_u[:, 2:FW], cv_u[:, 2:FW], cv_g[:, 2:FW], ALU.mult).then_inc(gate_ok, 1)
            dve.wait_ge(gh_ok, U * 2 + 2)
            dve.tensor_tensor(g_lo[:, par, 0:SEQ], cv_u[:, 2:2 + SEQ], g_hi[:, par, 0:SEQ].bitcast(F32),
                              ALU.subtract).then_inc(g_ok, 1)
            dve.tensor_tensor(g_lo[:, par, SEQ:NTOK].rearrange("p (b t) -> p b t", t=NQ), samp_cv(cv_u),
                              g_hi[:, par, SEQ:NTOK].rearrange("p (b t) -> p b t", t=NQ).bitcast(F32),
                              ALU.subtract).then_inc(g_ok, 1)

        def act_ffn(act, l):
            ffn_units(act, l, lambda: act_unit(act, l, 0, 0, True), lambda u, par: act_unit(act, l, u, par, False))
            split_d_hi(act, l, NFT - 1)

        def dve_ffn(dve, l):
            ffn_units(dve, l, lambda: dve_unit(dve, l, 0, 0, True), lambda u, par: dve_unit(dve, l, u, par, False))
            split_d_lo(dve, l, NFT - 1)
            dve_adds(dve, l, NFT - 1)

        def pool_ffn(pool, l):
            pool.wait_ge(ms_lo, 2 * (l + 1))
            def load(v):
                if not (isinstance(v, int) and v == 0):
                    pool.wait_ge(d_ok, v + NFT * l)
                pool.dma_start(d_raw[:, :], A["w_down"][l][bass.ds(v * P, P), :]).then_inc(dr_ld, 16)
            load(0)
            with pool.Fori(0, NFT - 1) as i:
                load(i + 1)

        TAILS = [("p", 0, 2 * 2 * NFT)] + [("s", r0, nr) for r0, nr in ROWCH]

        def tail_src(kind, r0, nr):
            t = tail_p[:, :, :].rearrange("p j t -> p (j t)") if kind == "p" else tail_s[:, :, :, :].rearrange("p b j t -> p (b j t)")
            return t[:, r0:r0 + nr]

        def pe_tails(pe, l):
            pe.wait_ge(tail_ok, 4 * NFT * (l + 1))
            for c, (kind, r0, nr) in enumerate(TAILS):
                if c >= 2:
                    pe.wait_ge(tl_ev, 7 * l + c - 1)
                pe.transpose(ps[0:nr, 4 + c % 2, 0:P], tail_src(kind, r0, nr), ident[:, :]).then_inc(tl_mm, 1)

        def dve_tails(dve, l):
            for c, (kind, r0, nr) in enumerate(TAILS):
                dve.wait_ge(tl_mm, 7 * l + c + 1)
                if c >= 2:
                    dve.wait_ge(tl_out[c % 2], 16 * ((4, 3)[c % 2] * l + c // 2))
                dve.tensor_copy(rows_st[0:nr, c % 2, :], ps[0:nr, 4 + c % 2, 0:P]).then_inc(tl_ev, 1)

        def pool_tails(pool, l):
            for c, (kind, r0, nr) in enumerate(TAILS):
                pool.wait_ge(tl_ev, 7 * l + c + 1)
                dst = (O["conv_p"][l, 0].rearrange("j (t f) -> (j t) f", f=P) if kind == "p"
                       else O["conv_s"][l].rearrange("b j (t f) -> (b j t) f", f=P))
                pool.dma_start(dst[r0:r0 + nr, :], rows_st[0:nr, c % 2, :]).then_inc(tl_out[c % 2], 16)

        def x_ready(act, t, l, ffn):
            if ffn:
                act.wait_ge(out_ev, CB + 9 * OUT_U * (l + 1))
            elif l:
                act.wait_ge(dn_ev, 2 + 18 * NFT)
            else:
                act.wait_ge(x_ld, 32)

        block = es.enter_context(nc.Block())

        @block.sync
        def _(sp):
            sp.dma_start(x[:, 0:NPT, :], A["x_prompt"][0].rearrange("(t p) d -> p t d", p=P)).then_inc(x_ld, 16)
            sp.dma_start(x[0:NS, NPT, :], A["x_sample"].rearrange("b t d -> (b t) d")).then_inc(x_ld, 16)
            for l in (0, 1):
                for u in range(KV_U):
                    load_cols(sp, kv0[l] + u, A["w_mem_kv"][l], u * UW)
                order = [(0, 0)]
                in_units(sp, l, lambda u, n, par, un: load_cols(sp, n, win[l], u * UW))
                load_cols(sp, out0[l], A["w_out"][l], 0)
                if l:
                    sp_bs(sp)
                sp_ms(sp, l)
                for u in range(1, OUT_U):
                    load_cols(sp, out0[l] + u, A["w_out"][l], u * UW)

                def load_up(u, par):
                    def half(h):
                        return A["w_up"][l][:, bass.ds(u * P + DFF * h, P)].rearrange("(k p) f -> p k f", p=P)
                    load_unit(sp, u + ffn0[l], half(0), half(1), w_raw[:, :, 0:P], w_raw[:, :, P:UW])

                ffn_units(sp, l, lambda: load_up(0, 0), load_up)
            sp.wait_ge(dn_ev, 2 + 18 * NFT * 2)
            sp.dma_start(O["y_p"][0].rearrange("(t p) d -> p t d", p=P), x[:, 0:NPT, :]).then_inc(y_out, 16)
            sp.dma_start(O["y_s"].rearrange("b t d -> (b t) d"), x[0:NS, NPT, :]).then_inc(y_out, 16)
            sp.wait_ge(y_out, 32)
            sp.wait_ge(tl_out[0], 16 * 8)
            sp.wait_ge(tl_out[1], 16 * 6)
            sp.wait_ge(kv_out, 64)
            sp.wait_ge(gm_out, 16)
            sp.wait_ge(copied, 64)
            sp.wait_ge(in_st, IN_ST[1])

        @block.gpsimd
        def _(pool):
            for s, v in ((in_ev, CB), (stage_free, 2), (out_ev, CB), (dn_ev, 2), (bp_free, 1), (bp_lo, 2), (bp_av, 2),
                         (bs_av, 5), (mq_lo, 2)):
                pool.sem_inc(s, v)
            pool.memset(eps_ap[:, :], EPS).then_inc(filled, 1)
            pool_masks.filled = 1
            pool_setup(pool)
            for l in (0, 1):
                pool_mem(pool, l)
                pool_kv(pool, l)
                in_units(pool, l, lambda u, n, par, un: pool_in_unit(pool, l, u, par, un))
                if l == 0:
                    pool_gm_load(pool)
                else:
                    pool_bp(pool)
                    pool_bs(pool)
                pool_mq(pool, l)
                pool_past(pool, l)
                pool_ffn(pool, l)
                pool_tails(pool, l)

        @block.scalar
        def _(act):
            c = Counts()
            act.wait_ge(filled, 1)
            act.wait_ge(set_ev, SET_EV)
            split_hi(act, 0, 0)
            for l in (0, 1):
                act_mem(act, c, l)
                act_norm_x(act, c, 8 * l, False, lambda e, t: x_ready(e, t, l, False))
                act_kv(act, c, l)
                in_units(act, l, lambda u, n, par, un: act_in_unit(act, l, u, n, par, 0, un))
                if l == 0:
                    act_gm(act, c)
                else:
                    act_bp(act)
                    act_bs(act)
                act_mq(act, l)
                act_ms(act, l)
                out_units(act, l, lambda u, n, par, un: split_hi(act, n + 1, 1 - par))
                act_norm_x(act, c, 16 + 8 * l, True, lambda e, t: x_ready(e, t, l, True))
                act_ffn(act, l)

        @block.vector
        def _(dve):
            c = Counts()
            dve_setup(dve)
            split_lo(dve, 0, 0)
            for l in (0, 1):
                dve_mem(dve, c, l)
                dve_norm_x(dve, c, 8 * l, False)
                dve_kv(dve, c, l)
                in_units(dve, l, lambda u, n, par, un: split_lo(dve, n + 1, 1 - par))
                dve_kv_turn(dve, l)
                if l == 0:
                    dve_gm(dve, c)
                else:
                    dve_bp(dve)
                    dve_bs(dve)
                dve_mq(dve, l)
                dve_ms(dve, l)
                out_units(dve, l, lambda u, n, par, un: dve_out_unit(dve, u, n, par, un))
                dve_past(dve, l)
                dve_norm_x(dve, c, 16 + 8 * l, True)
                dve_ffn(dve, l)
                dve_tails(dve, l)

        @block.tensor
        def _(pe):
            c = Counts()
            pe_setup(pe)
            for l in (0, 1):
                pe_mem(pe, c, l)
                pe_norm_x(pe, c)
                pe_kv(pe, c, l)
                in_units(pe, l, lambda u, n, par, un: pe_in_unit(pe, l, u, n, par, un * 9))
                pe_kv_turn(pe, c, l)
                if l == 0:
                    pe_gm(pe, c)
                else:
                    pe_bp(pe)
                    pe_bs(pe)
                pe_mq(pe, l)
                pe_ms(pe, l)
                if l:
                    pe.wait_ge(bs_lo, NB)
                pe.wait_ge(turn_lo, c.turn)
                pe.wait_ge(mq_lo, 2 + 8 * (l + 1))
                pe.wait_ge(ms_lo, 2 * (l + 1))
                out_units(pe, l, lambda u, n, par, un: pe_out_unit(pe, u, n, par, un))
                pe_past(pe, l)
                pe_norm_x(pe, c)
                pe.wait_ge(turn_lo, c.turn)
                pe_ffn(pe, l)
                pe_tails(pe, l)


_INS = ["x_prompt", "x_sample", "cache_mem_k", "cache_mem_v", "cache_sb_k", "cache_sb_v", "state_ffn_conv",
        "page_table", "mem_prompt", "norm_mix", "norm_ffn", "norm_mem", "w_in_a", "gm_v_norm", "gm_ws", "gm_bs",
        "w_in_b", "sb_bias", "w_mem_kv", "mem_q_norm", "mem_k_norm", "w_out", "w_up", "conv_w", "conv_b", "w_down"]
_OUTS = [("y_p", (1, SEQ, D)), ("y_s", (NB, NQ, D)), ("mem_k", (2, 1, M, MH, HD)), ("mem_v", (2, 1, M, MH, HD)),
         ("sb_k_p", (1, 1, SEQ, SH, HD)), ("sb_v_p", (1, 1, SEQ, SH, HD)), ("sb_k_s", (1, NB, NQ, SH, HD)),
         ("sb_v_s", (1, NB, NQ, SH, HD)), ("gm_v", (1, NB, NQ, MIX)), ("conv_p", (2, 1, 2, 2 * DFF)),
         ("conv_s", (2, NB, 2, 2 * DFF))]


def kernel(**inputs):
    import numpy as _np
    import concourse.bacc as _bacc
    from concourse import mybir as _mybir
    from concourse.bass_utils import run_bass_kernel_spmd as _run

    nc = _bacc.Bacc("TRN2", target_bir_lowering=False, num_devices=1)
    arrays, A, O = {}, {}, {}
    for name in _INS:
        a = _np.ascontiguousarray(inputs[name])
        arrays[f"in_{name}_dram"] = a
        A[name] = nc.dram_tensor(f"in_{name}_dram", a.shape, _mybir.dt.from_np(a.dtype), kind="ExternalInput").ap()
    A["state"] = A["state_ffn_conv"]
    for name, shape in _OUTS:
        O[name] = nc.dram_tensor(f"out_{name}_dram", shape, _mybir.dt.float32, kind="ExternalOutput").ap()
    scratch = nc.dram_tensor("projected", (NTOK, 3 * MIX + MEMW), _mybir.dt.float32, kind="Internal").ap()
    build(nc, A, O, scratch)
    r = _run(nc, [arrays], core_ids=[0])
    return tuple(r.results[0][f"out_{name}_dram"] for name, _ in _OUTS)
```

```python
from contextlib import ExitStack

import concourse.bass as bass
from concourse import mybir

F32 = mybir.dt.float32
F32R = mybir.dt.float32r
I32 = mybir.dt.int32
ALU = mybir.AluOpType
ACT = mybir.ActivationFunctionType
AX_X = mybir.AxisListType.X

P = 128
D = 1024
KT = D // P
SEQ = 1024
NPT = SEQ // P
NB, NQ = 8, 8
NS = NB * NQ
NT = NPT + 1
MIX = 768
MEMW = 256
MH, HD = 4, 64
M = 256
SH = 12
NPAIR = SH // 2
DFF = 2816
NFT = DFF // P
PAGES = 16
EPS = 1e-6
UW = 256
NTOK = SEQ + NS
EXT = NQ + 2
SAMP0 = 2 + SEQ
FW = 1110
TG = FW // 3
CB = 3
DC = 4

ROWS = [P] * NPT + [NS]


class Counts:

    def __init__(self):
        self.turn = 0
        self.xn = 0
        self.norm = 0
        self.ssq = 0
        self.kv = 0


def build(nc, A, O, scratch):
    es = ExitStack()
    with es:
        place = [16512]
        top = nc.sbuf_usable_end // 32 * 32 - 576

        def sb_at(name, shape, off, dt=F32):
            return nc.alloc_sbuf_tensor_at(name, shape, dt, offset=off)

        def size(shape):
            n = 4
            for s in shape[1:]:
                n *= s
            return (n + 31) // 32 * 32

        def sb(name, shape, dt=F32):
            t = sb_at(name, shape, place[0], dt)
            place[0] += size(shape)
            return t

        class Region:

            def __init__(self, at):
                self.at = at

            def __call__(self, name, shape, dt=F32):
                t = sb_at(name, shape, self.at, dt)
                self.at += size(shape)
                assert self.at <= top, (name, self.at, top)
                return t

        x = sb("x", [P, NT, D])
        act_hi = sb("act_hi", [P, KT, FW], F32R)
        act_lo = sb("act_lo", [P, KT, FW], F32R)
        w_hi = sb("w_hi", [P, 2, KT, UW], F32R)
        w_lo = sb("w_lo", [P, 2, KT, UW], F32R)
        w_raw = sb("w_raw", [P, KT, UW])
        ident = sb("ident", [P, P])
        gains = sb("gains", [P, 48])
        cwb = sb("cwb", [P, 2, 4, 2 * NFT])
        qk_gain = sb("qk_gain", [P, 4, HD])
        ssq = sb("ssq", [P, NT])
        root = sb("root", [P, NT])
        inv = sb("inv", [P, NT])
        head_of = sb("head_of", [P, MH])
        query_of = sb("query_of", [P, NQ])
        batch_of = sb("batch_of", [P, 4])
        rep8 = sb("rep8", [NQ, NB, NQ])
        phase0 = place[0]

        r = Region(phase0)
        gains_raw = r("gains_raw", [48, P])
        conv_raw = r("conv_raw", [2 * NFT, 2, 4, P])
        slot16 = r("slot16", [P, 16])

        r = Region(phase0)
        mk_bd = r("mk_bd", [P, 2, 2 * M])
        mv_pad = r("mv_pad", [P, 2, MH, P])
        keep = r.at
        diag = r("diag", [P, NT, P])
        mem_hi = r("mem_hi", [P, KT, M], F32R)
        mem_lo = r("mem_lo", [P, KT, M], F32R)
        mem_raw = r("mem_raw", [P, 2, D])
        r = Region(keep)
        v_all = r("v_all", [P, NT, MIX])
        mkv = r("mkv", [P, 2, 2 * MEMW])
        stage = sb_at("stage", [P, 2, NT, UW], r.at)
        kv_sq = r("kv_sq", [P, 2, MEMW])
        kv_stat = r("kv_stat", [P, 3, 8])

        r = Region(keep + size([P, NT, MIX]))
        gm_cat = r("gm_cat", [P, 4, MIX])
        w_t = r("w_t", [P, 6, P])
        ws_raw = sb_at("ws_raw", [P, 6, P], r.at)
        gm_gain = sb_at("gm_gain", [P, MIX], r.at)
        r.at += size([P, MIX])
        w_s = r("w_s", [NS, 6, NS])
        bias_raw = r("bias_raw", [6, P])
        bias_t = r("bias_t", [P, 6])
        bias_s = r("bias_s", [NS, 6])
        same_batch = r("same_batch", [NS, NS])

        r = Region(phase0)
        tri01 = r("tri01", [P, P])
        bias12 = r("bias12", [P, SH])
        new01 = r("new01", [96, NQ])
        head12 = r("head12", [96, SH])
        head_b = r("head_b", [96, SH])
        bias96 = r("bias96", [96, 1])
        zero1 = r("zero1", [P, 1])
        mid = r.at
        sbq_raw = r("sbq_raw", [P, NPT, P])
        sbk_raw = r("sbk_raw", [P, NPT, P])
        sb_v = r("sb_v", [P, NPT, P])
        sb_q = r("sb_q", [65, 2, SEQ])
        sb_k = r("sb_k", [65, 2, SEQ])
        brk = r("brk", [P, 3, SEQ])
        left = r("left", [P, SEQ + 1])
        brk_t = r("brk_t", [P, 2, 512])
        r = Region(mid)
        pk_raw = r("pk_raw", [P, 4, MIX])
        pk_hi = r("pk_hi", [P, NPAIR, 2 * P + NQ], F32R)
        pk_lo = r("pk_lo", [P, NPAIR, 2 * P + NQ], F32R)
        pv_hi1 = r("pv_hi1", [P, 2, MIX], F32R)
        pv_lo1 = r("pv_lo1", [P, 2, MIX], F32R)
        s_brk = r("s_brk", [96, 2, 2 * P + NQ])
        s_left = r("s_left", [96, 2, 2 * P + NQ + 1])
        at_hi = r("at_hi", [P, 2, 2, 96], F32R)
        at_lo = r("at_lo", [P, 2, 2, 96], F32R)
        at_new = r("at_new", [NQ, 96])
        v_new = r("v_new", [NQ, MIX])
        kn_t = r("kn_t", [P, NPAIR, NS])
        qb_hi = r("qb_hi", [P, NPAIR * 112], F32R)
        qb_lo = r("qb_lo", [P, NPAIR * 112], F32R)
        s_out = r("s_out", [96, MIX])

        r = Region(keep)
        mq = r("mq", [P, NT, MEMW])
        mq_sq = sb_at("mq_sq", [P, NT, MEMW], r.at)
        r.at += size([P, NT, MEMW])
        mq_n = r("mq_n", [P, 2, MEMW])
        mq_t = r("mq_t", [P, 2, 2, P])
        mq_stat = r("mq_stat", [P, 3, NT * MH])
        sm_max = r("sm_max", [P, 2, MH])
        sm_sum = r("sm_sum", [P, 2, MH])
        sm_inv = r("sm_inv", [P, 2, MH])
        mid = r.at
        prob = r("prob", [P, 2, MH, M])
        prob_t = r("prob_t", [P, 2, 2, MH, P])
        r = Region(mid)
        mkc = r("mkc", [P, 4, 2, MEMW])
        mvc = r("mvc", [P, 4, 2, MEMW])
        mkc_t = sb_at("mkc_t", [P, 4, 2, M], keep + size([P, NT, MEMW]))
        mq_bd = r("mq_bd", [P, 4 * 288])
        prob_s = r("prob_s", [P, M])
        prob_st = r("prob_st", [P, 2, P])
        ms_out = r("ms_out", [P, MEMW])
        pick = r("pick", [P, 4, NQ])

        r = Region(phase0)
        up_u = r("up_u", [P, FW])
        up_g = r("up_g", [P, FW])
        cv_u = r("cv_u", [P, FW])
        cv_g = r("cv_g", [P, FW])
        d_hi = r("d_hi", [P, D], F32R)
        d_lo = r("d_lo", [P, D], F32R)
        d_raw = r("d_raw", [P, D])
        g_hi = r("g_hi", [P, 2, NTOK], F32R)
        g_lo = r("g_lo", [P, 2, NTOK], F32R)
        past_t = r("past_t", [P, NB, 2, 2 * NFT])
        tail_p = r("tail_p", [P, 2, 2 * NFT])
        tail_s = r("tail_s", [P, NB, 2, 2 * NFT])
        rows_st = r("rows_st", [P, 2, P])

        ps = es.enter_context(nc.psum_tensor("ps", [P, 8, 512], F32))

        def sem(name):
            return es.enter_context(nc.semaphore(name))

        filled, masked, set_ld, set_mm, set_ev = (sem(n) for n in ("filled", "masked", "set_ld", "set_mm", "set_ev"))
        x_ld, mem_ld = sem("x_ld"), sem("mem_ld")
        wr_ld, wh_ok, w_ok, w_used = (sem(n) for n in ("wr_ld", "wh_ok", "w_ok", "w_used"))
        ssq_ok, root_ok, inv_ok, xn_ok = (sem(n) for n in ("ssq_ok", "root_ok", "inv_ok", "xn_ok"))
        turned, turn_hi, turn_lo = (sem(n) for n in ("turned", "turn_hi", "turn_lo"))
        kv_mm, kv_ev, kv_st, kv_root, kv_tr, kv_ok, kv_out = (
            sem(n) for n in ("kv_mm", "kv_ev", "kv_st", "kv_root", "kv_tr", "kv_ok", "kv_out"))
        in_mm, in_ev, in_st, stage_free = (sem(n) for n in ("in_mm", "in_ev", "in_st", "stage_free"))
        out_mm, out_ev = sem("out_mm"), sem("out_ev")
        gm_gelu, gm_v, gm_set, gm_setmm, gm_mix, gm_cat_ok, gm_out = (
            sem(n) for n in ("gm_gelu", "gm_v", "gm_set", "gm_setmm",
                             "gm_mix", "gm_cat_ok", "gm_out"))
        mq_ld, mq_step, mq_root, mq_tr, mq_tc, mq_s, mq_mx, mq_ex, mq_pr, mq_pt, mq_pc, mq_av, mq_hi, mq_lo = (
            sem(n) for n in ("mq_ld", "mq_step", "mq_root", "mq_tr", "mq_tc", "mq_s", "mq_mx", "mq_ex", "mq_pr",
                             "mq_pt", "mq_pc", "mq_av", "mq_hi", "mq_lo"))
        ms_ld, ms_tr, ms_tc, ms_q, ms_s, ms_step, ms_ex, ms_pt, ms_pc, ms_av, ms_ok, ms_mt, ms_hi, ms_lo = (
            sem(n) for n in ("ms_ld", "ms_tr", "ms_tc", "ms_q", "ms_s", "ms_step", "ms_ex", "ms_pt", "ms_pc",
                             "ms_av", "ms_ok", "ms_mt", "ms_hi", "ms_lo"))
        bp_ld, bp_v, bp_tr, bp_q, bp_k, bp_b, bp_z, bp_sig, bp_msk, bp_keep, bp_left, bp_a, bp_t, bp_at, bp_av, bp_hi, \
            bp_lo, bp_set, bp_one = (sem("bp_" + n) for n in ("ld", "v", "tr", "q", "k", "b", "z", "sig", "msk", "keep",
                                                              "left", "a", "t", "at", "av", "hi", "lo", "set", "one"))
        bs_in, bs_set, bs_tr, bs_q, bs_qb, bs_kn, bs_kh, bs_kl, bs_vh, bs_z, bs_sig, bs_a, bs_at, bs_ah, \
            bs_al, bs_vn, bs_av, bs_o, bs_mt, bs_hi, bs_lo = (sem("bs_" + n) for n in (
                "in", "set", "tr", "q", "qb", "kn", "kh", "kl", "vh", "z", "sig", "a", "at", "ah",
                "al", "vn", "av", "o", "mt", "hi", "lo"))
        up_mm, up_ev, cv_ok, silu_ok, gate_ok, gh_ok, g_ok, dr_ld, dh_ok, d_ok, dn_mm, dn_ev = (
            sem(n) for n in ("up_mm", "up_ev", "cv_ok", "silu_ok", "gate_ok", "gh_ok", "g_ok", "dr_ld",
                             "dh_ok", "d_ok", "dn_mm", "dn_ev"))
        gm_u = [sem(f"gm_u{n}") for n in range(4)]
        bs_k, bs_v, bs_vl = ([sem(f"bs_{n}{h}") for h in (0, 1)] for n in ("k", "v", "vl"))
        st_ld, tl_out = [sem("st_ld0"), sem("st_ld1")], [sem("tl_out0"), sem("tl_out1")]
        bs_n, bs_edge = sem("bs_n"), sem("bs_edge")
        tap_ok, mq_nm = sem("tap_ok"), sem("mq_nm")
        st_mm, st_ev, tl_mm, tl_ev = (sem(n) for n in ("st_mm", "st_ev", "tl_mm", "tl_ev"))
        pad_ok, copied, y_out, mem_pad = sem("pad_ok"), sem("copied"), sem("y_out"), sem("mem_pad")

        proj = scratch

        KV_U, OUT_U, FFN_U = 2, 4, NFT
        IN_U = [7, 10]
        LU = [KV_U + IN_U[0] + OUT_U + FFN_U, KV_U + IN_U[1] + OUT_U + FFN_U]
        kv0 = [0, LU[0]]
        in0 = [kv0[l] + KV_U for l in (0, 1)]
        out0 = [in0[l] + IN_U[l] for l in (0, 1)]
        ffn0 = [out0[l] + OUT_U for l in (0, 1)]
        N_UNITS = sum(LU)
        win = [A["w_in_a"][0], A["w_in_b"][0]]

        def tok_cols(t):
            return slice(t * P, t * P + ROWS[t])

        def samp_ffn(tile, k):
            return tile[:, k, SAMP0:SAMP0 + NB * EXT].rearrange("p (b t) -> p b t", t=EXT)[:, :, 2:EXT]

        def load_unit(sp, n, src_a, src_b, dst_a, dst_b):
            if not (isinstance(n, int) and n == 0):
                sp.wait_ge(w_ok, n)
            sp.dma_start(dst_a, src_a).then_inc(wr_ld, 16)
            sp.dma_start(dst_b, src_b).then_inc(wr_ld, 16)

        def load_cols(sp, n, w, c0):
            v = w[:, bass.ds(c0, UW)].rearrange("(k p) f -> p k f", p=P)
            load_unit(sp, n, v[:, 0:4, :], v[:, 4:8, :], w_raw[:, 0:4, :], w_raw[:, 4:8, :])

        def split_hi(act, n, par):
            act.wait_ge(wr_ld, 32 * n + 32)
            if not (isinstance(n, int) and n < 2):
                act.wait_ge(w_used, n - 1)
            act.activation(w_hi[:, par], w_raw[:, :, :], ACT.Copy).then_inc(wh_ok, 1)

        def split_lo(dve, n, par):
            dve.wait_ge(wh_ok, n + 1)
            dve.tensor_tensor(w_lo[:, par], w_raw[:, :, :], w_hi[:, par].bitcast(F32), ALU.subtract).then_inc(w_ok, 1)

        def mm3(pe, out, ahi, alo, bhi, blo, first, last, **kw):
            pe.matmul(out, ahi, bhi, start=first, stop=False, **kw)
            pe.matmul(out, ahi, blo, start=False, stop=False, **kw)
            return pe.matmul(out, alo, bhi, start=False, stop=last, **kw)

        def pool_masks(pool, fills, selects):
            f0 = pool_masks.filled
            m0 = pool_masks.masked
            for t, v in fills:
                pool.memset(t, v).then_inc(filled, 1)
            pool_masks.filled += len(fills)
            pool.wait_ge(filled, f0 + len(fills))
            for n, (t, cmp, fill, base, pattern, mult) in enumerate(selects):
                if n:
                    pool.wait_ge(masked, m0 + n)
                pool.affine_select(out=t, in_=t, compare_op=cmp, fill=fill, base=base, pattern=pattern,
                                   channel_multiplier=mult).then_inc(masked, 1)
            pool_masks.masked += len(selects)

        pool_masks.filled = 0
        pool_masks.masked = 0

        SET_MASKS = 5

        def pool_setup(pool):
            for n, name in enumerate(("norm_mix", "norm_ffn", "norm_mem")):
                pool.dma_start(gains_raw[16 * n:16 * n + 16, :],
                               A[name].rearrange("l (k p) -> (l k) p", p=P)).then_inc(set_ld, 16)
            for l in (0, 1):
                pool.dma_start(conv_raw[:, l, 0:3, :],
                               A["conv_w"][l].rearrange("j (t f) -> t j f", f=P)).then_inc(set_ld, 16)
                pool.dma_start(conv_raw[:, l, 3, :],
                               A["conv_b"][l].rearrange("(t f) -> t f", f=P)).then_inc(set_ld, 16)
            for n, name in enumerate(("mem_q_norm", "mem_k_norm")):
                pool.dma_start(qk_gain[:, 2 * n:2 * n + 2, :].rearrange("p l d -> p (l d)"),
                               A[name].rearrange("l d -> (l d)").partition_broadcast(P)).then_inc(set_ld, 16)
            pool_masks(pool, [(ident[:, :], 0.0), (slot16[:, :], 1.0), (batch_of[:, :], 1.0)], [
                (ident[:, :], ALU.not_equal, 1.0, 0, [[-1, P]], 1),
                (slot16[:, :], ALU.is_ge, 0.0, 0, [[-8, 16]], 1),
                (slot16[:, :], ALU.is_ge, 0.0, 7, [[8, 16]], -1),
                (batch_of[:, :], ALU.is_ge, 0.0, 0, [[-32, 4]], 1),
                (batch_of[:, :], ALU.is_ge, 0.0, 31, [[32, 4]], -1),
            ])

        def pe_setup(pe):
            pe.wait_ge(set_ld, 16 * 9)
            pe.wait_ge(masked, SET_MASKS)
            pe.transpose(ps[:, 0, 0:48], gains_raw[:, :], ident[0:48, 0:48]).then_inc(set_mm, 1)
            for l in (0, 1):
                for j in range(4):
                    at = (l * 4 + j) * 2 * NFT
                    last = pe.transpose(ps[:, 1, at:at + 2 * NFT], conv_raw[:, l, j, :], ident[0:2 * NFT, 0:2 * NFT])
            last.then_inc(set_mm, 1)

        def dve_setup(dve):
            dve.memset(ssq[:, :], 1.0).then_inc(set_ev, 1)
            dve.wait_ge(masked, SET_MASKS)
            dve.tensor_reduce(head_of[:, :], slot16[:, :].rearrange("p (b h) -> p h b", h=MH), AX_X, ALU.add).then_inc(set_ev, 1)
            dve.tensor_reduce(query_of[:, :], ident[:, :].rearrange("p (j q) -> p q j", q=NQ), AX_X, ALU.add).then_inc(set_ev, 1)
            dve.tensor_copy(rep8[:, :, :], ident[0:NQ, 0:NQ].unsqueeze(1).broadcast_to([NQ, NB, NQ])).then_inc(set_ev, 1)
            dve.wait_ge(set_mm, 2)
            dve.tensor_copy(gains[:, :], ps[:, 0, 0:48]).then_inc(set_ev, 1)
            dve.tensor_copy(cwb[:, :, :, :].rearrange("p l j t -> p (l j t)"), ps[:, 1, 0:8 * 2 * NFT]).then_inc(set_ev, 1)

        SET_EV = 6

        def act_norm(act, c, src, tiles, wait_src, width=D, bank=4):
            for t in tiles:
                wait_src(act, t)
                if c.ssq:
                    act.wait_ge(ssq_ok, c.ssq)
                act.activation(ps[0:ROWS[t], bank:bank + 2, :].rearrange("p a b -> p (a b)")[:, 0:width], src(t), ACT.Square,
                               accum_out=ssq[0:ROWS[t], t:t + 1]).then_inc(ssq_ok, 1)
                c.ssq += 1
            act.wait_ge(ssq_ok, c.ssq)
            a, b = tiles[0], tiles[-1] + 1
            act.activation(root[:, a:b], ssq[:, a:b], ACT.Sqrt, scale=1.0 / width, bias=eps_ap[:, 0:1]).then_inc(root_ok, 1)

        def dve_inv(dve, c, tiles):
            c.norm += 1
            a, b = tiles[0], tiles[-1] + 1
            dve.wait_ge(root_ok, c.norm)
            dve.reciprocal(inv[:, a:b], root[:, a:b]).then_inc(inv_ok, 1)
            dve.wait_ge(inv_ok, c.norm)

        def dve_diag(dve, c, t):
            n = ROWS[t]
            dve.tensor_scalar(diag[0:n, t, 0:n], ident[0:n, 0:n], inv[0:n, t:t + 1], None, ALU.mult).then_inc(xn_ok, 1)
            c.xn += 1

        def pe_turn(pe, c, src, group, ktiles, wait_src, scaled=False):
            wait_src(pe)
            for k in range(ktiles):
                bank = c.turn % 4
                if c.turn >= 4:
                    pe.wait_ge(turn_lo, c.turn - 3)
                for j, t in enumerate(group):
                    out = ps[:, bank, j * P:j * P + ROWS[t]]
                    if scaled:
                        last = pe.matmul(out, src(t, k), diag[0:ROWS[t], t, 0:ROWS[t]], start=True, stop=True, skip_group_check=True)
                    else:
                        last = pe.transpose(out, src(t, k), ident[0:ROWS[t], 0:ROWS[t]])
                last.then_inc(turned, 1)
                c.turn += 1

        def turn_dst(dst, k, group, ffn):
            if group[0] == NPT:
                if ffn:
                    return samp_ffn(dst, k)
                return dst[:, k, SEQ:NTOK].rearrange("p (b t) -> p b t", t=NQ)
            a = group[0] * P + (2 if ffn else 0)
            return dst[:, k, a:a + P * len(group)]

        def turn_src(bank, group):
            if group[0] == NPT:
                return ps[:, bank, 0:NS].rearrange("p (b t) -> p b t", t=NQ)
            return ps[:, bank, 0:P * len(group)]

        def act_turn(act, c, dst, group, ktiles, gain0, ffn):
            for k in range(ktiles):
                bank = c.turn % 4
                act.wait_ge(turned, c.turn + 1)
                scale = 1.0 if gain0 is None else gains[:, gain0 + k:gain0 + k + 1]
                act.activation(turn_dst(dst, k, group, ffn), turn_src(bank, group), ACT.Copy, scale=scale).then_inc(turn_hi, 1)
                c.turn += 1

        def dve_turn(dve, c, hi, lo, group, ktiles, gain0, ffn):
            for k in range(ktiles):
                bank = c.turn % 4
                dve.wait_ge(turn_hi, c.turn + 1)
                scale = 1.0 if gain0 is None else gains[:, gain0 + k:gain0 + k + 1]
                dve.scalar_tensor_tensor(out=turn_dst(lo, k, group, ffn), in0=turn_src(bank, group), scalar=scale,
                                         in1=turn_dst(hi, k, group, ffn).bitcast(F32), op0=ALU.mult,
                                         op1=ALU.subtract).then_inc(turn_lo, 1)
                c.turn += 1

        GROUPS = [[0, 1, 2, 3], [4, 5, 6, 7], [8]]
        eps_ap = sb_at("eps_ap", [P, 1], top)

        def xt(t):
            return x[0:ROWS[t], t, :]

        def mt(t):
            return mem_raw[:, t, :]

        def xt_k(t, k):
            return x[0:ROWS[t], t, k * P:(k + 1) * P]

        def mt_k(t, k):
            return mem_raw[:, t, k * P:(k + 1) * P]

        def dve_norm_x(dve, c, gain0, ffn):
            for group in GROUPS:
                dve_inv(dve, c, group)
                for t in group:
                    dve_diag(dve, c, t)
            for group in GROUPS:
                dve_turn(dve, c, act_hi, act_lo, group, KT, gain0, ffn)

        def pe_norm_x(pe, c):
            for group in GROUPS:
                c.xn += len(group)
                pe_turn(pe, c, xt_k, group, KT, lambda e: e.wait_ge(xn_ok, c.xn), True)

        def act_norm_x(act, c, gain0, ffn, wait_src):
            for group in GROUPS:
                act_norm(act, c, xt, group, wait_src, D, 6 if ffn else 4)
            for group in GROUPS:
                act_turn(act, c, act_hi, group, KT, gain0, ffn)

        def pool_mem(pool, l):
            if l:
                pool.wait_ge(dn_ev, DC + 18 * NFT)
                pool.wait_ge(tl_out[0], 16 * 4)
                pool.wait_ge(tl_out[1], 16 * 3)
            pool.dma_start(mem_raw[:, :, :], A["mem_prompt"][0].rearrange("(t p) d -> p t d", p=P)).then_inc(mem_ld, 16)

        def act_mem(act, c, l):
            act_norm(act, c, mt, [0, 1], lambda e, t: e.wait_ge(mem_ld, 16 * (l + 1)))
            act_turn(act, c, mem_hi, [0, 1], KT, 32 + 8 * l, False)

        def dve_mem(dve, c, l):
            dve_inv(dve, c, [0, 1])
            for t in range(2):
                dve_diag(dve, c, t)
            dve_turn(dve, c, mem_hi, mem_lo, [0, 1], KT, 32 + 8 * l, False)

        def pe_mem(pe, c, l):
            c.xn += 2
            if l:
                pe.wait_ge(dn_ev, DC + 18 * NFT)
                pe.wait_ge(tl_ev, 7)
            pe_turn(pe, c, mt_k, [0, 1], KT, lambda e: e.wait_ge(xn_ok, c.xn), True)

        def pe_kv(pe, c, l):
            pe.wait_ge(turn_lo, c.turn)
            for u in range(2):
                n = kv0[l] + u
                pe.wait_ge(w_ok, n + 1)
                for t in range(2):
                    for k in range(KT):
                        last = mm3(pe, ps[:, 4 + 2 * u + t, 0:UW], mem_hi[:, k, t * P:(t + 1) * P],
                                   mem_lo[:, k, t * P:(t + 1) * P], w_hi[:, n % 2, k, :], w_lo[:, n % 2, k, :],
                                   k == 0, k == KT - 1)
                    last.then_inc(w_used if t else kv_mm, 1)

        def act_kv(act, c, l):
            for u in range(2):
                n = kv0[l] + u
                split_hi(act, n + 1, (n + 1) % 2)
                for t in range(2):
                    if t:
                        act.wait_ge(w_used, n + 1)
                    else:
                        act.wait_ge(kv_mm, 2 * l + u + 1)
                    act.activation(mkv[:, t, u * UW:(u + 1) * UW], ps[:, 4 + 2 * u + t, 0:UW], ACT.Copy).then_inc(kv_ev, 1)
            act.wait_ge(kv_st, 7 * l + 2)
            act.activation(kv_stat[:, 1, :], kv_stat[:, 0, :], ACT.Sqrt, scale=1.0 / HD, bias=eps_ap[:, 0:1]).then_inc(kv_root, 1)

        def dve_kv(dve, c, l):
            for u in range(2):
                split_lo(dve, kv0[l] + u + 1, (kv0[l] + u + 1) % 2)
            dve.memset(mk_bd[:, :, :], 0.0).then_inc(kv_ok, 1)
            dve.memset(mv_pad[:, :, :, :], 0.0).then_inc(kv_ok, 1)
            dve.wait_ge(kv_ev, 4 * l + 4)
            keys = mkv[:, :, 0:MEMW].rearrange("p t (h d) -> p t h d", d=HD)
            dve.tensor_tensor(kv_sq[:, :, :], mkv[:, :, 0:MEMW], mkv[:, :, 0:MEMW], ALU.mult).then_inc(kv_st, 1)
            dve.wait_ge(kv_st, 7 * l + 1)
            dve.tensor_reduce(kv_stat[:, 0, :].rearrange("p (t h) -> p t h", h=MH),
                              kv_sq[:, :, :].rearrange("p t (h d) -> p t h d", d=HD), AX_X, ALU.add).then_inc(kv_st, 1)
            dve.wait_ge(kv_root, l + 1)
            dve.reciprocal(kv_stat[:, 2, :], kv_stat[:, 1, :]).then_inc(kv_st, 1)
            dve.wait_ge(kv_st, 7 * l + 3)
            for t in range(2):
                dve.tensor_tensor(keys[:, t], keys[:, t],
                                  kv_stat[:, 2, 4 * t:4 * t + 4].unsqueeze(2).broadcast_to([P, MH, HD]),
                                  ALU.mult).then_inc(kv_st, 1)
            dve.wait_ge(kv_st, 7 * l + 5)
            for t in range(2):
                dve.tensor_tensor(keys[:, t], keys[:, t], qk_gain[:, 2 + l, :].unsqueeze(1).broadcast_to([P, MH, HD]),
                                  ALU.mult).then_inc(kv_st, 1)
            dve.wait_ge(kv_ok, 8 * l + 2)
            for hh in range(2):
                dve.tensor_copy(mv_pad[:, :, :, :].rearrange("p t (a b) c -> p t a b c", b=2)[:, :, :, hh, hh * HD:(hh + 1) * HD],
                                mkv[:, :, MEMW:].rearrange("p t (a b d) -> p t a b d", b=2, d=HD)[:, :, :, hh, :]).then_inc(kv_ok, 1)

        def dve_kv_turn(dve, l):
            for a in range(2):
                dve.wait_ge(kv_tr, 2 * l + a + 1)
                for hh in range(2):
                    dve.tensor_copy(mk_bd[hh * HD:(hh + 1) * HD, a, hh * M:(hh + 1) * M],
                                    ps[hh * HD:(hh + 1) * HD, 4 + a, 0:M]).then_inc(kv_ok, 1)

        def pe_kv_turn(pe, c, l):
            pe.wait_ge(kv_st, 7 * l + 7)
            for a in range(2):
                for t in range(2):
                    last = pe.transpose(ps[:, 4 + a, t * P:(t + 1) * P], mkv[:, t, a * P:(a + 1) * P], ident[:, :])
                last.then_inc(kv_tr, 1)
            pe.wait_ge(kv_ok, 8 * (l + 1))

        def pool_kv(pool, l):
            pool.wait_ge(kv_st, 7 * l + 7)
            pool.wait_ge(kv_ev, 4 * l + 4)
            for half, name in enumerate(("mem_k", "mem_v")):
                pool.dma_start(O[name][l, 0].rearrange("(t p) h d -> p t (h d)", p=P),
                               mkv[:, :, half * MEMW:(half + 1) * MEMW]).then_inc(kv_out, 16)

        def pe_in_unit(pe, l, u, n, par, t0):
            pe.wait_ge(w_ok, n + 1)
            for t in range(NT):
                pe.wait_ge(in_ev, t0 + t + 1)
                for k in range(KT):
                    last = mm3(pe, ps[0:ROWS[t], t % CB, 0:UW], act_hi[:, k, tok_cols(t)], act_lo[:, k, tok_cols(t)],
                               w_hi[:, par, k, :], w_lo[:, par, k, :], k == 0, k == KT - 1)
                last.then_inc(w_used if t == NT - 1 else in_mm, 1)

        ORDER0 = [3, 4, 5, 0, 1, 2, 6]
        V_UNITS = MIX // UW
        STORED = [IN_U[0] - V_UNITS, IN_U[1]]

        def act_in_unit(act, n, par, un, dst, func, stored=None, after=None):
            split_hi(act, n + 1, 1 - par)
            if stored is not None:
                act.wait_ge(stage_free, stored + 1)
            for t in range(NT):
                if t == NT - 1:
                    act.wait_ge(w_used, n + 1)
                else:
                    act.wait_ge(in_mm, 8 * un + t + 1)
                act.activation(dst(t), ps[0:ROWS[t], t % CB, 0:UW], func).then_inc(in_ev, 1)
                if after:
                    after(t)

        def staged(h):
            return lambda t: stage[0:ROWS[t], h, t, :]

        def act_in(act, c, l):
            act.wait_ge(kv_st, 7 * (l + 1))
            if l:
                in_units(act, l, lambda u, n, par, un: act_in_unit(act, n, par, un, staged((IN_U[0] + 1 + in0[1] + par) % 2),
                                                                   ACT.Copy, un - (IN_U[0] - STORED[0])))
                return

            def square(t):
                if c.ssq:
                    act.wait_ge(ssq_ok, c.ssq)
                act.activation(ps[0:ROWS[t], 6:8, :].rearrange("p a b -> p (a b)")[:, 0:MIX], v_all[0:ROWS[t], t, :],
                               ACT.Square, accum_out=ssq[0:ROWS[t], t:t + 1]).then_inc(ssq_ok, 1)
                c.ssq += 1

            for n, u in enumerate(ORDER0):
                func = ACT.Copy if u == 6 else ACT.Gelu_apprx_tanh
                if n < V_UNITS:
                    act_in_unit(act, in0[0] + n, (in0[0] + n) % 2, n,
                                lambda t: v_all[0:ROWS[t], t, (u - V_UNITS) * UW:(u - V_UNITS + 1) * UW], func)
                else:
                    if n == V_UNITS:
                        act.wait_ge(in_ev, CB + 9 * V_UNITS)
                    act_in_unit(act, in0[0] + n, (in0[0] + n) % 2, n, staged((n - V_UNITS) % 2), func, n - V_UNITS,
                                square if n == V_UNITS else None)
            act.wait_ge(ssq_ok, c.ssq)
            act.activation(root[:, :], ssq[:, :], ACT.Sqrt, scale=1.0 / MIX, bias=eps_ap[:, 0:1]).then_inc(root_ok, 1)

        def pool_in_unit(pool, col, h, un, stored):
            pool.wait_ge(in_ev, CB + 9 * un + 9)
            pool.dma_start(proj[0:SEQ, bass.ds(col * UW, UW)].rearrange("(t p) f -> p t f", p=P),
                           stage[:, h, 0:NPT, :]).then_inc(in_st, 16)
            pool.dma_start(proj[SEQ:NTOK, bass.ds(col * UW, UW)], stage[0:NS, h, NPT, :]).then_inc(in_st, 16)
            pool.wait_ge(in_st, 32 * stored + 32)
            pool.sem_inc(stage_free, 1)

        def pool_in(pool, l):
            if l:
                in_units(pool, l, lambda u, n, par, un: pool_in_unit(pool, u, (IN_U[0] + 1 + in0[1] + par) % 2, un,
                                                                     un - (IN_U[0] - STORED[0])))
            else:
                for n in range(V_UNITS, IN_U[0]):
                    pool_in_unit(pool, ORDER0[n], (n - V_UNITS) % 2, n, n - V_UNITS)

        def in_units(eng, l, body):
            un0 = 0 if l == 0 else IN_U[0]
            with eng.Fori(0, IN_U[l] // 2) as i:
                for h in range(2):
                    body(i * 2 + h, i * 2 + (in0[l] + h), (in0[l] + h) % 2, i * 2 + (un0 + h))
            if IN_U[l] % 2:
                u = IN_U[l] - 1
                body(u, in0[l] + u, (in0[l] + u) % 2, un0 + u)

        IN_ST = [32 * STORED[0], 32 * (STORED[0] + STORED[1])]

        def pool_gm_load(pool):
            pool.wait_ge(in_st, IN_ST[0])
            pool.wait_ge(kv_out, 32)
            pool.wait_ge(kv_tr, 2)
            pool_masks(pool, [(same_batch[:, :], 1.0)], [
                (same_batch[:, :].rearrange("p (b t) -> p b t", t=NQ), ALU.is_ge, 0.0, 0, [[-8, NB], [0, NQ]], 1),
                (same_batch[:, :].rearrange("p (b t) -> p b t", t=NQ), ALU.is_ge, 0.0, 7, [[8, NB], [0, NQ]], -1)])
            pool.dma_start(ws_raw[:, :, :], A["gm_ws"][0].rearrange("g t s -> t g s")).then_inc(gm_set, 16)
            pool.dma_start(bias_raw[:, :], A["gm_bs"][0]).then_inc(gm_set, 16)
            pool.wait_ge(gm_set, 32)
            pool.affine_select(out=ws_raw[:, :, :], in_=ws_raw[:, :, :], compare_op=ALU.is_ge, fill=0.0, base=0,
                               pattern=[[0, 6], [-1, P]], channel_multiplier=1).then_inc(masked, 1)
            pool_masks.masked += 1
            GM["masked"] = pool_masks.masked
            pool.wait_ge(gm_setmm, 2)
            pool.dma_start(gm_gain[:, :], A["gm_v_norm"][0].partition_broadcast(P)).then_inc(gm_set, 16)
            for t in range(NT):
                if t >= 4:
                    pool.wait_ge(turned, TURN["gm"] + 6 * (t // 4))
                src = proj[t * P:t * P + ROWS[t], 0:MIX]
                pool.dma_start(gm_cat[0:ROWS[t], t % 4, :], src).then_inc(gm_u[t % 4], 16)
            pool.wait_ge(gm_v, NT)
            pool.dma_start(O["gm_v"][0].rearrange("b t f -> (b t) f"), v_all[0:NS, NPT, :]).then_inc(gm_out, 16)

        GM = {"masked": 0}
        TURN = {"gm": KT + 3 * KT}
        GM_MASKED = SET_MASKS + 2 + 1

        def pe_gm(pe, c):
            pe.wait_ge(masked, GM_MASKED)
            for g in range(6):
                last = pe.transpose(ps[:, 4 + g // 4, (g % 4) * P:(g % 4) * P + P], ws_raw[:, g, :], ident[:, :])
            last.then_inc(gm_setmm, 1)
            pe.transpose(ps[:, 6, 0:6], bias_raw[:, :], ident[0:6, 0:6]).then_inc(gm_setmm, 1)
            pe.wait_ge(gm_gelu, 3)
            rep = rep8[:, :, :].rearrange("p b q -> p (b q)")
            pe.matmul(ps[0:NS, 7, 0:6 * NQ], rep, w_t[0:NQ, :, 0:NQ], start=True, stop=True).then_inc(gm_setmm, 1)
            pe.matmul(ps[0:NS, 6, 8:14], rep, bias_t[0:NQ, :], start=True, stop=True).then_inc(gm_setmm, 1)
            pe.wait_ge(gm_gelu, 5)
            for group in GROUPS:
                for t in group:
                    pe.wait_ge(gm_v, t + 1)
                    if t >= 2:
                        pe.wait_ge(gm_cat_ok, 6 * (t - 1))
                    lhs = w_t if t < NPT else w_s
                    b = 4 + 2 * (t % 2)
                    for g in range(6):
                        last = pe.matmul(ps[0:ROWS[t], b + g // 4, (g % 4) * P:(g % 4) * P + P], lhs[0:ROWS[t], g, :],
                                         v_all[0:ROWS[t], t, g * P:(g + 1) * P], start=(g % 4 == 0), stop=True,
                                         skip_group_check=True)
                    last.then_inc(gm_mix, 1)
                pe_turn(pe, c, lambda t, k: gm_cat[0:ROWS[t], t % 4, k * P:(k + 1) * P], group, 6,
                        lambda e: e.wait_ge(gm_cat_ok, 6 * (group[-1] + 1)))

        def act_gm(act, c):
            for group in GROUPS:
                act_turn(act, c, act_hi, group, 6, None, False)

        def dve_gm(dve, c):
            dve.wait_ge(gm_setmm, 2)
            dve.tensor_copy(w_t[:, 0:4, :].rearrange("p g t -> p (g t)"), ps[:, 4, :]).then_inc(gm_gelu, 1)
            dve.tensor_copy(w_t[:, 4:6, :].rearrange("p g t -> p (g t)"), ps[:, 5, 0:2 * P]).then_inc(gm_gelu, 1)
            dve.tensor_copy(bias_t[:, :], ps[:, 6, 0:6]).then_inc(gm_gelu, 1)
            dve.wait_ge(gm_setmm, 4)
            dve.tensor_tensor(w_s[:, :, :].rearrange("p g (b t) -> p g b t", t=NQ),
                              ps[0:NS, 7, 0:6 * NQ].rearrange("p (g t) -> p g t", t=NQ).unsqueeze(2).broadcast_to([NS, 6, NB, NQ]),
                              same_batch[:, :].rearrange("p (b t) -> p b t", t=NQ).unsqueeze(1).broadcast_to([NS, 6, NB, NQ]),
                              ALU.mult).then_inc(gm_gelu, 1)
            dve.tensor_copy(bias_s[:, :], ps[0:NS, 6, 8:14]).then_inc(gm_gelu, 1)
            dve_inv(dve, c, range(NT))
            dve.wait_ge(gm_set, 48)
            for group in GROUPS:
                for t in group:
                    v = v_all[0:ROWS[t], t, :]
                    dve.scalar_tensor_tensor(out=v, in0=v, scalar=inv[0:ROWS[t], t:t + 1], in1=gm_gain[0:ROWS[t], :],
                                             op0=ALU.mult, op1=ALU.mult).then_inc(gm_v, 1)
            for group in GROUPS:
                for t in group:
                    dve.wait_ge(gm_mix, t + 1)
                    dve.wait_ge(gm_u[t % 4], 16 * (t // 4 + 1))
                    b = 4 + 2 * (t % 2)
                    bias = bias_t if t < NPT else bias_s
                    for g in range(6):
                        u = gm_cat[0:ROWS[t], t % 4, g * P:(g + 1) * P]
                        dve.scalar_tensor_tensor(out=u, in0=ps[0:ROWS[t], b + g // 4, (g % 4) * P:(g % 4) * P + P],
                                                 scalar=bias[0:ROWS[t], g:g + 1], in1=u, op0=ALU.add,
                                                 op1=ALU.mult).then_inc(gm_cat_ok, 1)
                dve_turn(dve, c, act_hi, act_lo, group, 6, None, False)

        BROWS = [(0, t) for t in range(NPT)] + [(1, t) for t in range(NPT - 1, -1, -1)]
        NR = len(BROWS)
        BGROUPS = [(r, k0, min(4, t + 1 - k0)) for r, (hh, t) in enumerate(BROWS) for k0 in range(0, t + 1, 4)]
        NG = len(BGROUPS)
        SEG_END = [max(n for n, (r, _, _) in enumerate(BGROUPS) if r // 4 == j) for j in range(4)]

        def row_groups(r):
            return [n for n, g in enumerate(BGROUPS) if g[0] == r]

        def pool_bp(pool):
            pool.wait_ge(ms_lo, 4)
            for name, c0 in (("sb_k", MIX), ("sb_v", 2 * MIX)):
                pool.dma_start(O[name + "_p"][0, 0].rearrange("t h d -> t (h d)"), proj[0:SEQ, c0:c0 + MIX]).then_inc(copied, 16)
                pool.dma_start(O[name + "_s"][0].rearrange("b t h d -> (b t) (h d)"), proj[SEQ:NTOK, c0:c0 + MIX]).then_inc(copied, 16)
            pool.dma_start(bias12[:, :], A["sb_bias"][0].partition_broadcast(P)).then_inc(bp_set, 16)
            pool_masks(pool, [(tri01[:, :], 1.0), (head12[:, :], 1.0)], [
                (tri01[:, :], ALU.is_gt, 0.0, 0, [[-1, P]], 1),
                (head12[:, :], ALU.is_ge, 0.0, 0, [[-8, SH]], 1),
                (head12[:, :], ALU.is_ge, 0.0, 7, [[8, SH]], -1)])

            def load(dst, c0, i, done):
                pool.dma_start(dst[:, :, :], proj[0:SEQ, bass.ds(i * P + c0, P)].rearrange("(t p) f -> p t f", p=P)).then_inc(done, 16)

            load(sbq_raw, 0, 0, bp_ld)
            load(sbk_raw, MIX, 0, bp_ld)
            load(sb_v, 2 * MIX, 0, bp_v)
            with pool.Fori(0, NPAIR - 1) as i:
                pool.wait_ge(bp_tr, i * 2 + 2)
                load(sbq_raw, 0, i + 1, bp_ld)
                load(sbk_raw, MIX, i + 1, bp_ld)
                pool.wait_ge(bp_av, i * NG + (NG + 2))
                load(sb_v, 2 * MIX, i + 1, bp_v)

        BP_MASKED = GM_MASKED + 3

        def pe_bp(pe):
            pe.wait_ge(ms_lo, 4)
            with pe.Fori(0, NPAIR) as i:
                pe.wait_ge(bp_ld, i * 32 + 32)
                pe.wait_ge(bp_sig, i * NR + 2)
                for n, raw in enumerate((sbq_raw, sbk_raw)):
                    for t in range(NPT):
                        last = pe.transpose(ps[:, 2 * n + t // 4, (t % 4) * P:(t % 4) * P + P], raw[:, t, :], ident[:, :])
                    last.then_inc(bp_tr, 1)
                pe.wait_ge(bp_q, i * 2 + 2)
                pe.wait_ge(bp_k, i * 2 + 2)
                pe.wait_ge(bp_b, i * 2 + 2)

                def scores(r):
                    hh, t = BROWS[r]
                    pe.wait_ge(bp_sig, i * NR + (r + 1))
                    w = (t + 1) * P
                    for c in range(0, w, 512):
                        n = min(512, w - c)
                        last = pe.matmul(ps[:, 2 * (r % 2) + c // 512, 0:n], sb_q[0:65, hh, t * P:(t + 1) * P],
                                         sb_k[0:65, hh, c:c + n], start=True, stop=True)
                    last.then_inc(bp_z, 1)

                def turn(n):
                    r, k0, nk = BGROUPS[n]
                    if k0 == 0:
                        pe.wait_ge(bp_a, i * NR + (r + 1))
                    for j in range(nk):
                        last = pe.transpose(ps[:, 4 + n % 2, j * P:(j + 1) * P], brk[:, r % 3, (k0 + j) * P:(k0 + j + 1) * P], ident[:, :])
                    last.then_inc(bp_t, 1)

                def use(n):
                    r, k0, nk = BGROUPS[n]
                    hh, t = BROWS[r]
                    if n == 0:
                        pe.wait_ge(bp_v, i * 16 + 16)
                    if r % 4 == 0 and k0 == 0:
                        pe.wait_ge(bp_lo, i * 4 + (r // 4 + 1))
                    pe.wait_ge(bp_at, i * NG + (n + 1))
                    for j in range(nk):
                        last = pe.matmul(ps[0:HD, 6 + (r // 4) % 2, (t % 4) * P:(t % 4) * P + P],
                                         sb_v[:, k0 + j, hh * HD:(hh + 1) * HD], brk_t[:, n % 2, j * P:(j + 1) * P],
                                         start=(k0 + j == 0), stop=(k0 + j == t), skip_group_check=True)
                    last.then_inc(bp_av, 1)

                for r in range(NR + 2):
                    if r < NR:
                        scores(r)
                    if r >= 2:
                        for n in row_groups(r - 2):
                            turn(n)
                            if n:
                                use(n - 1)
                use(NG - 1)

        def head_rows(tile, hh, i, r0):
            return tile[hh * HD:(hh + 1) * HD, bass.ds(i, 1), r0 * P:r0 * P + 512].rearrange("p a c -> p (a c)")

        def segment(j):
            return j // 2, (0, 4, 4, 0)[j], 6 + j % 2

        def act_bp(act):
            with act.Fori(0, NPAIR) as i:
                act.wait_ge(bp_tr, i * 2 + 1)
                for hh in range(2):
                    act.activation(sb_q[0:HD, hh, :], ps[hh * HD:(hh + 1) * HD, 0:2, :].rearrange("p a b -> p (a b)"),
                                   ACT.Copy, scale=HD ** -0.5).then_inc(bp_q, 1)

                def copy_out(j):
                    hh, t0, bank = segment(j)
                    act.wait_ge(bp_av, i * NG + (SEG_END[j] + 3))
                    act.activation(head_rows(act_hi, hh, i, t0), ps[0:HD, bank, :], ACT.Copy).then_inc(bp_hi, 1)

                for r in range(NR + 2):
                    if r < NR:
                        w = (BROWS[r][1] + 1) * P
                        act.wait_ge(bp_z, i * NR + (r + 1))
                        z = ps[:, 2 * (r % 2):2 * (r % 2) + 2, :].rearrange("p a b -> p (a b)")
                        act.activation(brk[:, r % 3, 0:w], z[:, 0:w], ACT.Sigmoid).then_inc(bp_sig, 1)
                    if r >= 2:
                        for n in row_groups(r - 2):
                            nk = BGROUPS[n][2]
                            act.wait_ge(bp_t, i * NG + (n + 1))
                            act.wait_ge(bp_av, i * NG + (n + 1))
                            act.activation(brk_t[:, n % 2, 0:nk * P], ps[:, 4 + n % 2, 0:nk * P], ACT.Copy).then_inc(bp_at, 1)
                            if n >= 2 and n - 2 in SEG_END:
                                copy_out(SEG_END.index(n - 2))
                copy_out(3)

        def dve_bp(dve):
            dve.wait_ge(ms_lo, 4)
            dve.memset(sb_k[HD:HD + 1, :, :], 1.0).then_inc(bp_one, 1)
            dve.memset(left[:, SEQ:SEQ + 1], 1.0).then_inc(bp_one, 1)
            dve.memset(zero1[:, :], 0.0).then_inc(bp_one, 1)
            dve.wait_ge(bp_one, 3)
            dve.wait_ge(bp_set, 16)
            dve.wait_ge(masked, BP_MASKED)
            with dve.Fori(0, NPAIR) as i:
                dve.wait_ge(bp_tr, i * 2 + 2)
                for hh in range(2):
                    dve.tensor_copy(sb_k[0:HD, hh, :], ps[hh * HD:(hh + 1) * HD, 2:4, :].rearrange("p a b -> p (a b)")).then_inc(bp_k, 1)
                    dve.tensor_scalar(sb_q[HD:HD + 1, hh, :], sb_k[HD:HD + 1, hh, :], bias12[HD:HD + 1, bass.ds(i * 2 + hh, 1)],
                                      None, ALU.mult).then_inc(bp_b, 1)

                def copy_out(j):
                    hh, t0, bank = segment(j)
                    dve.wait_ge(bp_hi, i * 4 + (j + 1))
                    dve.tensor_tensor(head_rows(act_lo, hh, i, t0), ps[0:HD, bank, :], head_rows(act_hi, hh, i, t0).bitcast(F32),
                                      ALU.subtract).then_inc(bp_lo, 1)

                for r in range(NR):
                    t = BROWS[r][1]
                    w = (t + 1) * P
                    s = brk[:, r % 3, 0:w]
                    c = left[:, SEQ - w:SEQ]
                    dve.wait_ge(bp_sig, i * NR + (r + 3))
                    d = brk[:, r % 3, t * P:w]
                    dve.tensor_tensor(d, d, tri01[:, :], ALU.mult).then_inc(bp_msk, 1)
                    dve.wait_ge(bp_msk, i * NR + (r + 1))
                    dve.tensor_scalar(c, s, -1.0, 1.0, ALU.mult, ALU.add).then_inc(bp_keep, 1)
                    dve.wait_ge(bp_keep, i * NR + (r + 1))
                    dve.tensor_tensor_scan(c[:, ::-1], c[:, ::-1], zero1[:, 0:1].broadcast_to([P, w]), 1.0, ALU.mult,
                                           ALU.add).then_inc(bp_left, 1)
                    dve.wait_ge(bp_left, i * NR + (r + 1))
                    dve.tensor_tensor(s, s, left[:, SEQ - w + 1:SEQ + 1], ALU.mult).then_inc(bp_a, 1)
                    dve.wait_ge(bp_a, i * NR + (r + 1))
                    done = [j for j in range(4) if r >= 2 and BGROUPS[SEG_END[j]][0] == r - 3]
                    for j in done:
                        copy_out(j)
                copy_out(3)

        NGR = PAGES // 2
        page_t = sb_at("page_t", [1, NB * PAGES], top + 64, I32)
        free_half = 1 - out0[1] % 2
        pv_raw = w_raw[:, :, :].rearrange("p k f -> p (k f)")[:, 0:2 * MIX].rearrange("p (j f) -> p j f", j=2)

        def pv(hi, g, j):
            if g % 2:
                return (pv_hi1 if hi else pv_lo1)[:, j, :]
            return (w_hi if hi else w_lo)[:, free_half].rearrange("p k f -> p (k f)")[:, j * MIX:(j + 1) * MIX]

        q_hi, q_lo = (w[:, free_half].rearrange("p k f -> p (k f)")[:, 2 * MIX:2 * MIX + NPAIR * NS]
                      .rearrange("p (a c) -> p a c", a=NPAIR) for w in (w_hi, w_lo))

        def gw(g):
            return 2 * P + (NQ if g == 0 else 0)

        def sp_bs(sp):
            sp.wait_ge(bs_set, 16)
            sp.wait_ge(bp_lo, 2 + 4 * NPAIR)
            sp.wait_ge(w_ok, out0[1] + 1)
            sp.dma_start(pk_raw[0:NS, 0, :], proj[SEQ:NTOK, 0:MIX]).then_inc(bs_in, 16)
            sp.dma_start(pk_raw[0:NS, 1, :], proj[SEQ:NTOK, MIX:2 * MIX]).then_inc(bs_in, 16)
            with sp.Fori(0, NB) as b:

                def page(g, j):
                    return sp.value_load(page_t[0:1, bass.ds(b * PAGES + (PAGES - 2 - 2 * g + j), 1)])

                for g in range(NGR + 1):
                    if g < NGR:
                        pages = [page(g, j) for j in range(2)]
                        sp.wait_ge(bs_tr, b * (3 * NGR) + (3 * g + 3))
                        for j in range(2):
                            sp.dma_start(pk_raw[:, 2 * (g % 2) + j, :],
                                         A["cache_sb_k"][0, bass.ds(pages[j], 1)].rearrange("a t h d -> t (a h d)")).then_inc(bs_k[g % 2], 16)
                    if g == 0:
                        sp.wait_ge(bs_av, b * NGR + 2)
                        sp.dma_start(v_new[:, :], proj[bass.ds(b * NQ + SEQ, NQ), 2 * MIX:3 * MIX]).then_inc(bs_vn, 16)
                    else:
                        pages = [page(g - 1, j) for j in range(2)]
                        for j in range(2):
                            sp.wait_ge(bs_vl[j], b * NGR + g)
                            sp.dma_start(pv_raw[:, j, :],
                                         A["cache_sb_v"][0, bass.ds(pages[j], 1)].rearrange("a t h d -> t (a h d)")).then_inc(bs_v[j], 16)

        def pool_bs(pool):
            pool.dma_start(page_t[:, :], A["page_table"].rearrange("b p -> (b p)").unsqueeze(0)).then_inc(bs_set, 16)
            with pool.Fori(0, NB) as b:
                for g in range(NGR):
                    pool.wait_ge(bs_vh, b * (2 * NGR) + (2 * g + 2))
                    pool.tensor_tensor(pv(False, g, 1), pv_raw[:, 1, :], pv(True, g, 1).bitcast(F32), ALU.subtract).then_inc(bs_vl[1], 1)

        def pe_bs(pe):
            pe.wait_ge(bs_in, 32)
            pe.wait_ge(bp_lo, 2 + 4 * NPAIR)
            for n in range(2):
                for a in range(NPAIR):
                    last = pe.transpose(ps[:, n, a * NS:(a + 1) * NS], pk_raw[0:NS, n, a * P:(a + 1) * P], ident[0:NS, 0:NS])
            last.then_inc(bs_tr, 6)
            with pe.Fori(0, NB) as b:

                def turn(g, c):
                    if c == 0:
                        pe.wait_ge(bs_k[g % 2], b * (16 * NGR) + 32 * (g // 2 + 1))
                    for u in range(2):
                        for j in range(2):
                            a = 2 * c + u
                            last = pe.transpose(ps[:, c, (2 * u + j) * P:(2 * u + j + 1) * P],
                                                pk_raw[:, 2 * (g % 2) + j, a * P:(a + 1) * P], ident[:, :])
                    last.then_inc(bs_tr, 1)

                def scores(g, c):
                    pe.wait_ge(bs_kl, b * (3 * NGR) + (3 * g + c + 1))
                    w = gw(g)
                    for a in (2 * c, 2 * c + 1):
                        last = mm3(pe, ps[0:96, 3 + g % 2, 0:w], qb_hi[:, a * 96:(a + 1) * 96], qb_lo[:, a * 96:(a + 1) * 96],
                                   pk_hi[:, a, 0:w], pk_lo[:, a, 0:w], a == 0, a == NPAIR - 1)
                    if c == 2:
                        last.then_inc(bs_z, 1)

                def turn_weights(g):
                    pe.wait_ge(bs_a, b * NGR + (g + 1))
                    for j in range(2):
                        last = pe.transpose(ps[:, 5, j * 96:(j + 1) * 96], s_brk[:, g % 2, j * P:(j + 1) * P], ident[0:96, 0:96])
                    if g == 0:
                        last = pe.transpose(ps[0:NQ, 5, 192:288], s_brk[:, 0, 2 * P:2 * P + NQ], ident[0:96, 0:96])
                    last.then_inc(bs_at, 1)

                def use(g):
                    pe.wait_ge(bs_al, b * NGR + (g + 1))
                    for j in range(2):
                        pe.wait_ge(bs_vl[j], b * NGR + (g + 2))
                    if g == 0:
                        pe.wait_ge(bs_vn, b * 16 + 16)
                    for j in range(2):
                        for c in range(2):
                            cols = slice(c * 384, (c + 1) * 384)
                            last = mm3(pe, ps[0:96, 6 + c, 0:384], at_hi[:, g % 2, j, :], at_lo[:, g % 2, j, :],
                                       pv(True, g, j)[:, cols], pv(False, g, j)[:, cols], g == 0 and j == 0,
                                       g == NGR - 1 and j == 1)
                    if g == 0:
                        for c in range(2):
                            last = pe.matmul(ps[0:96, 6 + c, 0:384], at_new[:, :], v_new[:, c * 384:(c + 1) * 384],
                                             start=False, stop=False)
                    last.then_inc(bs_av, 1)

                pe.wait_ge(bs_qb, b * 4 + 4)
                pe.wait_ge(bs_kn, b * 2 + 2)
                for c in range(3):
                    turn(0, c)
                for g in range(NGR):
                    if g:
                        turn_weights(g - 1)
                    for c in range(3):
                        scores(g, c)
                        if g + 1 < NGR:
                            turn(g + 1, c)
                    if g:
                        use(g - 1)
                turn_weights(NGR - 1)
                use(NGR - 1)
                pe.wait_ge(bs_o, b * 2 + 2)
                for a in range(NPAIR):
                    last = pe.matmul(ps[:, 5, a * NQ:(a + 1) * NQ], s_out[:, a * P:(a + 1) * P], query_of[0:96, :],
                                     start=True, stop=True, skip_group_check=True)
                last.then_inc(bs_mt, 1)
                pe.wait_ge(bs_lo, b + 1)

        def act_bs(act):
            act.wait_ge(bs_tr, 6)
            act.activation(q_hi[:, :, :].rearrange("p a c -> p (a c)"), ps[:, 0, 0:NPAIR * NS], ACT.Copy,
                           scale=HD ** -0.5).then_inc(bs_q, 1)
            act.wait_ge(bs_n, NQ + 5)
            act.wait_ge(bs_q, 3)
            with act.Fori(0, NB) as b:

                def keys(g, c):
                    act.wait_ge(bs_tr, b * (3 * NGR) + (3 * g + c + 7))
                    act.activation(pk_hi[:, 2 * c:2 * c + 2, 0:2 * P], ps[:, c, :].rearrange("p (u c) -> p u c", u=2),
                                   ACT.Copy).then_inc(bs_kh, 1)

                def values(g, j):
                    act.wait_ge(bs_v[j], b * (16 * NGR) + 16 * (g + 1))
                    act.wait_ge(bs_av, b * NGR + (g + 1))
                    act.activation(pv(True, g, j), pv_raw[:, j, :], ACT.Copy).then_inc(bs_vh, 1)

                def breaks(g):
                    w = gw(g)
                    act.wait_ge(bs_z, b * NGR + (g + 1))
                    act.activation(s_brk[:, g % 2, 0:w], ps[0:96, 3 + g % 2, 0:w], ACT.Sigmoid, bias=bias96[:, 0:1]).then_inc(bs_sig, 1)

                def weights(g):
                    act.wait_ge(bs_at, b * NGR + (g + 1))
                    act.activation(at_hi[:, g % 2, :, :].rearrange("p j c -> p (j c)"), ps[:, 5, 0:192], ACT.Copy).then_inc(bs_ah, 1)
                    if g == 0:
                        act.activation(at_new[:, :], ps[0:NQ, 5, 192:288], ACT.Copy).then_inc(bs_ah, 1)

                for hh in range(2):
                    rows = slice(hh * HD, (hh + 1) * HD)
                    act.activation(qb_hi[rows, :].rearrange("p (a c) -> p a c", c=112)[:, :, hh * NQ:(hh + 1) * NQ],
                                   q_hi[rows, :, bass.ds(b * NQ, NQ)].bitcast(F32), ACT.Copy).then_inc(bs_qb, 1)
                act.activation(pk_hi[:, :, 2 * P:2 * P + NQ], kn_t[:, :, bass.ds(b * NQ, NQ)], ACT.Copy).then_inc(bs_kn, 1)
                for c in range(3):
                    keys(0, c)
                for g in range(NGR):
                    if g:
                        weights(g - 1)
                    more = g + 1 < NGR
                    if more:
                        keys(g + 1, 0)
                    values(g, 0)
                    if more:
                        keys(g + 1, 1)
                    values(g, 1)
                    breaks(g)
                    if more:
                        keys(g + 1, 2)
                weights(NGR - 1)
                act.wait_ge(bs_mt, b + 1)
                act.activation(act_hi[:, 0:NPAIR, bass.ds(b * NQ + SEQ, NQ)],
                               ps[:, 5, 0:NPAIR * NQ].rearrange("p (a q) -> p a q", q=NQ), ACT.Copy).then_inc(bs_hi, 1)

        def dve_bs(dve):
            dve.wait_ge(bp_lo, 2 + 4 * NPAIR)
            dve.memset(qb_hi[:, :].bitcast(F32), 0.0).then_inc(bs_n, 1)
            dve.memset(qb_lo[:, :].bitcast(F32), 0.0).then_inc(bs_n, 1)
            dve.memset(s_left[:, 0, gw(0):gw(0) + 1], 1.0).then_inc(bs_n, 1)
            dve.tensor_tensor(head_b[:, :], head12[:, :], bias12[0:96, :], ALU.mult).then_inc(bs_n, 1)
            dve.wait_ge(bs_n, 4)
            dve.tensor_reduce(bias96[:, :], head_b[:, :], AX_X, ALU.add).then_inc(bs_n, 1)
            dve.memset(new01[:, :], 0.0).then_inc(bs_n, 1)
            dve.wait_ge(bs_n, 6)
            for t in range(NQ - 1):
                dve.tensor_reduce(new01[:, t:t + 1], query_of[0:96, t + 1:NQ], AX_X, ALU.add).then_inc(bs_n, 1)
            dve.wait_ge(bs_n, NQ + 5)
            dve.wait_ge(bs_q, 1)
            dve.scalar_tensor_tensor(out=q_lo[:, :, :].rearrange("p a c -> p (a c)"), in0=ps[:, 0, 0:NPAIR * NS], scalar=HD ** -0.5,
                                     in1=q_hi[:, :, :].rearrange("p a c -> p (a c)").bitcast(F32), op0=ALU.mult,
                                     op1=ALU.subtract).then_inc(bs_q, 1)
            dve.tensor_copy(kn_t[:, :, :].rearrange("p a c -> p (a c)"), ps[:, 1, 0:NPAIR * NS]).then_inc(bs_q, 1)
            dve.wait_ge(bs_q, 3)
            with dve.Fori(0, NB) as b:

                def keys(g, c):
                    dve.wait_ge(bs_kh, b * (3 * NGR) + (3 * g + c + 1))
                    hi = pk_hi[:, 2 * c:2 * c + 2, 0:2 * P].bitcast(F32)
                    dve.tensor_tensor(pk_lo[:, 2 * c:2 * c + 2, 0:2 * P], ps[:, c, :].rearrange("p (u c) -> p u c", u=2), hi,
                                      ALU.subtract).then_inc(bs_kl, 1)

                def values(g):
                    dve.wait_ge(bs_vh, b * (2 * NGR) + (2 * g + 1))
                    dve.tensor_tensor(pv(False, g, 0), pv_raw[:, 0, :], pv(True, g, 0).bitcast(F32), ALU.subtract).then_inc(bs_vl[0], 1)

                def left_of(g):
                    w = gw(g)
                    n0 = b * NGR + (g + 1)
                    s = s_brk[:, g % 2, 0:w]
                    c = s_left[:, g % 2, 0:w]
                    before = s_left[:, 1 - g % 2, 0:1]
                    dve.wait_ge(bs_sig, n0)
                    if g == 0:
                        d = s_brk[:, 0, 2 * P:w]
                        dve.tensor_tensor(d, d, new01[:, :], ALU.mult).then_inc(bs_edge, 1)
                    else:
                        dve.tensor_copy(s_left[:, g % 2, w:w + 1], before).then_inc(bs_edge, 1)
                    dve.wait_ge(bs_edge, n0)
                    dve.tensor_scalar(c, s, -1.0, 1.0, ALU.mult, ALU.add).then_inc(bp_keep, 1)
                    dve.wait_ge(bp_keep, n0 + NPAIR * NR)
                    dve.tensor_tensor_scan(c[:, ::-1], c[:, ::-1], zero1[0:96, 0:1].broadcast_to([96, w]),
                                           before if g else 1.0, ALU.mult, ALU.add).then_inc(bp_left, 1)
                    dve.wait_ge(bp_left, n0 + NPAIR * NR)
                    dve.tensor_tensor(s, s, s_left[:, g % 2, 1:w + 1], ALU.mult).then_inc(bs_a, 1)
                    dve.wait_ge(bs_a, n0)

                def weights(g):
                    dve.wait_ge(bs_ah, b * (NGR + 1) + (g + 2))
                    dve.tensor_tensor(at_lo[:, g % 2, :, :].rearrange("p j c -> p (j c)"), ps[:, 5, 0:192],
                                      at_hi[:, g % 2, :, :].rearrange("p j c -> p (j c)").bitcast(F32), ALU.subtract).then_inc(bs_al, 1)

                for hh in range(2):
                    rows = slice(hh * HD, (hh + 1) * HD)
                    dve.tensor_copy(qb_lo[rows, :].rearrange("p (a c) -> p a c", c=112)[:, :, hh * NQ:(hh + 1) * NQ],
                                    q_lo[rows, :, bass.ds(b * NQ, NQ)].bitcast(F32)).then_inc(bs_qb, 1)
                dve.wait_ge(bs_kn, b * 2 + 1)
                dve.tensor_tensor(pk_lo[:, :, 2 * P:2 * P + NQ], kn_t[:, :, bass.ds(b * NQ, NQ)],
                                  pk_hi[:, :, 2 * P:2 * P + NQ].bitcast(F32), ALU.subtract).then_inc(bs_kn, 1)
                for c in range(3):
                    keys(0, c)
                for g in range(NGR):
                    if g:
                        weights(g - 1)
                    more = g + 1 < NGR
                    if more:
                        keys(g + 1, 0)
                    values(g)
                    if more:
                        keys(g + 1, 1)
                    left_of(g)
                    if more:
                        keys(g + 1, 2)
                weights(NGR - 1)
                dve.wait_ge(bs_av, b * NGR + (NGR + 2))
                for c in range(2):
                    dve.tensor_tensor(s_out[:, c * 384:(c + 1) * 384].rearrange("p (h d) -> p h d", d=HD),
                                      ps[0:96, 6 + c, 0:384].rearrange("p (h d) -> p h d", d=HD),
                                      head12[:, 6 * c:6 * c + 6].unsqueeze(2).broadcast_to([96, 6, HD]),
                                      ALU.mult).then_inc(bs_o, 1)
                dve.wait_ge(bs_hi, b + 1)
                cols = bass.ds(b * NQ + SEQ, NQ)
                dve.tensor_tensor(act_lo[:, 0:NPAIR, cols], ps[:, 5, 0:NPAIR * NQ].rearrange("p (a q) -> p a q", q=NQ),
                                  act_hi[:, 0:NPAIR, cols].bitcast(F32), ALU.subtract).then_inc(bs_lo, 1)

        def wait_attended(eng, l):
            if l == 0:
                eng.wait_ge(turn_lo, TURN["gm"] + 18)
                eng.wait_ge(gm_out, 16)
            else:
                eng.wait_ge(in_st, IN_ST[1])
                eng.wait_ge(kv_out, 64)
                eng.wait_ge(kv_tr, 4)

        MQC = [2304, 1024]

        def pool_mq(pool, l):
            wait_attended(pool, l)
            q0 = (2 * MIX, 3 * MIX)[l]
            pool.wait_ge(mem_pad, l + 1)
            pool.dma_start(mq[:, 0:NPT, :], proj[0:SEQ, q0:q0 + MEMW].rearrange("(t p) f -> p t f", p=P)).then_inc(mq_ld, 16)
            pool.dma_start(mq[0:NS, NPT, :], proj[SEQ:NTOK, q0:q0 + MEMW]).then_inc(mq_ld, 16)

        def dve_mq(dve, l):
            wait_attended(dve, l)
            dve.memset(mq[HD:P, NPT, :], 1.0).then_inc(mem_pad, 1)
            dve.wait_ge(mq_ld, 32 * l + 32)
            s0 = 4 * l
            heads = mq[:, :, :].rearrange("p t (h d) -> p (t h) d", d=HD)
            dve.tensor_tensor(mq_sq[:, :, :], mq[:, :, :], mq[:, :, :], ALU.mult).then_inc(mq_step, 1)
            dve.wait_ge(mq_step, s0 + 1)
            dve.tensor_reduce(mq_stat[:, 0, :], mq_sq[:, :, :].rearrange("p t (h d) -> p (t h) d", d=HD), AX_X,
                              ALU.add).then_inc(mq_step, 1)
            dve.wait_ge(mq_root, l + 1)
            dve.reciprocal(mq_stat[:, 2, :], mq_stat[:, 1, :]).then_inc(mq_step, 1)
            dve.wait_ge(mq_step, s0 + 3)
            dve.tensor_tensor(heads, heads, mq_stat[:, 2, :].unsqueeze(2).broadcast_to([P, NT * MH, HD]),
                              ALU.mult).then_inc(mq_step, 1)
            dve.wait_ge(mq_step, s0 + 4)
            gain = qk_gain[:, l, :].unsqueeze(1).broadcast_to([P, MH, HD])

            def scaled(t, h):
                if not (isinstance(t, int) and t < 2):
                    dve.wait_ge(mq_tr, t + (9 * l - 1))
                dve.tensor_tensor(mq_n[:, h, :].rearrange("p (h d) -> p h d", d=HD),
                                  mq[:, bass.ds(t, 1), :].rearrange("p a (h d) -> p (a h) d", d=HD), gain,
                                  ALU.mult).then_inc(mq_nm, 1)

            def largest(t, h):
                b = 2 + 2 * h
                dve.wait_ge(mq_s, t + (8 * l + 1))
                dve.tensor_reduce(sm_max[:, h, :], ps[:, b:b + 2, :].rearrange("p a (h m) -> p (a h) m", m=M), AX_X,
                                  ALU.max).then_inc(mq_mx, 1)
                dve.wait_ge(mq_mx, t * 2 + (16 * l + 1))
                dve.tensor_scalar(sm_max[:, h, :], sm_max[:, h, :], -HD ** -0.5, None, ALU.mult).then_inc(mq_mx, 1)

            def shares(t, h):
                dve.wait_ge(mq_ex, t * 4 + (32 * l + 4))
                dve.reciprocal(sm_inv[:, h, :], sm_sum[:, h, :]).then_inc(mq_pr, 1)
                dve.wait_ge(mq_pr, t * 2 + (16 * l + 1))
                dve.tensor_tensor(prob[:, h, :, :], prob[:, h, :, :],
                                  sm_inv[:, h, :].unsqueeze(2).broadcast_to([P, MH, M]), ALU.mult).then_inc(mq_pr, 1)

            def low(t, h):
                cols = bass.ds(t * P, P)
                dve.wait_ge(mq_hi, t + (8 * l + 1))
                dve.tensor_tensor(act_lo[:, NPAIR:KT, cols], ps[:, 1, 0:2 * P].rearrange("p (a c) -> p a c", c=P),
                                  act_hi[:, NPAIR:KT, cols].bitcast(F32), ALU.subtract).then_inc(mq_lo, 1)

            def body(t, h, more):
                if more:
                    scaled(t + 2, h)
                shares(t, h)
                if more:
                    largest(t + 2, h)
                low(t, h)

            scaled(0, 0)
            scaled(1, 1)
            largest(0, 0)
            largest(1, 1)
            mq_tiles(dve, body)

        def mq_tiles(eng, body):
            with eng.Fori(0, NPT // 2 - 1) as i:
                for h in range(2):
                    body(i * 2 + h, h, True)
            for h in range(2):
                body(NPT - 2 + h, h, False)

        def act_mq(act, l):
            act.wait_ge(mq_step, 4 * l + 2)
            act.activation(mq_stat[:, 1, :], mq_stat[:, 0, :], ACT.Sqrt, scale=1.0 / HD, bias=eps_ap[:, 0:1]).then_inc(mq_root, 1)

            def turned_q(t, h):
                act.wait_ge(mq_tr, t + (9 * l + 1))
                act.activation(mq_t[:, h, :, :].rearrange("p a c -> p (a c)"), ps[:, 0, 0:2 * P], ACT.Copy).then_inc(mq_tc, 1)

            def exps(t, h):
                act.wait_ge(mq_mx, t * 2 + (16 * l + 2))
                for hd in range(MH):
                    act.activation(prob[:, h, hd, :], ps[:, 2 + 2 * h + hd // 2, (hd % 2) * M:(hd % 2 + 1) * M], ACT.Exp,
                                   bias=sm_max[:, h, hd:hd + 1], scale=HD ** -0.5,
                                   accum_out=sm_sum[:, h, hd:hd + 1]).then_inc(mq_ex, 1)

            def body(t, h, more):
                if more:
                    turned_q(t + 2, h)
                act.wait_ge(mq_pt, t + (8 * l + 1))
                act.activation(prob_t[:, h].rearrange("p a h c -> p a (h c)"), ps[:, 6:8, :], ACT.Copy).then_inc(mq_pc, 1)
                if more:
                    exps(t + 2, h)
                act.wait_ge(mq_av, t + (8 * l + 1))
                act.activation(act_hi[:, NPAIR:KT, bass.ds(t * P, P)], ps[:, 1, 0:2 * P].rearrange("p (a c) -> p a c", c=P),
                               ACT.Copy).then_inc(mq_hi, 1)

            for h in range(2):
                turned_q(h, h)
            for h in range(2):
                exps(h, h)
            mq_tiles(act, body)

        def pe_mq(pe, l):

            def turn_q(t, h):
                pe.wait_ge(mq_nm, t + (9 * l + 1))
                if not (isinstance(t, int) and t == 0):
                    pe.wait_ge(mq_tc, t + 9 * l)
                for a in range(2):
                    last = pe.transpose(ps[:, 0, a * P:(a + 1) * P], mq_n[:, h, a * P:(a + 1) * P], ident[:, :])
                last.then_inc(mq_tr, 1)

            def scores(t, h):
                pe.wait_ge(mq_tc, t + (9 * l + 1))
                for a in range(2):
                    last = pe.matmul(ps[:, 2 + 2 * h + a, :], mq_t[:, h, a, :], mk_bd[:, a, :], start=True, stop=True)
                last.then_inc(mq_s, 1)

            def body(t, h, more):
                if more:
                    turn_q(t + 2, h)
                pe.wait_ge(mq_pr, t * 2 + (16 * l + 2))
                for m in range(2):
                    for hd in range(MH):
                        last = pe.transpose(ps[:, 6 + m, hd * P:(hd + 1) * P], prob[:, h, hd, m * P:(m + 1) * P], ident[:, :])
                last.then_inc(mq_pt, 1)
                if more:
                    scores(t + 2, h)
                pe.wait_ge(mq_pc, t + (8 * l + 1))
                pe.wait_ge(mq_lo, t + (8 * l + 2))
                for a in range(2):
                    for n in range(4):
                        hd, m = 2 * a + n // 2, n % 2
                        last = pe.matmul(ps[:, 1, a * P:(a + 1) * P], mv_pad[:, m, hd, :], prob_t[:, h, m, hd, :],
                                         start=(n == 0), stop=(n == 3), skip_group_check=True)
                last.then_inc(mq_av, 1)

            for h in range(2):
                turn_q(h, h)
                scores(h, h)
            mq_tiles(pe, body)
            pe.wait_ge(mq_lo, 2 + 8 * (l + 1))

        def sp_ms(sp, l):
            sp.wait_ge(mq_lo, 2 + 8 * (l + 1))
            for gr in range(2):
                G = 2 * l + gr
                if gr:
                    sp.wait_ge(ms_tr, 4 * G)
                    sp.wait_ge(ms_av, G)
                for b in range(4):
                    for dst, name in ((mkc, "cache_mem_k"), (mvc, "cache_mem_v")):
                        sp.dma_start(dst[:, b], A[name][l, 4 * gr + b].rearrange("(t p) h d -> p t (h d)", p=P)).then_inc(ms_ld, 16)

        def dve_ms(dve, l):
            gain = qk_gain[0:NS, l, :].unsqueeze(1).broadcast_to([NS, MH, HD])
            dve.tensor_tensor(mq_n[0:NS, 0, :].rearrange("p (h d) -> p h d", d=HD),
                              mq[0:NS, NPT, :].rearrange("p (h d) -> p h d", d=HD), gain, ALU.mult).then_inc(mq_nm, 1)
            dve.memset(mq_bd[:, :], 0.0).then_inc(ms_q, 1)
            dve.tensor_tensor(pick[:, :, :], batch_of[:, :].unsqueeze(2).broadcast_to([P, 4, NQ]),
                              query_of[:, :].unsqueeze(1).broadcast_to([P, 4, NQ]), ALU.mult).then_inc(ms_q, 1)
            dve.wait_ge(mq_tc, 9 * l + 9)
            for gr in range(2):
                G = 2 * l + gr
                if gr:
                    dve.wait_ge(ms_s, G)
                dve.wait_ge(ms_q, 10 * l + 2 + 4 * gr)
                for a in range(2):
                    for hh in range(2):
                        rows = slice(hh * HD, (hh + 1) * HD)
                        c = a * P + (2 * a + hh) * NQ
                        dve.tensor_copy(mq_bd[rows, :].rearrange("p (b c) -> p b c", c=288)[:, :, c:c + NQ],
                                        mq_t[rows, 0, a, gr * 32:gr * 32 + 32].rearrange("p (b q) -> p b q", q=NQ)).then_inc(ms_q, 1)
                s0 = 4 * G
                dve.wait_ge(ms_s, G + 1)
                dve.tensor_reduce(sm_max[:, 0, 0:1], ps[:, 4, 0:M], AX_X, ALU.max).then_inc(ms_step, 1)
                dve.wait_ge(ms_step, s0 + 1)
                dve.tensor_scalar(sm_max[:, 0, 0:1], sm_max[:, 0, 0:1], -HD ** -0.5, None, ALU.mult).then_inc(ms_step, 1)
                dve.wait_ge(ms_ex, G + 1)
                dve.reciprocal(sm_inv[:, 0, 0:1], sm_sum[:, 0, 0:1]).then_inc(ms_step, 1)
                dve.wait_ge(ms_step, s0 + 3)
                dve.tensor_scalar(prob_s[:, :], prob_s[:, :], sm_inv[:, 0, 0:1], None, ALU.mult).then_inc(ms_step, 1)
                dve.wait_ge(ms_av, G + 1)
                dve.tensor_tensor(ms_out[:, :].rearrange("p (h d) -> p h d", d=HD),
                                  ps[:, 6, 0:MEMW].rearrange("p (h d) -> p h d", d=HD),
                                  head_of[:, :].unsqueeze(2).broadcast_to([P, MH, HD]), ALU.mult).then_inc(ms_ok, 1)
                dve.wait_ge(ms_hi, G + 1)
                cols = slice(SEQ + 32 * gr, SEQ + 32 * gr + 32)
                dve.tensor_tensor(act_lo[:, NPAIR:KT, cols], ps[:, 7, 0:64].rearrange("p (a c) -> p a c", c=32),
                                  act_hi[:, NPAIR:KT, cols].bitcast(F32), ALU.subtract).then_inc(ms_lo, 1)

        def act_ms(act, l):
            act.wait_ge(mq_tr, 9 * l + 9)
            act.activation(mq_t[:, 0, :, 0:NS], ps[:, 0, 0:2 * NS].rearrange("p (a c) -> p a c", c=NS), ACT.Copy).then_inc(mq_tc, 1)
            for gr in range(2):
                G = 2 * l + gr
                if gr:
                    act.wait_ge(ms_s, G)
                for b in range(4):
                    act.wait_ge(ms_tr, 4 * G + b + 1)
                    act.activation(mkc_t[:, b, :, :].rearrange("p a m -> p (a m)"), ps[:, b, :], ACT.Copy).then_inc(ms_tc, 1)
                act.wait_ge(ms_step, 4 * G + 2)
                act.activation(prob_s[:, :], ps[:, 4, 0:M], ACT.Exp, bias=sm_max[:, 0, 0:1], scale=HD ** -0.5,
                               accum_out=sm_sum[:, 0, 0:1]).then_inc(ms_ex, 1)
                act.wait_ge(ms_pt, G + 1)
                act.activation(prob_st[:, :, :].rearrange("p a c -> p (a c)"), ps[:, 5, 0:2 * P], ACT.Copy).then_inc(ms_pc, 1)
                act.wait_ge(ms_mt, G + 1)
                cols = slice(SEQ + 32 * gr, SEQ + 32 * gr + 32)
                act.activation(act_hi[:, NPAIR:KT, cols], ps[:, 7, 0:64].rearrange("p (a c) -> p a c", c=32), ACT.Copy).then_inc(ms_hi, 1)

        def pe_ms(pe, l):
            pe.wait_ge(mq_nm, 9 * l + 9)
            for a in range(2):
                last = pe.transpose(ps[:, 0, a * NS:(a + 1) * NS], mq_n[0:NS, 0, a * P:(a + 1) * P], ident[0:NS, 0:NS])
            last.then_inc(mq_tr, 1)
            pe.wait_ge(mq_tc, 9 * l + 9)
            for gr in range(2):
                G = 2 * l + gr
                pe.wait_ge(ms_ld, 128 * (G + 1))
                for b in range(4):
                    if gr:
                        pe.wait_ge(ms_tc, 4 * (G - 1) + b + 1)
                    for a in range(2):
                        for m in range(2):
                            last = pe.transpose(ps[:, b, (2 * a + m) * P:(2 * a + m + 1) * P], mkc[:, b, m, a * P:(a + 1) * P], ident[:, :])
                    last.then_inc(ms_tr, 1)
                pe.wait_ge(ms_q, 10 * l + 6 + 4 * gr)
                pe.wait_ge(ms_tc, 4 * G + 4)
                for b in range(4):
                    for a in range(2):
                        n = 2 * b + a
                        last = pe.matmul(ps[:, 4, 0:M], mq_bd[:, n * P:(n + 1) * P], mkc_t[:, b, a, :], start=(n == 0), stop=(n == 7))
                last.then_inc(ms_s, 1)
                pe.wait_ge(ms_step, 4 * G + 4)
                for m in range(2):
                    last = pe.transpose(ps[:, 5, m * P:(m + 1) * P], prob_s[:, m * P:(m + 1) * P], ident[:, :])
                last.then_inc(ms_pt, 1)
                pe.wait_ge(ms_pc, G + 1)
                for b in range(4):
                    for m in range(2):
                        last = pe.matmul(ps[32 * b:32 * b + 32, 6, 0:MEMW], prob_st[:, m, 32 * b:32 * b + 32], mvc[:, b, m, :],
                                         start=(m == 0), stop=(m == 1))
                last.then_inc(ms_av, 1)
                pe.wait_ge(ms_ok, G + 1)
                for a in range(2):
                    last = pe.matmul(ps[:, 7, a * 32:(a + 1) * 32], ms_out[:, a * P:(a + 1) * P],
                                     pick[:, :, :].rearrange("p b q -> p (b q)"), start=True, stop=True, skip_group_check=True)
                last.then_inc(ms_mt, 1)

        def out_units(eng, l, body):
            with eng.Fori(0, OUT_U // 2) as i:
                for h in range(2):
                    body(i * 2 + h, i * 2 + (out0[l] + h), (out0[l] + h) % 2, i * 2 + (OUT_U * l + h))

        def pe_out_unit(pe, u, n, par, un):
            pe.wait_ge(w_ok, n + 1)
            for t in range(NT):
                pe.wait_ge(out_ev, un * 9 + (t + 1))
                for k in range(KT):
                    last = mm3(pe, ps[0:ROWS[t], t % CB, 0:UW], act_hi[:, k, tok_cols(t)], act_lo[:, k, tok_cols(t)],
                               w_hi[:, par, k, :], w_lo[:, par, k, :], k == 0, k == KT - 1)
                last.then_inc(w_used if t == NT - 1 else out_mm, 1)

        def dve_out_unit(dve, u, n, par, un):
            split_lo(dve, n + 1, 1 - par)
            for t in range(NT):
                if t == NT - 1:
                    dve.wait_ge(w_used, n + 1)
                else:
                    dve.wait_ge(out_mm, un * 8 + (t + 1))
                xs = x[0:ROWS[t], t, bass.ds(u * UW, UW)]
                dve.tensor_tensor(xs, xs, ps[0:ROWS[t], t % CB, 0:UW], ALU.add).then_inc(out_ev, 1)

        ROWCH = [(c * P, min(P, 16 * 2 * NFT - c * P)) for c in range(6)]

        def pool_past(pool, l):
            pool.wait_ge(ms_lo, 2 * (l + 1))
            v = A["state"][l].rearrange("b j (t f) -> (b j t) f", f=P)
            for c, (r0, nr) in enumerate(ROWCH):
                if c >= 2:
                    pool.wait_ge(st_mm, 6 * l + c - 1)
                pool.dma_start(rows_st[0:nr, c % 2, :], v[r0:r0 + nr, :]).then_inc(st_ld[c % 2], 16)

        def pe_past(pe, l):
            for c, (r0, nr) in enumerate(ROWCH):
                pe.wait_ge(st_ld[c % 2], 16 * (3 * l + c // 2 + 1))
                if c >= 2:
                    pe.wait_ge(st_ev, 6 * l + c - 1)
                pe.transpose(ps[:, 4 + c % 2, 0:nr], rows_st[0:nr, c % 2, :], ident[0:nr, 0:nr]).then_inc(st_mm, 1)

        def dve_past(dve, l):
            for c, (r0, nr) in enumerate(ROWCH):
                dve.wait_ge(st_mm, 6 * l + c + 1)
                dve.tensor_copy(past_t[:, :, :, :].rearrange("p b j t -> p (b j t)")[:, r0:r0 + nr], ps[:, 4 + c % 2, 0:nr]).then_inc(st_ev, 1)
            for t in (act_hi, act_lo):
                dve.memset(t[:, :, 0:2].bitcast(F32), 0.0).then_inc(pad_ok, 1)
                for k in range(KT):
                    dve.memset(t[:, k, SAMP0:SAMP0 + NB * EXT].rearrange("p (b t) -> p b t", t=EXT)[:, :, 0:2].bitcast(F32),
                               0.0).then_inc(pad_ok, 1)
                dve.memset(t[:, :, SAMP0 + NB * EXT:FW].bitcast(F32), 0.0).then_inc(pad_ok, 1)

        def ffn_units(eng, l, first, body):
            first()
            with eng.Fori(0, (NFT - 2) // 2) as i:
                for h in range(2):
                    body(i * 2 + (1 + h), (1 + h) % 2)
            body(NFT - 1, (NFT - 1) % 2)

        def wpar(l, par):
            return (ffn0[l] + par) % 2

        def pe_up(pe, l, u, par):
            n = u + ffn0[l]
            U = u + NFT * l
            pe.wait_ge(w_ok, n + 1)
            w = wpar(l, par)
            for h in range(2):
                if h == 0 and not (isinstance(u, int) and u < 2):
                    pe.wait_ge(dn_ev, U * 18 + (DC + 16 - 36))
                if not (isinstance(u, int) and u == 0):
                    pe.wait_ge(up_ev, U * 2 + (h - 1))
                for g in range(3):
                    for k in range(KT):
                        last = mm3(pe, ps[:, 3 * h + g, 0:TG], w_hi[:, w, k, h * P:(h + 1) * P],
                                   w_lo[:, w, k, h * P:(h + 1) * P], act_hi[:, k, g * TG:(g + 1) * TG],
                                   act_lo[:, k, g * TG:(g + 1) * TG], k == 0, k == KT - 1)
                last.then_inc(w_used if h else up_mm, 1)

        DN_BANK = [6, 7, 0, 1]

        def pe_down(pe, l, v, par, final=False):
            V = v + NFT * l
            pe.wait_ge(g_ok, V * 2 + 2)
            pe.wait_ge(d_ok, V + 1)
            if not final:
                pe.wait_ge(up_ev, V * 2 + 3)
            for t in range(NT):
                for c in range(2):
                    q = 2 * t + c
                    pe.wait_ge(dn_ev, V * 18 + max(q + 1, min(q + DC - 1, DC)))
                    last = mm3(pe, ps[0:ROWS[t], DN_BANK[(2 * t + c) % 4], :], g_hi[:, par, tok_cols(t)], g_lo[:, par, tok_cols(t)],
                               d_hi[:, c * 512:(c + 1) * 512], d_lo[:, c * 512:(c + 1) * 512], True, True)
                    last.then_inc(dn_mm, 1)

        def pe_ffn(pe, l):
            pe.wait_ge(pad_ok, 2 * (KT + 2) * (l + 1))
            def body(u, par):
                pe_up(pe, l, u, par)
                pe_down(pe, l, u - 1, 1 - par)
            ffn_units(pe, l, lambda: pe_up(pe, l, 0, 0), body)
            pe_down(pe, l, NFT - 1, (NFT - 1) % 2, True)

        def split_d_hi(act, l, v):
            V = v + NFT * l
            act.wait_ge(dr_ld, V * 16 + 16)
            if not (isinstance(v, int) and v == 0):
                act.wait_ge(dn_ev, V * 18 + DC)
            act.activation(d_hi[:, :], d_raw[:, :], ACT.Copy).then_inc(dh_ok, 1)

        def split_d_lo(dve, l, v):
            V = v + NFT * l
            dve.wait_ge(dh_ok, V + 1)
            dve.tensor_tensor(d_lo[:, :], d_raw[:, :], d_hi[:, :].bitcast(F32), ALU.subtract).then_inc(d_ok, 1)

        def coef(l, j, u, h):
            return cwb[:, l, j, bass.ds(u + NFT * h, 1)]

        def act_unit(act, l, u, par, first):
            U = u + NFT * l
            n = u + ffn0[l]
            if not first:
                split_d_hi(act, l, u - 1)
            if not (isinstance(n, int) and n + 1 >= N_UNITS):
                split_hi(act, n + 1, 1 - wpar(l, par))
            for h, (up, cv) in enumerate(((up_u, cv_u), (up_g, cv_g))):
                if h:
                    act.wait_ge(w_used, n + 1)
                else:
                    act.wait_ge(up_mm, U + 1)
                if not first:
                    act.wait_ge(tap_ok, U * 2 + (h - 1))
                    act.wait_ge(gate_ok if h else g_ok, U if h else U * 2)
                src = ps[:, 3 * h:3 * h + 3, 0:TG]
                act.activation(up[:, :].rearrange("p (g c) -> p g c", c=TG), src, ACT.Copy)
                act.activation(cv[:, :].rearrange("p (g c) -> p g c", c=TG), src, ACT.Identity, scale=coef(l, 2, u, h),
                               bias=coef(l, 3, u, h)).then_inc(up_ev, 1)
            act.wait_ge(cv_ok, U * 4 + 2)
            act.activation(cv_u[:, 2:FW], cv_u[:, 2:FW], ACT.Silu).then_inc(silu_ok, 1)
            act.wait_ge(gate_ok, U + 1)
            if not first:
                act.wait_ge(dn_ev, U * 18 + (DC - 18))
            act.activation(g_hi[:, par, 0:SEQ], cv_u[:, 2:2 + SEQ], ACT.Copy).then_inc(gh_ok, 1)
            act.activation(g_hi[:, par, SEQ:NTOK].rearrange("p (b t) -> p b t", t=NQ), samp_cv(cv_u), ACT.Copy).then_inc(gh_ok, 1)

        def samp_cv(t):
            return t[:, SAMP0:SAMP0 + NB * EXT].rearrange("p (b t) -> p b t", t=EXT)[:, :, 2:EXT]

        def dve_taps(dve, l, u, h, first):
            U = u + NFT * l
            up, cv = ((up_u, cv_u), (up_g, cv_g))[h]
            ft = bass.ds(u + NFT * h, 1)
            ext = up[:, SAMP0:SAMP0 + NB * EXT].rearrange("p (b t) -> p b t", t=EXT)
            dve.wait_ge(up_ev, U * 2 + (h + 1))
            dve.tensor_copy(ext[:, :, 0:2], past_t[:, :, :, ft].rearrange("p b j a -> p b (j a)")).then_inc(ins_ok, 1)
            dve.tensor_copy(tail_p[:, :, ft].rearrange("p j a -> p (j a)"), up[:, SEQ:SEQ + 2]).then_inc(tail_ok, 1)
            dve.tensor_copy(tail_s[:, :, :, ft].rearrange("p b j a -> p b (j a)"), ext[:, :, EXT - 2:EXT]).then_inc(tail_ok, 1)
            dve.wait_ge(ins_ok, U * 2 + (h + 1))
            dve.scalar_tensor_tensor(out=cv[:, 2:FW], in0=up[:, 1:FW - 1], scalar=coef(l, 1, u, h), in1=cv[:, 2:FW],
                                     op0=ALU.mult, op1=ALU.add).then_inc(cv_ok, 1)
            dve.wait_ge(cv_ok, U * 4 + (2 * h + 1))
            dve.scalar_tensor_tensor(out=cv[:, 2:FW], in0=up[:, 0:FW - 2], scalar=coef(l, 0, u, h), in1=cv[:, 2:FW],
                                     op0=ALU.mult, op1=ALU.add).then_inc(cv_ok, 1)
            dve.wait_ge(cv_ok, U * 4 + (2 * h + 2))
            dve.sem_inc(tap_ok, 1)

        ins_ok, tail_ok = sem("ins_ok"), sem("tail_ok")

        def dve_adds(dve, l, v):
            V = v + NFT * l
            for t in range(NT):
                for c in range(2):
                    dve.wait_ge(dn_mm, V * 18 + (2 * t + c + 1))
                    xs = x[0:ROWS[t], t, c * 512:(c + 1) * 512]
                    dve.tensor_tensor(xs, xs, ps[0:ROWS[t], DN_BANK[(2 * t + c) % 4], :], ALU.add).then_inc(dn_ev, 1)

        def dve_unit(dve, l, u, par, first):
            U = u + NFT * l
            n = u + ffn0[l]
            if not first:
                split_d_lo(dve, l, u - 1)
            if not (isinstance(n, int) and n + 1 >= N_UNITS):
                split_lo(dve, n + 1, 1 - wpar(l, par))
            dve_taps(dve, l, u, 0, first)
            if not first:
                dve_adds(dve, l, u - 1)
            dve_taps(dve, l, u, 1, first)
            dve.wait_ge(silu_ok, U + 1)
            dve.tensor_tensor(cv_u[:, 2:FW], cv_u[:, 2:FW], cv_g[:, 2:FW], ALU.mult).then_inc(gate_ok, 1)
            dve.wait_ge(gh_ok, U * 2 + 2)
            dve.tensor_tensor(g_lo[:, par, 0:SEQ], cv_u[:, 2:2 + SEQ], g_hi[:, par, 0:SEQ].bitcast(F32),
                              ALU.subtract).then_inc(g_ok, 1)
            dve.tensor_tensor(g_lo[:, par, SEQ:NTOK].rearrange("p (b t) -> p b t", t=NQ), samp_cv(cv_u),
                              g_hi[:, par, SEQ:NTOK].rearrange("p (b t) -> p b t", t=NQ).bitcast(F32),
                              ALU.subtract).then_inc(g_ok, 1)

        def act_ffn(act, l):
            ffn_units(act, l, lambda: act_unit(act, l, 0, 0, True), lambda u, par: act_unit(act, l, u, par, False))
            split_d_hi(act, l, NFT - 1)

        def dve_ffn(dve, l):
            ffn_units(dve, l, lambda: dve_unit(dve, l, 0, 0, True), lambda u, par: dve_unit(dve, l, u, par, False))
            split_d_lo(dve, l, NFT - 1)
            dve_adds(dve, l, NFT - 1)

        def pool_ffn(pool, l):
            pool.wait_ge(ms_lo, 2 * (l + 1))
            def load(v):
                if not (isinstance(v, int) and v == 0):
                    pool.wait_ge(d_ok, v + NFT * l)
                pool.dma_start(d_raw[:, :], A["w_down"][l][bass.ds(v * P, P), :]).then_inc(dr_ld, 16)
            load(0)
            with pool.Fori(0, NFT - 1) as i:
                load(i + 1)

        TAILS = [("p", 0, 2 * 2 * NFT)] + [("s", r0, nr) for r0, nr in ROWCH]

        def tail_src(kind, r0, nr):
            t = tail_p[:, :, :].rearrange("p j t -> p (j t)") if kind == "p" else tail_s[:, :, :, :].rearrange("p b j t -> p (b j t)")
            return t[:, r0:r0 + nr]

        def pe_tails(pe, l):
            pe.wait_ge(tail_ok, 4 * NFT * (l + 1))
            for c, (kind, r0, nr) in enumerate(TAILS):
                if c >= 2:
                    pe.wait_ge(tl_ev, 7 * l + c - 1)
                pe.transpose(ps[0:nr, 2 + c % 2, 0:P], tail_src(kind, r0, nr), ident[:, :]).then_inc(tl_mm, 1)

        def dve_tails(dve, l):
            for c, (kind, r0, nr) in enumerate(TAILS):
                dve.wait_ge(tl_mm, 7 * l + c + 1)
                if c >= 2:
                    dve.wait_ge(tl_out[c % 2], 16 * ((4, 3)[c % 2] * l + c // 2))
                dve.tensor_copy(rows_st[0:nr, c % 2, :], ps[0:nr, 2 + c % 2, 0:P]).then_inc(tl_ev, 1)

        def pool_tails(pool, l):
            for c, (kind, r0, nr) in enumerate(TAILS):
                pool.wait_ge(tl_ev, 7 * l + c + 1)
                dst = (O["conv_p"][l, 0].rearrange("j (t f) -> (j t) f", f=P) if kind == "p"
                       else O["conv_s"][l].rearrange("b j (t f) -> (b j t) f", f=P))
                pool.dma_start(dst[r0:r0 + nr, :], rows_st[0:nr, c % 2, :]).then_inc(tl_out[c % 2], 16)

        def x_ready(act, t, l, ffn):
            if ffn:
                act.wait_ge(out_ev, CB + 9 * OUT_U * (l + 1) - (NT - 1 - t))
            elif l:
                act.wait_ge(dn_ev, DC + 18 * NFT - 2 * (NT - 1 - t))
            else:
                act.wait_ge(x_ld, 32)

        block = es.enter_context(nc.Block())

        @block.sync
        def _(sp):
            sp.dma_start(x[:, 0:NPT, :], A["x_prompt"][0].rearrange("(t p) d -> p t d", p=P)).then_inc(x_ld, 16)
            sp.dma_start(x[0:NS, NPT, :], A["x_sample"].rearrange("b t d -> (b t) d")).then_inc(x_ld, 16)
            for l in (0, 1):
                for u in range(KV_U):
                    load_cols(sp, kv0[l] + u, A["w_mem_kv"][l], u * UW)
                order = [(0, 0)]
                if l:
                    in_units(sp, l, lambda u, n, par, un: load_cols(sp, n, win[l], u * UW))
                else:
                    for n, u in enumerate(ORDER0):
                        load_cols(sp, in0[0] + n, win[0], u * UW)
                load_cols(sp, out0[l], A["w_out"][l], 0)
                sp_ms(sp, l)
                if l:
                    sp_bs(sp)
                    sp.wait_ge(bs_vl[0], NB * NGR + 1)
                    sp.wait_ge(bs_vl[1], NB * NGR + 1)
                for u in range(1, OUT_U):
                    load_cols(sp, out0[l] + u, A["w_out"][l], u * UW)

                def load_up(u, par):
                    def half(h):
                        return A["w_up"][l][:, bass.ds(u * P + DFF * h, P)].rearrange("(k p) f -> p k f", p=P)
                    load_unit(sp, u + ffn0[l], half(0), half(1), w_raw[:, :, 0:P], w_raw[:, :, P:UW])

                ffn_units(sp, l, lambda: load_up(0, 0), load_up)
            sp.wait_ge(dn_ev, DC + 18 * NFT * 2)
            sp.dma_start(O["y_p"][0].rearrange("(t p) d -> p t d", p=P), x[:, 0:NPT, :]).then_inc(y_out, 16)
            sp.dma_start(O["y_s"].rearrange("b t d -> (b t) d"), x[0:NS, NPT, :]).then_inc(y_out, 16)
            sp.wait_ge(y_out, 32)
            sp.wait_ge(tl_out[0], 16 * 8)
            sp.wait_ge(tl_out[1], 16 * 6)
            sp.wait_ge(kv_out, 64)
            sp.wait_ge(gm_out, 16)
            sp.wait_ge(copied, 64)
            sp.wait_ge(in_st, IN_ST[1])

        @block.gpsimd
        def _(pool):
            for s, v in ((bs_vl[0], 1), (bs_vl[1], 1), (in_ev, CB), (stage_free, 2), (out_ev, CB), (dn_ev, DC), (bp_sig, 2),
                         (bp_lo, 2), (bp_av, 2),
                         (bs_av, 2), (mq_lo, 2)):
                pool.sem_inc(s, v)
            pool.memset(eps_ap[:, :], EPS).then_inc(filled, 1)
            pool_masks.filled = 1
            pool_setup(pool)
            for l in (0, 1):
                pool_mem(pool, l)
                pool_kv(pool, l)
                pool_in(pool, l)
                if l == 0:
                    pool_gm_load(pool)
                pool_mq(pool, l)
                if l:
                    pool_bp(pool)
                    pool_bs(pool)
                    pool.wait_ge(bs_lo, NB)
                pool_past(pool, l)
                pool_ffn(pool, l)
                pool_tails(pool, l)

        @block.scalar
        def _(act):
            c = Counts()
            act.wait_ge(filled, 1)
            act.wait_ge(set_ev, SET_EV)
            split_hi(act, 0, 0)
            for l in (0, 1):
                act_mem(act, c, l)
                act_norm_x(act, c, 8 * l, False, lambda e, t: x_ready(e, t, l, False))
                act_kv(act, c, l)
                act_in(act, c, l)
                if l == 0:
                    act_gm(act, c)
                act_mq(act, l)
                act_ms(act, l)
                if l:
                    act_bp(act)
                    act_bs(act)
                out_units(act, l, lambda u, n, par, un: split_hi(act, n + 1, 1 - par))
                act_norm_x(act, c, 16 + 8 * l, True, lambda e, t: x_ready(e, t, l, True))
                act_ffn(act, l)

        @block.vector
        def _(dve):
            c = Counts()
            dve_setup(dve)
            split_lo(dve, 0, 0)
            for l in (0, 1):
                dve_mem(dve, c, l)
                dve_norm_x(dve, c, 8 * l, False)
                dve_kv(dve, c, l)
                in_units(dve, l, lambda u, n, par, un: split_lo(dve, n + 1, 1 - par))
                dve_kv_turn(dve, l)
                if l == 0:
                    dve_gm(dve, c)
                dve_mq(dve, l)
                dve_ms(dve, l)
                if l:
                    dve_bp(dve)
                    dve_bs(dve)
                out_units(dve, l, lambda u, n, par, un: dve_out_unit(dve, u, n, par, un))
                dve_past(dve, l)
                dve_norm_x(dve, c, 16 + 8 * l, True)
                dve_ffn(dve, l)
                dve_tails(dve, l)

        @block.tensor
        def _(pe):
            c = Counts()
            pe_setup(pe)
            for l in (0, 1):
                pe_mem(pe, c, l)
                pe_norm_x(pe, c)
                pe_kv(pe, c, l)
                in_units(pe, l, lambda u, n, par, un: pe_in_unit(pe, l, u, n, par, un * 9))
                pe_kv_turn(pe, c, l)
                if l == 0:
                    pe_gm(pe, c)
                pe_mq(pe, l)
                pe_ms(pe, l)
                if l:
                    pe_bp(pe)
                    pe_bs(pe)
                pe.wait_ge(turn_lo, c.turn)
                pe.wait_ge(mq_lo, 2 + 8 * (l + 1))
                pe.wait_ge(ms_lo, 2 * (l + 1))
                out_units(pe, l, lambda u, n, par, un: pe_out_unit(pe, u, n, par, un))
                pe_past(pe, l)
                pe_norm_x(pe, c)
                pe.wait_ge(turn_lo, c.turn)
                pe_ffn(pe, l)
                pe_tails(pe, l)


_INS = ["x_prompt", "x_sample", "cache_mem_k", "cache_mem_v", "cache_sb_k", "cache_sb_v", "state_ffn_conv",
        "page_table", "mem_prompt", "norm_mix", "norm_ffn", "norm_mem", "w_in_a", "gm_v_norm", "gm_ws", "gm_bs",
        "w_in_b", "sb_bias", "w_mem_kv", "mem_q_norm", "mem_k_norm", "w_out", "w_up", "conv_w", "conv_b", "w_down"]
_OUTS = [("y_p", (1, SEQ, D)), ("y_s", (NB, NQ, D)), ("mem_k", (2, 1, M, MH, HD)), ("mem_v", (2, 1, M, MH, HD)),
         ("sb_k_p", (1, 1, SEQ, SH, HD)), ("sb_v_p", (1, 1, SEQ, SH, HD)), ("sb_k_s", (1, NB, NQ, SH, HD)),
         ("sb_v_s", (1, NB, NQ, SH, HD)), ("gm_v", (1, NB, NQ, MIX)), ("conv_p", (2, 1, 2, 2 * DFF)),
         ("conv_s", (2, NB, 2, 2 * DFF))]


def kernel(**inputs):
    import numpy as _np
    import concourse.bacc as _bacc
    from concourse import mybir as _mybir
    from concourse.bass_utils import run_bass_kernel_spmd as _run

    nc = _bacc.Bacc("TRN2", target_bir_lowering=False, num_devices=1)
    arrays, A, O = {}, {}, {}
    for name in _INS:
        a = _np.ascontiguousarray(inputs[name])
        arrays[f"in_{name}_dram"] = a
        A[name] = nc.dram_tensor(f"in_{name}_dram", a.shape, _mybir.dt.from_np(a.dtype), kind="ExternalInput").ap()
    A["state"] = A["state_ffn_conv"]
    for name, shape in _OUTS:
        O[name] = nc.dram_tensor(f"out_{name}_dram", shape, _mybir.dt.float32, kind="ExternalOutput").ap()
    scratch = nc.dram_tensor("projected", (NTOK, 3 * MIX + MEMW), _mybir.dt.float32, kind="Internal").ap()
    build(nc, A, O, scratch)
    r = _run(nc, [arrays], core_ids=[0])
    return tuple(r.results[0][f"out_{name}_dram"] for name, _ in _OUTS)
```

```python
from contextlib import ExitStack

import concourse.bass as bass
from concourse import mybir

F32 = mybir.dt.float32
F32R = mybir.dt.float32r
I32 = mybir.dt.int32
ALU = mybir.AluOpType
ACT = mybir.ActivationFunctionType
AX_X = mybir.AxisListType.X

P = 128
D = 1024
KT = D // P
SEQ = 1024
NPT = SEQ // P
NB, NQ = 8, 8
NS = NB * NQ
NT = NPT + 1
MIX = 768
MEMW = 256
MH, HD = 4, 64
M = 256
SH = 12
NPAIR = SH // 2
DFF = 2816
NFT = DFF // P
PAGES = 16
EPS = 1e-6
UW = 256
NTOK = SEQ + NS
EXT = NQ + 2
SAMP0 = 2 + SEQ
FW = 1110
TG = FW // 3
CB = 3
DC = 4

ROWS = [P] * NPT + [NS]


class Counts:

    def __init__(self):
        self.turn = 0
        self.xn = 0
        self.norm = 0
        self.ssq = 0
        self.kv = 0


def build(nc, A, O, scratch):
    es = ExitStack()
    with es:
        place = [16512]
        top = nc.sbuf_usable_end // 32 * 32 - 576

        def sb_at(name, shape, off, dt=F32):
            return nc.alloc_sbuf_tensor_at(name, shape, dt, offset=off)

        def size(shape):
            n = 4
            for s in shape[1:]:
                n *= s
            return (n + 31) // 32 * 32

        def sb(name, shape, dt=F32):
            t = sb_at(name, shape, place[0], dt)
            place[0] += size(shape)
            return t

        class Region:

            def __init__(self, at):
                self.at = at

            def __call__(self, name, shape, dt=F32):
                t = sb_at(name, shape, self.at, dt)
                self.at += size(shape)
                assert self.at <= top, (name, self.at, top)
                return t

        x = sb("x", [P, NT, D])
        act_hi = sb("act_hi", [P, KT, FW], F32R)
        act_lo = sb("act_lo", [P, KT, FW], F32R)
        w_hi_at = place[0]
        w_hi = sb("w_hi", [P, 2, KT, UW], F32R)
        w_lo = sb("w_lo", [P, 2, KT, UW], F32R)
        w_raw = sb("w_raw", [P, KT, UW])
        ident = sb("ident", [P, P])
        gains = sb("gains", [P, 48])
        cwb = sb("cwb", [P, 2, 4, 2 * NFT])
        qk_gain = sb("qk_gain", [P, 4, HD])
        ssq = sb("ssq", [P, NT])
        root = sb("root", [P, NT])
        inv = sb("inv", [P, NT])
        head_of = sb("head_of", [P, MH])
        query_of = sb("query_of", [P, NQ])
        batch_of = sb("batch_of", [P, 4])
        rep8 = sb("rep8", [NQ, NB, NQ])
        phase0 = place[0]

        r = Region(phase0)
        gains_raw = r("gains_raw", [48, P])
        conv_raw = r("conv_raw", [2 * NFT, 2, 4, P])
        slot16 = r("slot16", [P, 16])

        r = Region(phase0)
        mk_bd = r("mk_bd", [P, 2, 2 * M])
        mv_pad = r("mv_pad", [P, 2, MH, P])
        keep = r.at
        diag = r("diag", [P, NT, P])
        mem_hi = r("mem_hi", [P, KT, M], F32R)
        mem_lo = r("mem_lo", [P, KT, M], F32R)
        mem_raw = r("mem_raw", [P, 2, D])
        r = Region(keep)
        v_all = r("v_all", [P, NT, MIX])
        mkv = r("mkv", [P, 2, 2 * MEMW])
        stage = sb_at("stage", [P, 2, NT, UW], r.at)
        kv_sq = r("kv_sq", [P, 2, MEMW])
        kv_stat = r("kv_stat", [P, 3, 8])

        r = Region(keep + size([P, NT, MIX]))
        gm_cat = r("gm_cat", [P, 4, MIX])
        r = Region(phase0)
        tri01 = r("tri01", [P, P])
        bias12 = r("bias12", [P, SH])
        new01 = r("new01", [96, NQ])
        head12 = r("head12", [96, SH])
        head_b = r("head_b", [96, SH])
        bias96 = r("bias96", [96, 1])
        zero1 = r("zero1", [P, 1])
        mid = r.at
        sbq_raw = r("sbq_raw", [P, NPT, P])
        sbk_raw = r("sbk_raw", [P, NPT, P])
        sb_v = r("sb_v", [P, NPT, P])
        sb_q = r("sb_q", [65, 2, SEQ])
        sb_k = r("sb_k", [65, 2, SEQ])
        brk = r("brk", [P, 3, SEQ])
        left = r("left", [P, SEQ + 1])
        brk_t = r("brk_t", [P, 2, 512])
        r = Region(mid)
        pk_raw = r("pk_raw", [P, 4, MIX])
        pk_hi = r("pk_hi", [P, NPAIR, 2 * P + NQ], F32R)
        pk_lo = r("pk_lo", [P, NPAIR, 2 * P + NQ], F32R)
        pv_hi1 = r("pv_hi1", [P, 2, MIX], F32R)
        pv_lo1 = r("pv_lo1", [P, 2, MIX], F32R)
        s_brk = r("s_brk", [96, 2, 2 * P + NQ])
        s_left = r("s_left", [96, 2, 2 * P + NQ + 1])
        at_hi = r("at_hi", [P, 2, 2, 96], F32R)
        at_lo = r("at_lo", [P, 2, 2, 96], F32R)
        at_new = r("at_new", [NQ, 96])
        v_new = r("v_new", [NQ, MIX])
        kn_t = r("kn_t", [P, NPAIR, NS])
        qb_hi = r("qb_hi", [P, NPAIR * 112], F32R)
        qb_lo = r("qb_lo", [P, NPAIR * 112], F32R)
        s_out = r("s_out", [96, MIX])

        r = Region(keep)
        mq = r("mq", [P, NT, MEMW])
        mq_sq = sb_at("mq_sq", [P, NT, MEMW], r.at)
        r.at += size([P, NT, MEMW])
        mq_n = r("mq_n", [P, 2, MEMW])
        mq_t = r("mq_t", [P, 2, 2, P])
        mq_stat = r("mq_stat", [P, 3, NT * MH])
        sm_max = r("sm_max", [P, 2, MH])
        sm_sum = r("sm_sum", [P, 2, MH])
        sm_inv = r("sm_inv", [P, 2, MH])
        mid = r.at
        prob = r("prob", [P, 2, MH, M])
        prob_t = r("prob_t", [P, 2, 2, MH, P])
        mkc = sb_at("mkc", [P, 4, 2, MEMW], keep + size([P, NT, MEMW]))
        mvc = [r("mvc0", [P, 4, 2, MEMW]), sb_at("mvc1", [P, 4, 2, MEMW], keep)]
        r = Region(mid)
        mkc_t = r("mkc_t", [P, 4, 2, M])
        mq_bd = r("mq_bd", [P, 4 * 288])
        prob_s = r("prob_s", [P, M])
        prob_st = r("prob_st", [P, 2, P])
        ms_out = r("ms_out", [P, MEMW])
        pick = r("pick", [P, 4, NQ])

        r = Region(phase0)
        up_u = r("up_u", [P, FW])
        up_g = r("up_g", [P, FW])
        cv_u = r("cv_u", [P, FW])
        cv_g = r("cv_g", [P, FW])
        d_hi = r("d_hi", [P, D], F32R)
        d_lo = r("d_lo", [P, D], F32R)
        d_raw = r("d_raw", [P, D])
        g_hi = r("g_hi", [P, 2, NTOK], F32R)
        g_lo = r("g_lo", [P, 2, NTOK], F32R)
        past_t = r("past_t", [P, NB, 2, 2 * NFT])
        tail_p = r("tail_p", [P, 2, 2 * NFT])
        tail_s = r("tail_s", [P, NB, 2, 2 * NFT])
        rows_st = r("rows_st", [P, 7, P])

        ps = es.enter_context(nc.psum_tensor("ps", [P, 8, 512], F32))

        def sem(name):
            return es.enter_context(nc.semaphore(name))

        filled, masked, set_ld, set_mm, set_ev = (sem(n) for n in ("filled", "masked", "set_ld", "set_mm", "set_ev"))
        x_ld, mem_ld = [sem(f"x_ld{g}") for g in range(3)], sem("mem_ld")
        wr_ld, wh_ok, w_ok, w_used = (sem(n) for n in ("wr_ld", "wh_ok", "w_ok", "w_used"))
        ssq_ok, root_ok, inv_ok, xn_ok = (sem(n) for n in ("ssq_ok", "root_ok", "inv_ok", "xn_ok"))
        turned, turn_hi, turn_lo = (sem(n) for n in ("turned", "turn_hi", "turn_lo"))
        kv_mm, kv_ev, kv_st, kv_root, kv_tr, kv_ok, kv_out = (
            sem(n) for n in ("kv_mm", "kv_ev", "kv_st", "kv_root", "kv_tr", "kv_ok", "kv_out"))
        in_mm, in_ev, in_st, stage_free = (sem(n) for n in ("in_mm", "in_ev", "in_st", "stage_free"))
        out_mm, out_ev = sem("out_mm"), sem("out_ev")
        gm_gelu, gm_v, gm_set, gm_setmm, gm_mix, gm_cat_ok, gm_out = (
            sem(n) for n in ("gm_gelu", "gm_v", "gm_set", "gm_setmm",
                             "gm_mix", "gm_cat_ok", "gm_out"))
        mq_ld, mq_step, mq_root, mq_tr, mq_tc, mq_s, mq_mx, mq_ex, mq_pr, mq_pt, mq_pc, mq_av, mq_hi, mq_lo = (
            sem(n) for n in ("mq_ld", "mq_step", "mq_root", "mq_tr", "mq_tc", "mq_s", "mq_mx", "mq_ex", "mq_pr",
                             "mq_pt", "mq_pc", "mq_av", "mq_hi", "mq_lo"))
        ms_tr, ms_tc, ms_q, ms_s, ms_step, ms_ex, ms_pt, ms_pc, ms_av, ms_ok, ms_mt, ms_hi, ms_lo = (
            sem(n) for n in ("ms_tr", "ms_tc", "ms_q", "ms_s", "ms_step", "ms_ex", "ms_pt", "ms_pc",
                             "ms_av", "ms_ok", "ms_mt", "ms_hi", "ms_lo"))
        bp_ld, bp_v, bp_tr, bp_q, bp_k, bp_b, bp_z, bp_sig, bp_msk, bp_keep, bp_left, bp_a, bp_t, bp_at, bp_av, bp_hi, \
            bp_lo, bp_set, bp_one = (sem("bp_" + n) for n in ("ld", "v", "tr", "q", "k", "b", "z", "sig", "msk", "keep",
                                                              "left", "a", "t", "at", "av", "hi", "lo", "set", "one"))
        bs_in, bs_set, bs_tr, bs_q, bs_qb, bs_kn, bs_kh, bs_kl, bs_vh, bs_z, bs_sig, bs_a, bs_at, bs_ah, \
            bs_al, bs_vn, bs_av, bs_o, bs_mt, bs_hi, bs_lo = (sem("bs_" + n) for n in (
                "in", "set", "tr", "q", "qb", "kn", "kh", "kl", "vh", "z", "sig", "a", "at", "ah",
                "al", "vn", "av", "o", "mt", "hi", "lo"))
        up_mm, up_ev, cv_ok, silu_ok, gate_ok, gh_ok, g_ok, dr_ld, dh_ok, d_ok, dn_mm, dn_ev = (
            sem(n) for n in ("up_mm", "up_ev", "cv_ok", "silu_ok", "gate_ok", "gh_ok", "g_ok", "dr_ld",
                             "dh_ok", "d_ok", "dn_mm", "dn_ev"))
        gm_u = [sem(f"gm_u{n}") for n in range(4)]
        ms_ld = [sem("ms_ld0"), sem("ms_ld1")]
        bs_k, bs_v, bs_vl = ([sem(f"bs_{n}{h}") for h in (0, 1)] for n in ("k", "v", "vl"))
        st_ld, tl_out = sem("st_ld"), sem("tl_out")
        bs_n, bs_edge = sem("bs_n"), sem("bs_edge")
        tap_ok, mq_nm = sem("tap_ok"), sem("mq_nm")
        st_mm, st_ev, tl_mm, tl_ev = (sem(n) for n in ("st_mm", "st_ev", "tl_mm", "tl_ev"))
        pad_ok, copied, y_out, mem_pad = sem("pad_ok"), sem("copied"), sem("y_out"), sem("mem_pad")

        proj = scratch

        KV_U, OUT_U, FFN_U = 2, 4, NFT
        IN_U = [7, 10]
        LU = [KV_U + IN_U[0] + OUT_U + FFN_U, KV_U + IN_U[1] + OUT_U + FFN_U]
        kv0 = [0, LU[0]]
        in0 = [kv0[l] + KV_U for l in (0, 1)]
        out0 = [in0[l] + IN_U[l] for l in (0, 1)]
        ffn0 = [out0[l] + OUT_U for l in (0, 1)]
        N_UNITS = sum(LU)
        win = [A["w_in_a"][0], A["w_in_b"][0]]

        def tok_cols(t):
            return slice(t * P, t * P + ROWS[t])

        def samp_ffn(tile, k):
            return tile[:, k, SAMP0:SAMP0 + NB * EXT].rearrange("p (b t) -> p b t", t=EXT)[:, :, 2:EXT]

        def load_unit(sp, n, src_a, src_b, dst_a, dst_b):
            if not (isinstance(n, int) and n == 0):
                sp.wait_ge(w_ok, n)
            sp.dma_start(dst_a, src_a).then_inc(wr_ld, 16)
            sp.dma_start(dst_b, src_b).then_inc(wr_ld, 16)

        def load_cols(sp, n, w, c0):
            v = w[:, bass.ds(c0, UW)].rearrange("(k p) f -> p k f", p=P)
            load_unit(sp, n, v[:, 0:4, :], v[:, 4:8, :], w_raw[:, 0:4, :], w_raw[:, 4:8, :])

        def split_hi(act, n, par):
            act.wait_ge(wr_ld, 32 * n + 32)
            if not (isinstance(n, int) and n < 2):
                act.wait_ge(w_used, n - 1)
            act.activation(w_hi[:, par], w_raw[:, :, :], ACT.Copy).then_inc(wh_ok, 1)

        def split_lo(dve, n, par):
            dve.wait_ge(wh_ok, n + 1)
            dve.tensor_tensor(w_lo[:, par], w_raw[:, :, :], w_hi[:, par].bitcast(F32), ALU.subtract).then_inc(w_ok, 1)

        def mm3(pe, out, ahi, alo, bhi, blo, first, last, **kw):
            pe.matmul(out, ahi, bhi, start=first, stop=False, **kw)
            pe.matmul(out, ahi, blo, start=False, stop=False, **kw)
            return pe.matmul(out, alo, bhi, start=False, stop=last, **kw)

        def pool_masks(pool, fills, selects):
            f0 = pool_masks.filled
            m0 = pool_masks.masked
            for t, v in fills:
                pool.memset(t, v).then_inc(filled, 1)
            pool_masks.filled += len(fills)
            pool.wait_ge(filled, f0 + len(fills))
            for n, (t, cmp, fill, base, pattern, mult) in enumerate(selects):
                if n:
                    pool.wait_ge(masked, m0 + n)
                pool.affine_select(out=t, in_=t, compare_op=cmp, fill=fill, base=base, pattern=pattern,
                                   channel_multiplier=mult).then_inc(masked, 1)
            pool_masks.masked += len(selects)

        pool_masks.filled = 0
        pool_masks.masked = 0

        SET_MASKS = 5

        def pool_setup(pool):
            pool_masks(pool, [(ident[:, :], 0.0), (slot16[:, :], 1.0), (batch_of[:, :], 1.0)], [
                (ident[:, :], ALU.not_equal, 1.0, 0, [[-1, P]], 1),
                (slot16[:, :], ALU.is_ge, 0.0, 0, [[-8, 16]], 1),
                (slot16[:, :], ALU.is_ge, 0.0, 7, [[8, 16]], -1),
                (batch_of[:, :], ALU.is_ge, 0.0, 0, [[-32, 4]], 1),
                (batch_of[:, :], ALU.is_ge, 0.0, 31, [[32, 4]], -1),
            ])

        def act_setup(act):
            for n, name in enumerate(("norm_mix", "norm_ffn", "norm_mem")):
                act.dma_start(gains_raw[16 * n:16 * n + 16, :],
                               A[name].rearrange("l (k p) -> (l k) p", p=P)).then_inc(set_ld, 16)
            for l in (0, 1):
                act.dma_start(conv_raw[:, l, 0:3, :],
                               A["conv_w"][l].rearrange("j (t f) -> t j f", f=P)).then_inc(set_ld, 16)
                act.dma_start(conv_raw[:, l, 3, :],
                               A["conv_b"][l].rearrange("(t f) -> t f", f=P)).then_inc(set_ld, 16)
            for n, name in enumerate(("mem_q_norm", "mem_k_norm")):
                act.dma_start(qk_gain[:, 2 * n:2 * n + 2, :].rearrange("p l d -> p (l d)"),
                               A[name].rearrange("l d -> (l d)").partition_broadcast(P)).then_inc(set_ld, 16)

        def pe_setup(pe):
            pe.wait_ge(set_ld, 16 * 9)
            pe.wait_ge(masked, SET_MASKS)
            pe.transpose(ps[:, 0, 0:48], gains_raw[:, :], ident[0:48, 0:48]).then_inc(set_mm, 1)
            for l in (0, 1):
                for j in range(4):
                    at = (l * 4 + j) * 2 * NFT
                    last = pe.transpose(ps[:, 1, at:at + 2 * NFT], conv_raw[:, l, j, :], ident[0:2 * NFT, 0:2 * NFT])
            last.then_inc(set_mm, 1)

        def dve_setup(dve):
            dve.memset(ssq[:, :], 1.0).then_inc(set_ev, 1)
            dve.wait_ge(masked, SET_MASKS)
            dve.tensor_reduce(head_of[:, :], slot16[:, :].rearrange("p (b h) -> p h b", h=MH), AX_X, ALU.add).then_inc(set_ev, 1)
            dve.tensor_reduce(query_of[:, :], ident[:, :].rearrange("p (j q) -> p q j", q=NQ), AX_X, ALU.add).then_inc(set_ev, 1)
            dve.tensor_copy(rep8[:, :, :], ident[0:NQ, 0:NQ].unsqueeze(1).broadcast_to([NQ, NB, NQ])).then_inc(set_ev, 1)
            dve.wait_ge(set_mm, 2)
            dve.tensor_copy(gains[:, :], ps[:, 0, 0:48]).then_inc(set_ev, 1)
            dve.tensor_copy(cwb[:, :, :, :].rearrange("p l j t -> p (l j t)"), ps[:, 1, 0:8 * 2 * NFT]).then_inc(set_ev, 1)

        SET_EV = 6

        def act_norm(act, c, src, tiles, wait_src, width=D, bank=4):
            for t in tiles:
                wait_src(act, t)
                if c.ssq:
                    act.wait_ge(ssq_ok, c.ssq)
                act.activation(ps[0:ROWS[t], bank:bank + 2, :].rearrange("p a b -> p (a b)")[:, 0:width], src(t), ACT.Square,
                               accum_out=ssq[0:ROWS[t], t:t + 1]).then_inc(ssq_ok, 1)
                c.ssq += 1
            act.wait_ge(ssq_ok, c.ssq)
            a, b = tiles[0], tiles[-1] + 1
            act.activation(root[:, a:b], ssq[:, a:b], ACT.Sqrt, scale=1.0 / width, bias=eps_ap[:, 0:1]).then_inc(root_ok, 1)

        def dve_inv(dve, c, tiles):
            c.norm += 1
            a, b = tiles[0], tiles[-1] + 1
            dve.wait_ge(root_ok, c.norm)
            dve.reciprocal(inv[:, a:b], root[:, a:b]).then_inc(inv_ok, 1)
            dve.wait_ge(inv_ok, c.norm)

        def dve_diag(dve, c, t):
            n = ROWS[t]
            dve.tensor_scalar(diag[0:n, t, 0:n], ident[0:n, 0:n], inv[0:n, t:t + 1], None, ALU.mult).then_inc(xn_ok, 1)
            c.xn += 1

        def pe_turn(pe, c, src, group, ktiles, wait_src, scaled=False):
            wait_src(pe)
            for k in range(ktiles):
                bank = c.turn % 4
                if c.turn >= 4:
                    pe.wait_ge(turn_lo, c.turn - 3)
                for j, t in enumerate(group):
                    out = ps[:, bank, j * P:j * P + ROWS[t]]
                    if scaled:
                        last = pe.matmul(out, src(t, k), diag[0:ROWS[t], t, 0:ROWS[t]], start=True, stop=True, skip_group_check=True)
                    else:
                        last = pe.transpose(out, src(t, k), ident[0:ROWS[t], 0:ROWS[t]])
                last.then_inc(turned, 1)
                c.turn += 1

        def turn_dst(dst, k, group, ffn):
            if group[0] == NPT:
                if ffn:
                    return samp_ffn(dst, k)
                return dst[:, k, SEQ:NTOK].rearrange("p (b t) -> p b t", t=NQ)
            a = group[0] * P + (2 if ffn else 0)
            return dst[:, k, a:a + P * len(group)]

        def turn_src(bank, group):
            if group[0] == NPT:
                return ps[:, bank, 0:NS].rearrange("p (b t) -> p b t", t=NQ)
            return ps[:, bank, 0:P * len(group)]

        def act_turn(act, c, dst, group, ktiles, gain0, ffn):
            if c.turn == 0:
                act.wait_ge(set_ev, SET_EV)
            for k in range(ktiles):
                bank = c.turn % 4
                act.wait_ge(turned, c.turn + 1)
                scale = 1.0 if gain0 is None else gains[:, gain0 + k:gain0 + k + 1]
                act.activation(turn_dst(dst, k, group, ffn), turn_src(bank, group), ACT.Copy, scale=scale).then_inc(turn_hi, 1)
                c.turn += 1

        def dve_turn(dve, c, hi, lo, group, ktiles, gain0, ffn):
            for k in range(ktiles):
                bank = c.turn % 4
                dve.wait_ge(turn_hi, c.turn + 1)
                scale = 1.0 if gain0 is None else gains[:, gain0 + k:gain0 + k + 1]
                dve.scalar_tensor_tensor(out=turn_dst(lo, k, group, ffn), in0=turn_src(bank, group), scalar=scale,
                                         in1=turn_dst(hi, k, group, ffn).bitcast(F32), op0=ALU.mult,
                                         op1=ALU.subtract).then_inc(turn_lo, 1)
                c.turn += 1

        GROUPS = [[0, 1, 2, 3], [4, 5, 6, 7], [8]]
        eps_ap = sb_at("eps_ap", [P, 1], top)

        def xt(t):
            return x[0:ROWS[t], t, :]

        def mt(t):
            return mem_raw[:, t, :]

        def xt_k(t, k):
            return x[0:ROWS[t], t, k * P:(k + 1) * P]

        def mt_k(t, k):
            return mem_raw[:, t, k * P:(k + 1) * P]

        def dve_norm_x(dve, c, gain0, ffn):
            for group in GROUPS:
                dve_inv(dve, c, group)
                for t in group:
                    dve_diag(dve, c, t)
            for group in GROUPS:
                dve_turn(dve, c, act_hi, act_lo, group, KT, gain0, ffn)

        def pe_norm_x(pe, c):
            for group in GROUPS:
                c.xn += len(group)
                pe_turn(pe, c, xt_k, group, KT, lambda e: e.wait_ge(xn_ok, c.xn), True)

        def act_norm_x(act, c, gain0, ffn, wait_src):
            for group in GROUPS:
                act_norm(act, c, xt, group, wait_src, D, 6 if ffn else 4)
            for group in GROUPS:
                act_turn(act, c, act_hi, group, KT, gain0, ffn)

        def load_mem(eng):
            eng.dma_start(mem_raw[:, :, :], A["mem_prompt"][0].rearrange("(t p) d -> p t d", p=P)).then_inc(mem_ld, 16)

        def act_mem(act, c, l):
            act_norm(act, c, mt, [0, 1], lambda e, t: e.wait_ge(mem_ld, 16 * (l + 1)))
            act_turn(act, c, mem_hi, [0, 1], KT, 32 + 8 * l, False)

        def dve_mem(dve, c, l):
            dve_inv(dve, c, [0, 1])
            for t in range(2):
                dve_diag(dve, c, t)
            dve_turn(dve, c, mem_hi, mem_lo, [0, 1], KT, 32 + 8 * l, False)

        def pe_mem(pe, c, l):
            c.xn += 2
            pe_turn(pe, c, mt_k, [0, 1], KT, lambda e: e.wait_ge(xn_ok, c.xn), True)

        def pe_kv(pe, c, l):
            pe.wait_ge(turn_lo, c.turn)
            for u in range(2):
                n = kv0[l] + u
                pe.wait_ge(w_ok, n + 1)
                for t in range(2):
                    for k in range(KT):
                        last = mm3(pe, ps[:, 4 + 2 * u + t, 0:UW], mem_hi[:, k, t * P:(t + 1) * P],
                                   mem_lo[:, k, t * P:(t + 1) * P], w_hi[:, n % 2, k, :], w_lo[:, n % 2, k, :],
                                   k == 0, k == KT - 1)
                    last.then_inc(w_used if t else kv_mm, 1)

        def act_kv(act, c, l):
            for u in range(2):
                n = kv0[l] + u
                split_hi(act, n + 1, (n + 1) % 2)
                for t in range(2):
                    if t:
                        act.wait_ge(w_used, n + 1)
                    else:
                        act.wait_ge(kv_mm, 2 * l + u + 1)
                    act.activation(mkv[:, t, u * UW:(u + 1) * UW], ps[:, 4 + 2 * u + t, 0:UW], ACT.Copy).then_inc(kv_ev, 1)
            act.wait_ge(kv_st, 7 * l + 2)
            act.activation(kv_stat[:, 1, :], kv_stat[:, 0, :], ACT.Sqrt, scale=1.0 / HD, bias=eps_ap[:, 0:1]).then_inc(kv_root, 1)

        def dve_kv(dve, c, l):
            for u in range(2):
                split_lo(dve, kv0[l] + u + 1, (kv0[l] + u + 1) % 2)
            dve.memset(mk_bd[:, :, :], 0.0).then_inc(kv_ok, 1)
            dve.memset(mv_pad[:, :, :, :], 0.0).then_inc(kv_ok, 1)
            dve.wait_ge(kv_ev, 4 * l + 4)
            keys = mkv[:, :, 0:MEMW].rearrange("p t (h d) -> p t h d", d=HD)
            dve.tensor_tensor(kv_sq[:, :, :], mkv[:, :, 0:MEMW], mkv[:, :, 0:MEMW], ALU.mult).then_inc(kv_st, 1)
            dve.wait_ge(kv_st, 7 * l + 1)
            dve.tensor_reduce(kv_stat[:, 0, :].rearrange("p (t h) -> p t h", h=MH),
                              kv_sq[:, :, :].rearrange("p t (h d) -> p t h d", d=HD), AX_X, ALU.add).then_inc(kv_st, 1)
            dve.wait_ge(kv_root, l + 1)
            dve.reciprocal(kv_stat[:, 2, :], kv_stat[:, 1, :]).then_inc(kv_st, 1)
            dve.wait_ge(kv_st, 7 * l + 3)
            for t in range(2):
                dve.tensor_tensor(keys[:, t], keys[:, t],
                                  kv_stat[:, 2, 4 * t:4 * t + 4].unsqueeze(2).broadcast_to([P, MH, HD]),
                                  ALU.mult).then_inc(kv_st, 1)
            dve.wait_ge(kv_st, 7 * l + 5)
            for t in range(2):
                dve.tensor_tensor(keys[:, t], keys[:, t], qk_gain[:, 2 + l, :].unsqueeze(1).broadcast_to([P, MH, HD]),
                                  ALU.mult).then_inc(kv_st, 1)
            dve.wait_ge(kv_ok, 8 * l + 2)
            for hh in range(2):
                dve.tensor_copy(mv_pad[:, :, :, :].rearrange("p t (a b) c -> p t a b c", b=2)[:, :, :, hh, hh * HD:(hh + 1) * HD],
                                mkv[:, :, MEMW:].rearrange("p t (a b d) -> p t a b d", b=2, d=HD)[:, :, :, hh, :]).then_inc(kv_ok, 1)

        def dve_kv_turn(dve, l):
            for a in range(2):
                dve.wait_ge(kv_tr, 2 * l + a + 1)
                for hh in range(2):
                    dve.tensor_copy(mk_bd[hh * HD:(hh + 1) * HD, a, hh * M:(hh + 1) * M],
                                    ps[hh * HD:(hh + 1) * HD, 4 + a, 0:M]).then_inc(kv_ok, 1)

        def pe_kv_turn(pe, c, l):
            pe.wait_ge(kv_st, 7 * l + 7)
            for a in range(2):
                for t in range(2):
                    last = pe.transpose(ps[:, 4 + a, t * P:(t + 1) * P], mkv[:, t, a * P:(a + 1) * P], ident[:, :])
                last.then_inc(kv_tr, 1)

        def pool_kv(pool, l):
            pool.wait_ge(kv_st, 7 * l + 7)
            pool.wait_ge(kv_ev, 4 * l + 4)
            for half, name in enumerate(("mem_k", "mem_v")):
                pool.dma_start(O[name][l, 0].rearrange("(t p) h d -> p t (h d)", p=P),
                               mkv[:, :, half * MEMW:(half + 1) * MEMW]).then_inc(kv_out, 16)

        def pe_in_unit(pe, l, u, n, par, t0):
            pe.wait_ge(w_ok, n + 1)
            for t in range(NT):
                pe.wait_ge(in_ev, t0 + t + 1)
                for k in range(KT):
                    last = mm3(pe, ps[0:ROWS[t], t % CB, 0:UW], act_hi[:, k, tok_cols(t)], act_lo[:, k, tok_cols(t)],
                               w_hi[:, par, k, :], w_lo[:, par, k, :], k == 0, k == KT - 1)
                last.then_inc(w_used if t == NT - 1 else in_mm, 1)

        ORDER0 = [3, 4, 5, 0, 1, 2, 6]
        V_UNITS = MIX // UW
        STORED = [IN_U[0] - V_UNITS, IN_U[1] - 1]

        def stored_of(par, un):
            return (par + in0[1] + 1) % 2, un - (IN_U[0] + 1 - STORED[0])

        def act_in_unit(act, n, par, un, dst, func, stored=None, after=None):
            split_hi(act, n + 1, 1 - par)
            if stored is not None:
                act.wait_ge(stage_free, stored + 1)
            for t in range(NT):
                if t == NT - 1:
                    act.wait_ge(w_used, n + 1)
                else:
                    act.wait_ge(in_mm, 8 * un + t + 1)
                act.activation(dst(t), ps[0:ROWS[t], t % CB, 0:UW], func).then_inc(in_ev, 1)
                if after:
                    after(t)

        def staged(h):
            return lambda t: stage[0:ROWS[t], h, t, :]

        def act_in(act, c, l):
            act.wait_ge(kv_st, 7 * (l + 1))
            if l:
                act.wait_ge(tl_out, 16 * 7)
                act_in_unit(act, in0[1], in0[1] % 2, IN_U[0], lambda t: mq[0:ROWS[t], t, :], ACT.Copy)
                act_mq_root(act, l)

                def body(u, n, par, un):
                    half, stored = stored_of(par, un)
                    act_in_unit(act, n, par, un, staged(half), ACT.Copy, stored)

                in_rest(act, l, body)
                return

            def square(t):
                if c.ssq:
                    act.wait_ge(ssq_ok, c.ssq)
                act.activation(ps[0:ROWS[t], 6:8, :].rearrange("p a b -> p (a b)")[:, 0:MIX], v_all[0:ROWS[t], t, :],
                               ACT.Square, accum_out=ssq[0:ROWS[t], t:t + 1]).then_inc(ssq_ok, 1)
                c.ssq += 1

            for n, u in enumerate(ORDER0):
                func = ACT.Copy if u == 6 else ACT.Gelu_apprx_tanh
                if n < V_UNITS:
                    act_in_unit(act, in0[0] + n, (in0[0] + n) % 2, n,
                                lambda t: v_all[0:ROWS[t], t, (u - V_UNITS) * UW:(u - V_UNITS + 1) * UW], func)
                else:
                    if n == V_UNITS:
                        act.wait_ge(in_ev, CB + 9 * V_UNITS)
                    act_in_unit(act, in0[0] + n, (in0[0] + n) % 2, n, staged((n - V_UNITS) % 2), func, n - V_UNITS,
                                square if n == V_UNITS else None)
                if n == V_UNITS:
                    act.wait_ge(ssq_ok, c.ssq)
                    act.activation(root[:, :], ssq[:, :], ACT.Sqrt, scale=1.0 / MIX, bias=eps_ap[:, 0:1]).then_inc(root_ok, 1)

        def pool_in_unit(pool, col, h, un, stored):
            pool.wait_ge(in_ev, CB + 9 * un + 9)
            pool.dma_start(proj[0:SEQ, bass.ds(col * UW, UW)].rearrange("(t p) f -> p t f", p=P),
                           stage[:, h, 0:NPT, :]).then_inc(in_st, 16)
            pool.dma_start(proj[SEQ:NTOK, bass.ds(col * UW, UW)], stage[0:NS, h, NPT, :]).then_inc(in_st, 16)
            pool.wait_ge(in_st, 32 * stored + 32)
            pool.sem_inc(stage_free, 1)

        def pool_in(pool, l):
            def body(u, n, par, un):
                half, stored = stored_of(par, un)
                pool_in_unit(pool, u - 1, half, un, stored)

            if l:
                in_rest(pool, l, body)
            else:
                for n in range(V_UNITS, IN_U[0]):
                    if n == IN_U[0] - 1:
                        pool_gm_load(pool)
                    pool_in_unit(pool, ORDER0[n], (n - V_UNITS) % 2, n, n - V_UNITS)

        def in_units(eng, l, body, then=None):
            body(0, in0[l], in0[l] % 2, IN_U[0] * l)
            if then:
                then()
            in_rest(eng, l, body)

        def in_rest(eng, l, body):
            with eng.Fori(0, (IN_U[l] - 1) // 2) as i:
                for h in (1, 2):
                    body(i * 2 + h, i * 2 + (in0[l] + h), (in0[l] + h) % 2, i * 2 + (IN_U[0] * l + h))
            if IN_U[l] % 2 == 0:
                u = IN_U[l] - 1
                body(u, in0[l] + u, (in0[l] + u) % 2, IN_U[0] * l + u)

        IN_ST = [32 * STORED[0], 32 * (STORED[0] + STORED[1])]

        raw = w_raw[:, :, :].rearrange("p k f -> p (k f)")
        ws_raw = raw[:, 0:6 * P].rearrange("p (g s) -> p g s", g=6)
        gm_gain = raw[:, MIX:2 * MIX]
        bias_raw = raw[0:6, 2 * MIX:2 * MIX + P]
        same_batch = raw[0:NS, 2 * MIX + P:2 * MIX + P + NS]
        r = Region(w_hi_at + (out0[0] - 1) % 2 * size([P, KT, UW]))
        w_t = r("w_t", [P, 6, P])
        w_s = r("w_s", [NS, 6, NS])
        bias_t = r("bias_t", [P, 6])
        bias_s = r("bias_s", [NS, 6])

        def gm_u_load(pool, t):
            pool.dma_start(gm_cat[0:ROWS[t], t % 4, :], proj[t * P:t * P + ROWS[t], 0:MIX]).then_inc(gm_u[t % 4], 16)

        def pool_gm_load(pool):
            pool.wait_ge(kv_out, 32)
            pool.wait_ge(kv_tr, 2)
            for t in range(4):
                gm_u_load(pool, t)
            pool.wait_ge(w_ok, out0[0] + 1)
            pool.dma_start(ws_raw, A["gm_ws"][0].rearrange("g t s -> t g s")).then_inc(gm_set, 16)
            pool.dma_start(bias_raw, A["gm_bs"][0]).then_inc(gm_set, 16)
            pool.dma_start(gm_gain, A["gm_v_norm"][0].partition_broadcast(P)).then_inc(gm_set, 16)
            pool_masks(pool, [(same_batch, 1.0)], [
                (same_batch.rearrange("p (b t) -> p b t", t=NQ), ALU.is_ge, 0.0, 0, [[-8, NB], [0, NQ]], 1),
                (same_batch.rearrange("p (b t) -> p b t", t=NQ), ALU.is_ge, 0.0, 7, [[8, NB], [0, NQ]], -1)])
            pool.wait_ge(gm_set, 48)
            pool.affine_select(out=ws_raw, in_=ws_raw, compare_op=ALU.is_ge, fill=0.0, base=0,
                               pattern=[[0, 6], [-1, P]], channel_multiplier=1).then_inc(masked, 1)
            pool_masks.masked += 1

        def pool_gm(pool):
            pool_mq(pool)
            for t in range(4, NT):
                pool.wait_ge(turned, TURN["gm"] + 6 * (t // 4))
                gm_u_load(pool, t)
            pool.wait_ge(gm_v, NT)
            pool.dma_start(O["gm_v"][0].rearrange("b t f -> (b t) f"), v_all[0:NS, NPT, :]).then_inc(gm_out, 16)

        TURN = {"gm": KT + 3 * KT}
        GM_MASKED = SET_MASKS + 2 + 1

        def pe_gm(pe, c):
            pe.wait_ge(kv_ok, 8)
            pe.wait_ge(masked, GM_MASKED)
            for g in range(6):
                last = pe.transpose(ps[:, 4 + g // 4, (g % 4) * P:(g % 4) * P + P], ws_raw[:, g, :], ident[:, :])
            last.then_inc(gm_setmm, 1)
            pe.transpose(ps[:, 6, 0:6], bias_raw[:, :], ident[0:6, 0:6]).then_inc(gm_setmm, 1)
            pe.wait_ge(gm_gelu, 3)
            rep = rep8[:, :, :].rearrange("p b q -> p (b q)")
            pe.matmul(ps[0:NS, 7, 0:6 * NQ], rep, w_t[0:NQ, :, 0:NQ], start=True, stop=True).then_inc(gm_setmm, 1)
            pe.matmul(ps[0:NS, 6, 8:14], rep, bias_t[0:NQ, :], start=True, stop=True).then_inc(gm_setmm, 1)
            pe.wait_ge(gm_gelu, 5)
            pe.wait_ge(in_ev, CB + 9 * IN_U[0])
            for group in GROUPS:
                for t in group:
                    pe.wait_ge(gm_v, t + 1)
                    if t >= 2:
                        pe.wait_ge(gm_cat_ok, 6 * (t - 1))
                    lhs = w_t if t < NPT else w_s
                    b = 4 + 2 * (t % 2)
                    for g in range(6):
                        last = pe.matmul(ps[0:ROWS[t], b + g // 4, (g % 4) * P:(g % 4) * P + P], lhs[0:ROWS[t], g, :],
                                         v_all[0:ROWS[t], t, g * P:(g + 1) * P], start=(g % 4 == 0), stop=True,
                                         skip_group_check=True)
                    last.then_inc(gm_mix, 1)
                pe_turn(pe, c, lambda t, k: gm_cat[0:ROWS[t], t % 4, k * P:(k + 1) * P], group, 6,
                        lambda e: e.wait_ge(gm_cat_ok, 6 * (group[-1] + 1)))

        def act_gm(act, c):
            for group in GROUPS:
                act_turn(act, c, act_hi, group, 6, None, False)

        def dve_gm_v(dve, c):
            dve_inv(dve, c, range(NT))
            dve.wait_ge(gm_set, 48)
            for t in range(NT):
                v = v_all[0:ROWS[t], t, :]
                dve.scalar_tensor_tensor(out=v, in0=v, scalar=inv[0:ROWS[t], t:t + 1], in1=gm_gain[0:ROWS[t], :],
                                         op0=ALU.mult, op1=ALU.mult).then_inc(gm_v, 1)

        def dve_gm(dve, c):
            dve.wait_ge(gm_setmm, 2)
            dve.tensor_copy(w_t[:, 0:4, :].rearrange("p g t -> p (g t)"), ps[:, 4, :]).then_inc(gm_gelu, 1)
            dve.tensor_copy(w_t[:, 4:6, :].rearrange("p g t -> p (g t)"), ps[:, 5, 0:2 * P]).then_inc(gm_gelu, 1)
            dve.tensor_copy(bias_t[:, :], ps[:, 6, 0:6]).then_inc(gm_gelu, 1)
            dve.wait_ge(gm_setmm, 4)
            dve.tensor_tensor(w_s[:, :, :].rearrange("p g (b t) -> p g b t", t=NQ),
                              ps[0:NS, 7, 0:6 * NQ].rearrange("p (g t) -> p g t", t=NQ).unsqueeze(2).broadcast_to([NS, 6, NB, NQ]),
                              same_batch.rearrange("p (b t) -> p b t", t=NQ).unsqueeze(1).broadcast_to([NS, 6, NB, NQ]),
                              ALU.mult).then_inc(gm_gelu, 1)
            dve.tensor_copy(bias_s[:, :], ps[0:NS, 6, 8:14]).then_inc(gm_gelu, 1)
            for group in GROUPS:
                for t in group:
                    dve.wait_ge(gm_mix, t + 1)
                    dve.wait_ge(gm_u[t % 4], 16 * (t // 4 + 1))
                    b = 4 + 2 * (t % 2)
                    bias = bias_t if t < NPT else bias_s
                    for g in range(6):
                        u = gm_cat[0:ROWS[t], t % 4, g * P:(g + 1) * P]
                        dve.scalar_tensor_tensor(out=u, in0=ps[0:ROWS[t], b + g // 4, (g % 4) * P:(g % 4) * P + P],
                                                 scalar=bias[0:ROWS[t], g:g + 1], in1=u, op0=ALU.add,
                                                 op1=ALU.mult).then_inc(gm_cat_ok, 1)
                dve_turn(dve, c, act_hi, act_lo, group, 6, None, False)

        BROWS = [(0, t) for t in range(NPT)] + [(1, t) for t in range(NPT - 1, -1, -1)]
        NR = len(BROWS)
        BGROUPS = [(r, k0, min(4, t + 1 - k0)) for r, (hh, t) in enumerate(BROWS) for k0 in range(0, t + 1, 4)]
        NG = len(BGROUPS)
        SEG_END = [max(n for n, (r, _, _) in enumerate(BGROUPS) if r // 4 == j) for j in range(4)]

        def row_groups(r):
            return [n for n, g in enumerate(BGROUPS) if g[0] == r]

        def pool_sb_out(pool):
            for name, c0 in (("sb_k", MIX), ("sb_v", 2 * MIX)):
                pool.dma_start(O[name + "_p"][0, 0].rearrange("t h d -> t (h d)"), proj[0:SEQ, c0:c0 + MIX]).then_inc(copied, 16)
                pool.dma_start(O[name + "_s"][0].rearrange("b t h d -> (b t) (h d)"), proj[SEQ:NTOK, c0:c0 + MIX]).then_inc(copied, 16)

        def pool_bp(pool):
            pool.wait_ge(ms_lo, 4)
            def load(dst, c0, i, done):
                pool.dma_start(dst[:, :, :], proj[0:SEQ, bass.ds(i * P + c0, P)].rearrange("(t p) f -> p t f", p=P)).then_inc(done, 16)

            load(sbq_raw, 0, 0, bp_ld)
            load(sbk_raw, MIX, 0, bp_ld)
            load(sb_v, 2 * MIX, 0, bp_v)
            pool.dma_start(bias12[:, :], A["sb_bias"][0].partition_broadcast(P)).then_inc(bp_set, 16)
            pool_masks(pool, [(tri01[:, :], 1.0), (head12[:, :], 1.0)], [
                (tri01[:, :], ALU.is_gt, 0.0, 0, [[-1, P]], 1),
                (head12[:, :], ALU.is_ge, 0.0, 0, [[-8, SH]], 1),
                (head12[:, :], ALU.is_ge, 0.0, 7, [[8, SH]], -1)])
            with pool.Fori(0, NPAIR - 1) as i:
                pool.wait_ge(bp_tr, i * 2 + 2)
                load(sbq_raw, 0, i + 1, bp_ld)
                load(sbk_raw, MIX, i + 1, bp_ld)
                pool.wait_ge(bp_av, i * NG + (NG + 2))
                load(sb_v, 2 * MIX, i + 1, bp_v)

        BP_MASKED = GM_MASKED + 3

        def pe_bp(pe):
            pe.wait_ge(ms_lo, 4)
            with pe.Fori(0, NPAIR) as i:
                pe.wait_ge(bp_ld, i * 32 + 32)
                pe.wait_ge(bp_lo, i * 4 + 2)
                for n, raw in enumerate((sbq_raw, sbk_raw)):
                    for t in range(NPT):
                        last = pe.transpose(ps[:, 4 + 2 * n + t // 4, (t % 4) * P:(t % 4) * P + P], raw[:, t, :], ident[:, :])
                    last.then_inc(bp_tr, 1)

                def scores(r):
                    hh, t = BROWS[r]
                    if r % NPT == 0:
                        pe.wait_ge(bp_q, i * 2 + (hh + 1))
                        pe.wait_ge(bp_k, i * 2 + (hh + 1))
                        pe.wait_ge(bp_b, i * 2 + (hh + 1))
                    pe.wait_ge(bp_sig, i * NR + (r + 1))
                    w = (t + 1) * P
                    for c in range(0, w, 512):
                        n = min(512, w - c)
                        last = pe.matmul(ps[:, 2 * (r % 2) + c // 512, 0:n], sb_q[0:65, hh, t * P:(t + 1) * P],
                                         sb_k[0:65, hh, c:c + n], start=True, stop=True)
                    last.then_inc(bp_z, 1)

                def turn(n):
                    r, k0, nk = BGROUPS[n]
                    if n == 0:
                        pe.wait_ge(bp_q, i * 2 + 2)
                        pe.wait_ge(bp_k, i * 2 + 2)
                    if k0 == 0:
                        pe.wait_ge(bp_a, i * NR + (r + 1))
                    for j in range(nk):
                        last = pe.transpose(ps[:, 4 + n % 2, j * P:(j + 1) * P], brk[:, r % 3, (k0 + j) * P:(k0 + j + 1) * P], ident[:, :])
                    last.then_inc(bp_t, 1)

                def use(n):
                    r, k0, nk = BGROUPS[n]
                    hh, t = BROWS[r]
                    if n == 0:
                        pe.wait_ge(bp_v, i * 16 + 16)
                    if r % 4 == 0 and k0 == 0:
                        pe.wait_ge(bp_lo, i * 4 + (r // 4 + 1))
                    pe.wait_ge(bp_at, i * NG + (n + 1))
                    for j in range(nk):
                        last = pe.matmul(ps[0:HD, 6 + (r // 4) % 2, (t % 4) * P:(t % 4) * P + P],
                                         sb_v[:, k0 + j, hh * HD:(hh + 1) * HD], brk_t[:, n % 2, j * P:(j + 1) * P],
                                         start=(k0 + j == 0), stop=(k0 + j == t), skip_group_check=True)
                    last.then_inc(bp_av, 1)

                for r in range(NR + 2):
                    if r < NR:
                        scores(r)
                    if r >= 2:
                        for n in row_groups(r - 2):
                            turn(n)
                            if n:
                                use(n - 1)
                use(NG - 1)

        def head_rows(tile, hh, i, r0):
            return tile[hh * HD:(hh + 1) * HD, bass.ds(i, 1), r0 * P:r0 * P + 512].rearrange("p a c -> p (a c)")

        def segment(j):
            return j // 2, (0, 4, 4, 0)[j], 6 + j % 2

        def act_bp(act):
            with act.Fori(0, NPAIR) as i:
                act.wait_ge(bp_tr, i * 2 + 1)
                for hh in range(2):
                    act.activation(sb_q[0:HD, hh, :], ps[hh * HD:(hh + 1) * HD, 4:6, :].rearrange("p a b -> p (a b)"),
                                   ACT.Copy, scale=HD ** -0.5).then_inc(bp_q, 1)

                def copy_out(j):
                    hh, t0, bank = segment(j)
                    act.wait_ge(bp_av, i * NG + (SEG_END[j] + 3))
                    act.activation(head_rows(act_hi, hh, i, t0), ps[0:HD, bank, :], ACT.Copy).then_inc(bp_hi, 1)

                for r in range(NR + 2):
                    if r < NR:
                        w = (BROWS[r][1] + 1) * P
                        act.wait_ge(bp_z, i * NR + (r + 1))
                        z = ps[:, 2 * (r % 2):2 * (r % 2) + 2, :].rearrange("p a b -> p (a b)")
                        act.activation(brk[:, r % 3, 0:w], z[:, 0:w], ACT.Sigmoid).then_inc(bp_sig, 1)
                    if r >= 2:
                        for n in row_groups(r - 2):
                            nk = BGROUPS[n][2]
                            act.wait_ge(bp_t, i * NG + (n + 1))
                            act.wait_ge(bp_av, i * NG + (n + 1))
                            act.activation(brk_t[:, n % 2, 0:nk * P], ps[:, 4 + n % 2, 0:nk * P], ACT.Copy).then_inc(bp_at, 1)
                            if n >= 2 and n - 2 in SEG_END:
                                copy_out(SEG_END.index(n - 2))
                copy_out(3)

        def dve_bp(dve):
            dve.wait_ge(ms_lo, 4)
            dve.memset(sb_k[HD:HD + 1, :, :], 1.0).then_inc(bp_one, 1)
            dve.memset(left[:, SEQ:SEQ + 1], 1.0).then_inc(bp_one, 1)
            dve.memset(zero1[:, :], 0.0).then_inc(bp_one, 1)
            dve.wait_ge(bp_one, 3)
            dve.wait_ge(bp_set, 16)
            dve.wait_ge(masked, BP_MASKED)
            with dve.Fori(0, NPAIR) as i:
                dve.wait_ge(bp_tr, i * 2 + 2)
                for hh in range(2):
                    dve.tensor_copy(sb_k[0:HD, hh, :], ps[hh * HD:(hh + 1) * HD, 6:8, :].rearrange("p a b -> p (a b)")).then_inc(bp_k, 1)
                    dve.tensor_scalar(sb_q[HD:HD + 1, hh, :], sb_k[HD:HD + 1, hh, :], bias12[HD:HD + 1, bass.ds(i * 2 + hh, 1)],
                                      None, ALU.mult).then_inc(bp_b, 1)

                def copy_out(j):
                    hh, t0, bank = segment(j)
                    dve.wait_ge(bp_hi, i * 4 + (j + 1))
                    dve.tensor_tensor(head_rows(act_lo, hh, i, t0), ps[0:HD, bank, :], head_rows(act_hi, hh, i, t0).bitcast(F32),
                                      ALU.subtract).then_inc(bp_lo, 1)

                for r in range(NR):
                    t = BROWS[r][1]
                    w = (t + 1) * P
                    s = brk[:, r % 3, 0:w]
                    c = left[:, SEQ - w:SEQ]
                    dve.wait_ge(bp_sig, i * NR + (r + 3))
                    d = brk[:, r % 3, t * P:w]
                    dve.tensor_tensor(d, d, tri01[:, :], ALU.mult).then_inc(bp_msk, 1)
                    dve.wait_ge(bp_msk, i * NR + (r + 1))
                    dve.tensor_scalar(c, s, -1.0, 1.0, ALU.mult, ALU.add).then_inc(bp_keep, 1)
                    dve.wait_ge(bp_keep, i * NR + (r + 1))
                    dve.tensor_tensor_scan(c[:, ::-1], c[:, ::-1], zero1[:, 0:1].broadcast_to([P, w]), 1.0, ALU.mult,
                                           ALU.add).then_inc(bp_left, 1)
                    dve.wait_ge(bp_left, i * NR + (r + 1))
                    dve.tensor_tensor(s, s, left[:, SEQ - w + 1:SEQ + 1], ALU.mult).then_inc(bp_a, 1)
                    dve.wait_ge(bp_a, i * NR + (r + 1))
                    done = [j for j in range(4) if r >= 2 and BGROUPS[SEG_END[j]][0] == r - 3]
                    for j in done:
                        copy_out(j)
                copy_out(3)

        NGR = PAGES // 2
        page_t = sb_at("page_t", [1, NB * PAGES], top + 64, I32)
        free_half = 1 - out0[1] % 2
        pv_raw = w_raw[:, :, :].rearrange("p k f -> p (k f)")[:, 0:2 * MIX].rearrange("p (j f) -> p j f", j=2)

        def pv(hi, g, j):
            if g % 2:
                return (pv_hi1 if hi else pv_lo1)[:, j, :]
            return (w_hi if hi else w_lo)[:, free_half].rearrange("p k f -> p (k f)")[:, j * MIX:(j + 1) * MIX]

        q_hi, q_lo = (w[:, free_half].rearrange("p k f -> p (k f)")[:, 2 * MIX:2 * MIX + NPAIR * NS]
                      .rearrange("p (a c) -> p a c", a=NPAIR) for w in (w_hi, w_lo))

        def gw(g):
            return 2 * P + (NQ if g == 0 else 0)

        def sp_bs(sp):
            sp.wait_ge(bs_set, 16)
            sp.wait_ge(bp_lo, 2 + 4 * NPAIR)
            sp.wait_ge(w_ok, out0[1] + 1)
            sp.dma_start(pk_raw[0:NS, 0, :], proj[SEQ:NTOK, 0:MIX]).then_inc(bs_in, 16)
            sp.dma_start(pk_raw[0:NS, 1, :], proj[SEQ:NTOK, MIX:2 * MIX]).then_inc(bs_in, 16)
            def pages(b, g):
                return [sp.value_load(page_t[0:1, bass.ds(b * PAGES + (PAGES - 2 - 2 * g + j), 1)]) for j in range(2)]

            def keys(b, g):
                page = pages(b, g)
                sp.wait_ge(bs_tr, b * (3 * NGR) + (3 * g + 3))
                for j in range(2):
                    sp.dma_start(pk_raw[:, 2 * (g % 2) + j, :],
                                 A["cache_sb_k"][0, bass.ds(page[j], 1)].rearrange("a t h d -> t (a h d)")).then_inc(bs_k[g % 2], 16)

            def values(b, g):
                page = pages(b, g)
                for j in range(2):
                    sp.wait_ge(bs_vl[j], b * NGR + (g + 1))
                    sp.dma_start(pv_raw[:, j, :],
                                 A["cache_sb_v"][0, bass.ds(page[j], 1)].rearrange("a t h d -> t (a h d)")).then_inc(bs_v[j], 16)

            def new_values(b):
                sp.dma_start(v_new[:, :], proj[bass.ds(b * NQ + SEQ, NQ), 2 * MIX:3 * MIX]).then_inc(bs_vn, 16)

            def batch(b, first_batch, last_batch):
                for g in range(NGR):
                    values(b, g)
                    if g + 2 < NGR:
                        keys(b, g + 2)
                    elif not last_batch:
                        keys(b + 1, g + 2 - NGR)
                    if g == 4 and not last_batch:
                        sp.wait_ge(bs_av, b * NGR + 3)
                        new_values(b + 1)

            keys(0, 0)
            keys(0, 1)
            new_values(0)
            batches(sp, batch)

        def pool_bs(pool):
            pool.dma_start(page_t[:, :], A["page_table"].rearrange("b p -> (b p)").unsqueeze(0)).then_inc(bs_set, 16)
            with pool.Fori(0, NB) as b:
                for g in range(NGR):
                    pool.wait_ge(bs_vh, b * (2 * NGR) + (2 * g + 2))
                    pool.tensor_tensor(pv(False, g, 1), pv_raw[:, 1, :], pv(True, g, 1).bitcast(F32), ALU.subtract).then_inc(bs_vl[1], 1)

        def pe_bs(pe):
            pe.wait_ge(bs_in, 32)
            pe.wait_ge(bp_lo, 2 + 4 * NPAIR)
            for n in range(2):
                for a in range(NPAIR):
                    last = pe.transpose(ps[:, n, a * NS:(a + 1) * NS], pk_raw[0:NS, n, a * P:(a + 1) * P], ident[0:NS, 0:NS])
            last.then_inc(bs_tr, 6)
            pe.wait_ge(bs_q, 3)

            def turn_of(b, g, c):
                if c == 0:
                    pe.wait_ge(bs_k[g % 2], b * (16 * NGR) + 32 * (g // 2 + 1))
                for u in range(2):
                    for j in range(2):
                        a = 2 * c + u
                        last = pe.transpose(ps[:, c, (2 * u + j) * P:(2 * u + j + 1) * P],
                                            pk_raw[:, 2 * (g % 2) + j, a * P:(a + 1) * P], ident[:, :])
                last.then_inc(bs_tr, 1)

            def batch(b, first_batch, last_batch):

                def turn(g, c):
                    turn_of(b, g, c)

                def turn_next(c):
                    turn_of(b + 1, 0, c)

                def scores(g, c):
                    pe.wait_ge(bs_kl, b * (3 * NGR) + (3 * g + c + 1))
                    if g == 1 and c == 0 and not first_batch:
                        pe.wait_ge(bs_lo, b)
                    w = gw(g)
                    for a in (2 * c, 2 * c + 1):
                        last = mm3(pe, ps[0:96, 3 + g % 2, 0:w], qb_hi[:, a * 96:(a + 1) * 96], qb_lo[:, a * 96:(a + 1) * 96],
                                   pk_hi[:, a, 0:w], pk_lo[:, a, 0:w], a == 0, a == NPAIR - 1)
                    if c == 2:
                        last.then_inc(bs_z, 1)

                def turn_weights(g):
                    pe.wait_ge(bs_a, b * NGR + (g + 1))
                    for j in range(2):
                        last = pe.transpose(ps[:, 5, j * 96:(j + 1) * 96], s_brk[:, g % 2, j * P:(j + 1) * P], ident[0:96, 0:96])
                    if g == 0:
                        last = pe.transpose(ps[0:NQ, 5, 192:288], s_brk[:, 0, 2 * P:2 * P + NQ], ident[0:96, 0:96])
                    last.then_inc(bs_at, 1)

                def use(g):
                    pe.wait_ge(bs_al, b * NGR + (g + 1))
                    for j in range(2):
                        pe.wait_ge(bs_vl[j], b * NGR + (g + 2))
                    if g == 0:
                        pe.wait_ge(bs_vn, b * 16 + 16)
                    for j in range(2):
                        for c in range(2):
                            cols = slice(c * 384, (c + 1) * 384)
                            last = mm3(pe, ps[0:96, 6 + c, 0:384], at_hi[:, g % 2, j, :], at_lo[:, g % 2, j, :],
                                       pv(True, g, j)[:, cols], pv(False, g, j)[:, cols], g == 0 and j == 0,
                                       g == NGR - 1 and j == 1)
                    if g == 0:
                        for c in range(2):
                            last = pe.matmul(ps[0:96, 6 + c, 0:384], at_new[:, :], v_new[:, c * 384:(c + 1) * 384],
                                             start=False, stop=False)
                    last.then_inc(bs_av, 1)

                pe.wait_ge(bs_qb, b * 4 + 4)
                pe.wait_ge(bs_kn, b * 2 + 2)
                for g in range(NGR):
                    for c in range(3):
                        scores(g, c)
                        if g + 1 < NGR:
                            turn(g + 1, c)
                        elif not last_batch:
                            turn_next(c)
                        if g and c == 0:
                            turn_weights(g - 1)
                        if g == 0 and c == 1 and not first_batch:
                            outputs(b - 1)
                    if g:
                        use(g - 1)
                turn_weights(NGR - 1)
                use(NGR - 1)
                if last_batch:
                    outputs(b)

            def outputs(b):
                pe.wait_ge(bs_o, b * 2 + 2)
                for a in range(NPAIR):
                    last = pe.matmul(ps[:, 4, a * NQ:(a + 1) * NQ], s_out[:, a * P:(a + 1) * P], query_of[0:96, :],
                                     start=True, stop=True, skip_group_check=True)
                last.then_inc(bs_mt, 1)

            for c in range(3):
                turn_of(0, 0, c)
            batches(pe, batch)

        def batches(eng, batch):
            batch(0, True, False)
            with eng.Fori(1, NB - 1) as b:
                batch(b, False, False)
            batch(NB - 1, False, True)

        def act_bs(act):
            act.wait_ge(bs_tr, 6)
            act.activation(q_hi[:, :, :].rearrange("p a c -> p (a c)"), ps[:, 0, 0:NPAIR * NS], ACT.Copy,
                           scale=HD ** -0.5).then_inc(bs_q, 1)
            act.wait_ge(bs_n, NQ + 5)
            act.wait_ge(bs_q, 3)

            def keys_of(b, g, c):
                act.wait_ge(bs_tr, b * (3 * NGR) + (3 * g + c + 7))
                act.activation(pk_hi[:, 2 * c:2 * c + 2, 0:2 * P], ps[:, c, :].rearrange("p (u c) -> p u c", u=2),
                               ACT.Copy).then_inc(bs_kh, 1)

            def outputs(b):
                act.wait_ge(bs_mt, b + 1)
                act.activation(act_hi[:, 0:NPAIR, bass.ds(b * NQ + SEQ, NQ)],
                               ps[:, 4, 0:NPAIR * NQ].rearrange("p (a q) -> p a q", q=NQ), ACT.Copy).then_inc(bs_hi, 1)

            def batch(b, first_batch, last_batch):

                def keys(g, c):
                    keys_of(b, g, c)

                def values(g, j):
                    act.wait_ge(bs_v[j], b * (16 * NGR) + 16 * (g + 1))
                    act.wait_ge(bs_av, b * NGR + (g + 1))
                    act.activation(pv(True, g, j), pv_raw[:, j, :], ACT.Copy).then_inc(bs_vh, 1)

                def breaks(g):
                    w = gw(g)
                    act.wait_ge(bs_z, b * NGR + (g + 1))
                    act.activation(s_brk[:, g % 2, 0:w], ps[0:96, 3 + g % 2, 0:w], ACT.Sigmoid, bias=bias96[:, 0:1]).then_inc(bs_sig, 1)

                def weights(g):
                    act.wait_ge(bs_at, b * NGR + (g + 1))
                    act.activation(at_hi[:, g % 2, :, :].rearrange("p j c -> p (j c)"), ps[:, 5, 0:192], ACT.Copy).then_inc(bs_ah, 1)
                    if g == 0:
                        act.activation(at_new[:, :], ps[0:NQ, 5, 192:288], ACT.Copy).then_inc(bs_ah, 1)

                for hh in range(2):
                    rows = slice(hh * HD, (hh + 1) * HD)
                    act.activation(qb_hi[rows, :].rearrange("p (a c) -> p a c", c=112)[:, :, hh * NQ:(hh + 1) * NQ],
                                   q_hi[rows, :, bass.ds(b * NQ, NQ)].bitcast(F32), ACT.Copy).then_inc(bs_qb, 1)
                act.activation(pk_hi[:, :, 2 * P:2 * P + NQ], kn_t[:, :, bass.ds(b * NQ, NQ)], ACT.Copy).then_inc(bs_kn, 1)
                for g in range(NGR):
                    for c in range(3):
                        if g + 1 < NGR:
                            keys(g + 1, c)
                        elif not last_batch:
                            keys_of(b + 1, 0, c)
                        if g and c == 0:
                            weights(g - 1)
                        if c < 2:
                            values(g, c)
                        if c == 1:
                            if g == 0 and not first_batch:
                                outputs(b - 1)
                            breaks(g)
                weights(NGR - 1)
                if last_batch:
                    outputs(b)

            for c in range(3):
                keys_of(0, 0, c)
            batches(act, batch)

        def dve_bs(dve):
            dve.wait_ge(bp_lo, 2 + 4 * NPAIR)
            dve.memset(qb_hi[:, :].bitcast(F32), 0.0).then_inc(bs_n, 1)
            dve.memset(qb_lo[:, :].bitcast(F32), 0.0).then_inc(bs_n, 1)
            dve.memset(s_left[:, 0, gw(0):gw(0) + 1], 1.0).then_inc(bs_n, 1)
            dve.tensor_tensor(head_b[:, :], head12[:, :], bias12[0:96, :], ALU.mult).then_inc(bs_n, 1)
            dve.wait_ge(bs_n, 4)
            dve.tensor_reduce(bias96[:, :], head_b[:, :], AX_X, ALU.add).then_inc(bs_n, 1)
            dve.memset(new01[:, :], 0.0).then_inc(bs_n, 1)
            dve.wait_ge(bs_n, 6)
            for t in range(NQ - 1):
                dve.tensor_reduce(new01[:, t:t + 1], query_of[0:96, t + 1:NQ], AX_X, ALU.add).then_inc(bs_n, 1)
            dve.wait_ge(bs_n, NQ + 5)
            dve.wait_ge(bs_q, 1)
            dve.scalar_tensor_tensor(out=q_lo[:, :, :].rearrange("p a c -> p (a c)"), in0=ps[:, 0, 0:NPAIR * NS], scalar=HD ** -0.5,
                                     in1=q_hi[:, :, :].rearrange("p a c -> p (a c)").bitcast(F32), op0=ALU.mult,
                                     op1=ALU.subtract).then_inc(bs_q, 1)
            dve.tensor_copy(kn_t[:, :, :].rearrange("p a c -> p (a c)"), ps[:, 1, 0:NPAIR * NS]).then_inc(bs_q, 1)
            dve.wait_ge(bs_q, 3)

            def keys_of(b, g, c):
                dve.wait_ge(bs_kh, b * (3 * NGR) + (3 * g + c + 1))
                hi = pk_hi[:, 2 * c:2 * c + 2, 0:2 * P].bitcast(F32)
                dve.tensor_tensor(pk_lo[:, 2 * c:2 * c + 2, 0:2 * P], ps[:, c, :].rearrange("p (u c) -> p u c", u=2), hi,
                                  ALU.subtract).then_inc(bs_kl, 1)

            def own_heads(b):
                dve.wait_ge(bs_av, b * NGR + (NGR + 2))
                for c in range(2):
                    dve.tensor_tensor(s_out[:, c * 384:(c + 1) * 384].rearrange("p (h d) -> p h d", d=HD),
                                      ps[0:96, 6 + c, 0:384].rearrange("p (h d) -> p h d", d=HD),
                                      head12[:, 6 * c:6 * c + 6].unsqueeze(2).broadcast_to([96, 6, HD]),
                                      ALU.mult).then_inc(bs_o, 1)

            def outputs(b):
                dve.wait_ge(bs_hi, b + 1)
                cols = bass.ds(b * NQ + SEQ, NQ)
                dve.tensor_tensor(act_lo[:, 0:NPAIR, cols], ps[:, 4, 0:NPAIR * NQ].rearrange("p (a q) -> p a q", q=NQ),
                                  act_hi[:, 0:NPAIR, cols].bitcast(F32), ALU.subtract).then_inc(bs_lo, 1)

            def batch(b, first_batch, last_batch):

                def keys(g, c):
                    keys_of(b, g, c)

                def values(g):
                    dve.wait_ge(bs_vh, b * (2 * NGR) + (2 * g + 1))
                    dve.tensor_tensor(pv(False, g, 0), pv_raw[:, 0, :], pv(True, g, 0).bitcast(F32), ALU.subtract).then_inc(bs_vl[0], 1)

                def left_of(g):
                    w = gw(g)
                    n0 = b * NGR + (g + 1)
                    s = s_brk[:, g % 2, 0:w]
                    c = s_left[:, g % 2, 0:w]
                    before = s_left[:, 1 - g % 2, 0:1]
                    dve.wait_ge(bs_sig, n0)
                    if g == 0:
                        d = s_brk[:, 0, 2 * P:w]
                        dve.tensor_tensor(d, d, new01[:, :], ALU.mult).then_inc(bs_edge, 1)
                    else:
                        dve.tensor_copy(s_left[:, g % 2, w:w + 1], before).then_inc(bs_edge, 1)
                    dve.wait_ge(bs_edge, n0)
                    dve.tensor_scalar(c, s, -1.0, 1.0, ALU.mult, ALU.add).then_inc(bp_keep, 1)
                    dve.wait_ge(bp_keep, n0 + NPAIR * NR)
                    dve.tensor_tensor_scan(c[:, ::-1], c[:, ::-1], zero1[0:96, 0:1].broadcast_to([96, w]),
                                           before if g else 1.0, ALU.mult, ALU.add).then_inc(bp_left, 1)
                    dve.wait_ge(bp_left, n0 + NPAIR * NR)
                    dve.tensor_tensor(s, s, s_left[:, g % 2, 1:w + 1], ALU.mult).then_inc(bs_a, 1)
                    dve.wait_ge(bs_a, n0)

                def weights(g):
                    dve.wait_ge(bs_ah, b * (NGR + 1) + (g + 2))
                    dve.tensor_tensor(at_lo[:, g % 2, :, :].rearrange("p j c -> p (j c)"), ps[:, 5, 0:192],
                                      at_hi[:, g % 2, :, :].rearrange("p j c -> p (j c)").bitcast(F32), ALU.subtract).then_inc(bs_al, 1)

                for hh in range(2):
                    rows = slice(hh * HD, (hh + 1) * HD)
                    dve.tensor_copy(qb_lo[rows, :].rearrange("p (a c) -> p a c", c=112)[:, :, hh * NQ:(hh + 1) * NQ],
                                    q_lo[rows, :, bass.ds(b * NQ, NQ)].bitcast(F32)).then_inc(bs_qb, 1)
                dve.wait_ge(bs_kn, b * 2 + 1)
                dve.tensor_tensor(pk_lo[:, :, 2 * P:2 * P + NQ], kn_t[:, :, bass.ds(b * NQ, NQ)],
                                  pk_hi[:, :, 2 * P:2 * P + NQ].bitcast(F32), ALU.subtract).then_inc(bs_kn, 1)
                if not first_batch:
                    own_heads(b - 1)
                for g in range(NGR):
                    for c in range(3):
                        if g + 1 < NGR:
                            keys(g + 1, c)
                        elif not last_batch:
                            keys_of(b + 1, 0, c)
                        if g and c == 0:
                            weights(g - 1)
                        if c == 0:
                            values(g)
                        if c == 1:
                            if g == 0 and not first_batch:
                                outputs(b - 1)
                            left_of(g)
                weights(NGR - 1)
                if last_batch:
                    own_heads(b)
                    outputs(b)

            for c in range(3):
                keys_of(0, 0, c)
            batches(dve, batch)

        def wait_attended(eng, l):
            if l == 0:
                eng.wait_ge(turn_lo, TURN["gm"] + 18)
                eng.wait_ge(gm_out, 16)
            else:
                eng.wait_ge(in_st, IN_ST[1])
                eng.wait_ge(kv_out, 64)
                eng.wait_ge(kv_tr, 4)

        MQC = [2304, 1024]

        def pool_mq(pool):
            pool.wait_ge(gm_mix, 3)
            q0 = 2 * MIX
            pool.wait_ge(in_st, IN_ST[0])
            pool.dma_start(mq[:, 0:NPT, :], proj[0:SEQ, q0:q0 + MEMW].rearrange("(t p) f -> p t f", p=P)).then_inc(mq_ld, 16)
            pool.dma_start(mq[0:NS, NPT, :], proj[SEQ:NTOK, q0:q0 + MEMW]).then_inc(mq_ld, 16)

        def dve_first(dve, l):
            dve_kv_turn(dve, l)
            if l:
                dve_mq_norm(dve, l)

        def dve_mq_norm(dve, l):
            if l == 0:
                wait_attended(dve, l)
            dve.memset(mq[HD:P, NPT, :], 1.0).then_inc(mem_pad, 1)
            dve.wait_ge(mem_pad, l + 1)
            if l:
                dve.wait_ge(in_ev, CB + 9 * (IN_U[0] + 1))
            else:
                dve.wait_ge(mq_ld, 32)
            s0 = 5 * l
            dve.tensor_tensor(mq_sq[:, :, :], mq[:, :, :], mq[:, :, :], ALU.mult).then_inc(mq_step, 1)
            dve.wait_ge(mq_step, s0 + 1)
            dve.tensor_reduce(mq_stat[:, 0, :], mq_sq[:, :, :].rearrange("p t (h d) -> p (t h) d", d=HD), AX_X,
                              ALU.add).then_inc(mq_step, 1)
            dve.wait_ge(mq_root, l + 1)
            dve.reciprocal(mq_stat[:, 2, :], mq_stat[:, 1, :]).then_inc(mq_step, 1)
            dve.wait_ge(mq_step, s0 + 3)
            scale_heads(dve, 0, 2)
            if l:
                scale_heads(dve, 2, NT)

        def scale_heads(dve, t0, t1):
            heads = mq[:, t0:t1, :].rearrange("p t (h d) -> p (t h) d", d=HD)
            n = (t1 - t0) * MH
            dve.tensor_tensor(heads, heads, mq_stat[:, 2, t0 * MH:t1 * MH].unsqueeze(2).broadcast_to([P, n, HD]),
                              ALU.mult).then_inc(mq_step, 1)

        def dve_mq(dve, l):
            if l:
                wait_attended(dve, l)
            else:
                dve_mq_norm(dve, l)
            dve.wait_ge(mq_step, 5 * l + 4)
            gain = qk_gain[:, l, :].unsqueeze(1).broadcast_to([P, MH, HD])

            def scaled(t, h):
                if not (isinstance(t, int) and t < 2):
                    dve.wait_ge(mq_tr, t + (9 * l - 1))
                dve.tensor_tensor(mq_n[:, h, :].rearrange("p (h d) -> p h d", d=HD),
                                  mq[:, bass.ds(t, 1), :].rearrange("p a (h d) -> p (a h) d", d=HD), gain,
                                  ALU.mult).then_inc(mq_nm, 1)

            def largest(t, h):
                b = 2 + 2 * h
                dve.wait_ge(mq_s, t + (8 * l + 1))
                dve.tensor_reduce(sm_max[:, h, :], ps[:, b:b + 2, :].rearrange("p a (h m) -> p (a h) m", m=M), AX_X,
                                  ALU.max).then_inc(mq_mx, 1)
                dve.wait_ge(mq_mx, t * 2 + (16 * l + 1))
                dve.tensor_scalar(sm_max[:, h, :], sm_max[:, h, :], -HD ** -0.5, None, ALU.mult).then_inc(mq_mx, 1)

            def shares(t, h):
                dve.wait_ge(mq_ex, t * 4 + (32 * l + 4))
                dve.reciprocal(sm_inv[:, h, :], sm_sum[:, h, :]).then_inc(mq_pr, 1)
                dve.wait_ge(mq_pr, t * 2 + (16 * l + 1))
                dve.tensor_tensor(prob[:, h, :, :], prob[:, h, :, :],
                                  sm_inv[:, h, :].unsqueeze(2).broadcast_to([P, MH, M]), ALU.mult).then_inc(mq_pr, 1)

            def low(t, h):
                cols = bass.ds(t * P, P)
                dve.wait_ge(mq_hi, t + (8 * l + 1))
                dve.tensor_tensor(act_lo[:, NPAIR:KT, cols], ps[:, 1, 0:2 * P].rearrange("p (a c) -> p a c", c=P),
                                  act_hi[:, NPAIR:KT, cols].bitcast(F32), ALU.subtract).then_inc(mq_lo, 1)

            def body(t, h, ahead):
                if ahead >= 3:
                    scaled(t + 3, 1 - h)
                if ahead >= 1:
                    shares(t + 1, 1 - h)
                if ahead >= 2:
                    largest(t + 2, h)
                low(t, h)

            scaled(0, 0)
            scaled(1, 1)
            if l == 0:
                scale_heads(dve, 2, NT)
            dve.wait_ge(mq_step, 5 * l + 5)
            largest(0, 0)
            largest(1, 1)
            shares(0, 0)
            scaled(2, 0)
            mq_tiles(dve, body)

        def mq_tiles(eng, body):
            with eng.Fori(0, NPT // 2 - 2) as i:
                for h in range(2):
                    body(i * 2 + h, h, 3)
            for t in range(NPT - 4, NPT):
                body(t, t % 2, min(3, NPT - 1 - t))

        def act_mq_root(act, l):
            act.wait_ge(mq_step, 5 * l + 2)
            act.activation(mq_stat[:, 1, :], mq_stat[:, 0, :], ACT.Sqrt, scale=1.0 / HD, bias=eps_ap[:, 0:1]).then_inc(mq_root, 1)

        def act_mq(act, l):
            if l == 0:
                act_mq_root(act, l)

            def turned_q(t, h):
                act.wait_ge(mq_tr, t + (9 * l + 1))
                act.activation(mq_t[:, h, :, :].rearrange("p a c -> p (a c)"), ps[:, 0, 0:2 * P], ACT.Copy).then_inc(mq_tc, 1)

            def exps(t, h):
                act.wait_ge(mq_mx, t * 2 + (16 * l + 2))
                for hd in range(MH):
                    act.activation(prob[:, h, hd, :], ps[:, 2 + 2 * h + hd // 2, (hd % 2) * M:(hd % 2 + 1) * M], ACT.Exp,
                                   bias=sm_max[:, h, hd:hd + 1], scale=HD ** -0.5,
                                   accum_out=sm_sum[:, h, hd:hd + 1]).then_inc(mq_ex, 1)

            def body(t, h, ahead):
                act.wait_ge(mq_pt, t + (8 * l + 1))
                act.activation(prob_t[:, h].rearrange("p a h c -> p a (h c)"), ps[:, 6:8, :], ACT.Copy).then_inc(mq_pc, 1)
                if ahead >= 3:
                    turned_q(t + 3, 1 - h)
                if ahead >= 2:
                    exps(t + 2, h)
                act.wait_ge(mq_av, t + (8 * l + 1))
                act.activation(act_hi[:, NPAIR:KT, bass.ds(t * P, P)], ps[:, 1, 0:2 * P].rearrange("p (a c) -> p a c", c=P),
                               ACT.Copy).then_inc(mq_hi, 1)

            for h in range(2):
                turned_q(h, h)
            for h in range(2):
                exps(h, h)
            turned_q(2, 0)
            mq_tiles(act, body)

        def pe_mq(pe, l):
            pe.wait_ge(kv_ok, 8 * (l + 1))
            pe.wait_ge(in_ev, CB + 9 * (IN_U[0] + l * IN_U[1]))

            def turn_q(t, h):
                pe.wait_ge(mq_nm, t + (9 * l + 1))
                if not (isinstance(t, int) and t == 0):
                    pe.wait_ge(mq_tc, t + 9 * l)
                for a in range(2):
                    last = pe.transpose(ps[:, 0, a * P:(a + 1) * P], mq_n[:, h, a * P:(a + 1) * P], ident[:, :])
                last.then_inc(mq_tr, 1)

            def scores(t, h):
                pe.wait_ge(mq_tc, t + (9 * l + 1))
                for a in range(2):
                    last = pe.matmul(ps[:, 2 + 2 * h + a, :], mq_t[:, h, a, :], mk_bd[:, a, :], start=True, stop=True)
                last.then_inc(mq_s, 1)

            def body(t, h, ahead):
                pe.wait_ge(mq_pr, t * 2 + (16 * l + 2))
                for m in range(2):
                    for hd in range(MH):
                        last = pe.transpose(ps[:, 6 + m, hd * P:(hd + 1) * P], prob[:, h, hd, m * P:(m + 1) * P], ident[:, :])
                last.then_inc(mq_pt, 1)
                if ahead >= 2:
                    scores(t + 2, h)
                if ahead >= 3:
                    turn_q(t + 3, 1 - h)
                pe.wait_ge(mq_pc, t + (8 * l + 1))
                pe.wait_ge(mq_lo, t + (8 * l + 2))
                for a in range(2):
                    for n in range(4):
                        hd, m = 2 * a + n // 2, n % 2
                        last = pe.matmul(ps[:, 1, a * P:(a + 1) * P], mv_pad[:, m, hd, :], prob_t[:, h, m, hd, :],
                                         start=(n == 0), stop=(n == 3), skip_group_check=True)
                last.then_inc(mq_av, 1)

            for h in range(2):
                turn_q(h, h)
                scores(h, h)
            turn_q(2, 0)
            mq_tiles(pe, body)
            pe.wait_ge(mq_lo, 2 + 8 * (l + 1))

        def sp_ms(sp, l):
            def load(dst, name, gr):
                for b in range(4):
                    sp.dma_start(dst[:, b], A[name][l, 4 * gr + b].rearrange("(t p) h d -> p t (h d)", p=P)).then_inc(ms_ld[gr], 16)

            sp.wait_ge(mq_step, 5 * l + 2)
            load(mkc, "cache_mem_k", 0)
            sp.wait_ge(in_st, IN_ST[l])
            load(mvc[0], "cache_mem_v", 0)
            sp.wait_ge(mq_nm, 9 * l + 9)
            load(mvc[1], "cache_mem_v", 1)
            sp.wait_ge(ms_tr, 8 * l + 4)
            load(mkc, "cache_mem_k", 1)

        def dve_ms(dve, l):
            gain = qk_gain[0:NS, l, :].unsqueeze(1).broadcast_to([NS, MH, HD])
            dve.tensor_tensor(mq_n[0:NS, 0, :].rearrange("p (h d) -> p h d", d=HD),
                              mq[0:NS, NPT, :].rearrange("p (h d) -> p h d", d=HD), gain, ALU.mult).then_inc(mq_nm, 1)
            dve.memset(mq_bd[:, :], 0.0).then_inc(ms_q, 1)
            dve.tensor_tensor(pick[:, :, :], batch_of[:, :].unsqueeze(2).broadcast_to([P, 4, NQ]),
                              query_of[:, :].unsqueeze(1).broadcast_to([P, 4, NQ]), ALU.mult).then_inc(ms_q, 1)
            dve.wait_ge(mq_tc, 9 * l + 9)
            for gr in range(2):
                G = 2 * l + gr
                if gr:
                    dve.wait_ge(ms_s, G)
                dve.wait_ge(ms_q, 10 * l + 2 + 4 * gr)
                for a in range(2):
                    for hh in range(2):
                        rows = slice(hh * HD, (hh + 1) * HD)
                        c = a * P + (2 * a + hh) * NQ
                        dve.tensor_copy(mq_bd[rows, :].rearrange("p (b c) -> p b c", c=288)[:, :, c:c + NQ],
                                        mq_t[rows, 0, a, gr * 32:gr * 32 + 32].rearrange("p (b q) -> p b q", q=NQ)).then_inc(ms_q, 1)
                s0 = 4 * G
                dve.wait_ge(ms_s, G + 1)
                dve.tensor_reduce(sm_max[:, 0, 0:1], ps[:, 4, 0:M], AX_X, ALU.max).then_inc(ms_step, 1)
                dve.wait_ge(ms_step, s0 + 1)
                dve.tensor_scalar(sm_max[:, 0, 0:1], sm_max[:, 0, 0:1], -HD ** -0.5, None, ALU.mult).then_inc(ms_step, 1)
                dve.wait_ge(ms_ex, G + 1)
                dve.reciprocal(sm_inv[:, 0, 0:1], sm_sum[:, 0, 0:1]).then_inc(ms_step, 1)
                dve.wait_ge(ms_step, s0 + 3)
                dve.tensor_scalar(prob_s[:, :], prob_s[:, :], sm_inv[:, 0, 0:1], None, ALU.mult).then_inc(ms_step, 1)
                dve.wait_ge(ms_av, G + 1)
                dve.tensor_tensor(ms_out[:, :].rearrange("p (h d) -> p h d", d=HD),
                                  ps[:, 6, 0:MEMW].rearrange("p (h d) -> p h d", d=HD),
                                  head_of[:, :].unsqueeze(2).broadcast_to([P, MH, HD]), ALU.mult).then_inc(ms_ok, 1)
                dve.wait_ge(ms_hi, G + 1)
                cols = slice(SEQ + 32 * gr, SEQ + 32 * gr + 32)
                dve.tensor_tensor(act_lo[:, NPAIR:KT, cols], ps[:, 7, 0:64].rearrange("p (a c) -> p a c", c=32),
                                  act_hi[:, NPAIR:KT, cols].bitcast(F32), ALU.subtract).then_inc(ms_lo, 1)

        def act_ms(act, l):
            act.wait_ge(mq_tr, 9 * l + 9)
            act.activation(mq_t[:, 0, :, 0:NS], ps[:, 0, 0:2 * NS].rearrange("p (a c) -> p a c", c=NS), ACT.Copy).then_inc(mq_tc, 1)
            for gr in range(2):
                G = 2 * l + gr
                if gr:
                    act.wait_ge(ms_s, G)
                for b in range(4):
                    act.wait_ge(ms_tr, 4 * G + b + 1)
                    act.activation(mkc_t[:, b, :, :].rearrange("p a m -> p (a m)"), ps[:, b, :], ACT.Copy).then_inc(ms_tc, 1)
                act.wait_ge(ms_step, 4 * G + 2)
                act.activation(prob_s[:, :], ps[:, 4, 0:M], ACT.Exp, bias=sm_max[:, 0, 0:1], scale=HD ** -0.5,
                               accum_out=sm_sum[:, 0, 0:1]).then_inc(ms_ex, 1)
                act.wait_ge(ms_pt, G + 1)
                act.activation(prob_st[:, :, :].rearrange("p a c -> p (a c)"), ps[:, 5, 0:2 * P], ACT.Copy).then_inc(ms_pc, 1)
                act.wait_ge(ms_mt, G + 1)
                cols = slice(SEQ + 32 * gr, SEQ + 32 * gr + 32)
                act.activation(act_hi[:, NPAIR:KT, cols], ps[:, 7, 0:64].rearrange("p (a c) -> p a c", c=32), ACT.Copy).then_inc(ms_hi, 1)

        def pe_ms(pe, l):
            pe.wait_ge(mq_nm, 9 * l + 9)
            for a in range(2):
                last = pe.transpose(ps[:, 0, a * NS:(a + 1) * NS], mq_n[0:NS, 0, a * P:(a + 1) * P], ident[0:NS, 0:NS])
            last.then_inc(mq_tr, 1)
            pe.wait_ge(mq_tc, 9 * l + 9)
            for gr in range(2):
                G = 2 * l + gr
                pe.wait_ge(ms_ld[gr], 128 * (l + 1))
                for b in range(4):
                    if gr:
                        pe.wait_ge(ms_tc, 4 * (G - 1) + b + 1)
                    for a in range(2):
                        for m in range(2):
                            last = pe.transpose(ps[:, b, (2 * a + m) * P:(2 * a + m + 1) * P], mkc[:, b, m, a * P:(a + 1) * P], ident[:, :])
                    last.then_inc(ms_tr, 1)
                pe.wait_ge(ms_q, 10 * l + 6 + 4 * gr)
                pe.wait_ge(ms_tc, 4 * G + 4)
                for b in range(4):
                    for a in range(2):
                        n = 2 * b + a
                        last = pe.matmul(ps[:, 4, 0:M], mq_bd[:, n * P:(n + 1) * P], mkc_t[:, b, a, :], start=(n == 0), stop=(n == 7))
                last.then_inc(ms_s, 1)
                pe.wait_ge(ms_step, 4 * G + 4)
                for m in range(2):
                    last = pe.transpose(ps[:, 5, m * P:(m + 1) * P], prob_s[:, m * P:(m + 1) * P], ident[:, :])
                last.then_inc(ms_pt, 1)
                pe.wait_ge(ms_pc, G + 1)
                for b in range(4):
                    for m in range(2):
                        last = pe.matmul(ps[32 * b:32 * b + 32, 6, 0:MEMW], prob_st[:, m, 32 * b:32 * b + 32], mvc[gr][:, b, m, :],
                                         start=(m == 0), stop=(m == 1))
                last.then_inc(ms_av, 1)
                pe.wait_ge(ms_ok, G + 1)
                for a in range(2):
                    last = pe.matmul(ps[:, 7, a * 32:(a + 1) * 32], ms_out[:, a * P:(a + 1) * P],
                                     pick[:, :, :].rearrange("p b q -> p (b q)"), start=True, stop=True, skip_group_check=True)
                last.then_inc(ms_mt, 1)

        def out_units(eng, l, body):
            with eng.Fori(0, OUT_U // 2) as i:
                for h in range(2):
                    body(i * 2 + h, i * 2 + (out0[l] + h), (out0[l] + h) % 2, i * 2 + (OUT_U * l + h))

        def pe_out_unit(pe, u, n, par, un):
            pe.wait_ge(w_ok, n + 1)
            for t in range(NT):
                pe.wait_ge(out_ev, un * 9 + (t + 1))
                for k in range(KT):
                    last = mm3(pe, ps[0:ROWS[t], t % CB, 0:UW], act_hi[:, k, tok_cols(t)], act_lo[:, k, tok_cols(t)],
                               w_hi[:, par, k, :], w_lo[:, par, k, :], k == 0, k == KT - 1)
                last.then_inc(w_used if t == NT - 1 else out_mm, 1)

        def dve_out_unit(dve, u, n, par, un):
            split_lo(dve, n + 1, 1 - par)
            for t in range(NT):
                if t == NT - 1:
                    dve.wait_ge(w_used, n + 1)
                else:
                    dve.wait_ge(out_mm, un * 8 + (t + 1))
                xs = x[0:ROWS[t], t, bass.ds(u * UW, UW)]
                dve.tensor_tensor(xs, xs, ps[0:ROWS[t], t % CB, 0:UW], ALU.add).then_inc(out_ev, 1)

        ROWCH = [(c * P, min(P, 16 * 2 * NFT - c * P)) for c in range(6)]

        def pool_past(pool, l):
            pool.wait_ge(ms_lo, 2 * (l + 1))
            v = A["state"][l].rearrange("b j (t f) -> (b j t) f", f=P)
            for c, (r0, nr) in enumerate(ROWCH):
                pool.dma_start(rows_st[0:nr, c, :], v[r0:r0 + nr, :]).then_inc(st_ld, 16)

        def pe_past(pe, l):
            for c, (r0, nr) in enumerate(ROWCH):
                pe.wait_ge(st_ld, 96 * (l + 1))
                if c >= 2:
                    pe.wait_ge(st_ev, 6 * l + c - 1)
                pe.transpose(ps[:, 4 + c % 2, 0:nr], rows_st[0:nr, c, :], ident[0:nr, 0:nr]).then_inc(st_mm, 1)

        def dve_past(dve, l):
            for c, (r0, nr) in enumerate(ROWCH):
                dve.wait_ge(st_mm, 6 * l + c + 1)
                dve.tensor_copy(past_t[:, :, :, :].rearrange("p b j t -> p (b j t)")[:, r0:r0 + nr], ps[:, 4 + c % 2, 0:nr]).then_inc(st_ev, 1)
            for t in (act_hi, act_lo):
                dve.memset(t[:, :, 0:2].bitcast(F32), 0.0).then_inc(pad_ok, 1)
                for k in range(KT):
                    dve.memset(t[:, k, SAMP0:SAMP0 + NB * EXT].rearrange("p (b t) -> p b t", t=EXT)[:, :, 0:2].bitcast(F32),
                               0.0).then_inc(pad_ok, 1)
                dve.memset(t[:, :, SAMP0 + NB * EXT:FW].bitcast(F32), 0.0).then_inc(pad_ok, 1)

        def ffn_units(eng, l, first, body):
            first()
            with eng.Fori(0, (NFT - 2) // 2) as i:
                for h in range(2):
                    body(i * 2 + (1 + h), (1 + h) % 2)
            body(NFT - 1, (NFT - 1) % 2)

        def wpar(l, par):
            return (ffn0[l] + par) % 2

        def pe_up(pe, l, u, par):
            n = u + ffn0[l]
            U = u + NFT * l
            pe.wait_ge(w_ok, n + 1)
            w = wpar(l, par)
            for h in range(2):
                if h == 0 and not (isinstance(u, int) and u < 2):
                    pe.wait_ge(dn_ev, U * 18 + (DC + 16 - 36))
                if not (isinstance(u, int) and u == 0):
                    pe.wait_ge(up_ev, U * 2 + (h - 1))
                for g in range(3):
                    for k in range(KT):
                        last = mm3(pe, ps[:, 3 * h + g, 0:TG], w_hi[:, w, k, h * P:(h + 1) * P],
                                   w_lo[:, w, k, h * P:(h + 1) * P], act_hi[:, k, g * TG:(g + 1) * TG],
                                   act_lo[:, k, g * TG:(g + 1) * TG], k == 0, k == KT - 1)
                last.then_inc(w_used if h else up_mm, 1)

        DN_BANK = [6, 7, 0, 1]

        def pe_down(pe, l, v, par, final=False):
            V = v + NFT * l
            pe.wait_ge(g_ok, V * 2 + 2)
            pe.wait_ge(d_ok, V + 1)
            if not final:
                pe.wait_ge(up_ev, V * 2 + 3)
            for t in range(NT):
                for c in range(2):
                    q = 2 * t + c
                    pe.wait_ge(dn_ev, V * 18 + max(q + 1, min(q + DC - 1, DC)))
                    last = mm3(pe, ps[0:ROWS[t], DN_BANK[(2 * t + c) % 4], :], g_hi[:, par, tok_cols(t)], g_lo[:, par, tok_cols(t)],
                               d_hi[:, c * 512:(c + 1) * 512], d_lo[:, c * 512:(c + 1) * 512], True, True)
                    last.then_inc(dn_mm, 1)

        def pe_ffn(pe, l):
            pe.wait_ge(pad_ok, 2 * (KT + 2) * (l + 1))
            def body(u, par):
                pe_up(pe, l, u, par)
                pe_down(pe, l, u - 1, 1 - par)
            ffn_units(pe, l, lambda: pe_up(pe, l, 0, 0), body)
            pe_down(pe, l, NFT - 1, (NFT - 1) % 2, True)

        def split_d_hi(act, l, v):
            V = v + NFT * l
            act.wait_ge(dr_ld, V * 16 + 16)
            if not (isinstance(v, int) and v == 0):
                act.wait_ge(dn_ev, V * 18 + DC)
            act.activation(d_hi[:, :], d_raw[:, :], ACT.Copy).then_inc(dh_ok, 1)

        def split_d_lo(dve, l, v):
            V = v + NFT * l
            dve.wait_ge(dh_ok, V + 1)
            dve.tensor_tensor(d_lo[:, :], d_raw[:, :], d_hi[:, :].bitcast(F32), ALU.subtract).then_inc(d_ok, 1)

        def coef(l, j, u, h):
            return cwb[:, l, j, bass.ds(u + NFT * h, 1)]

        def act_unit(act, l, u, par, first):
            U = u + NFT * l
            n = u + ffn0[l]
            if not first:
                split_d_hi(act, l, u - 1)
            if not (isinstance(n, int) and n + 1 >= N_UNITS):
                split_hi(act, n + 1, 1 - wpar(l, par))
            for h, (up, cv) in enumerate(((up_u, cv_u), (up_g, cv_g))):
                if h:
                    act.wait_ge(w_used, n + 1)
                else:
                    act.wait_ge(up_mm, U + 1)
                if not first:
                    act.wait_ge(tap_ok, U * 2 + (h - 1))
                    act.wait_ge(gate_ok if h else g_ok, U if h else U * 2)
                src = ps[:, 3 * h:3 * h + 3, 0:TG]
                act.activation(up[:, :].rearrange("p (g c) -> p g c", c=TG), src, ACT.Copy)
                act.activation(cv[:, :].rearrange("p (g c) -> p g c", c=TG), src, ACT.Identity, scale=coef(l, 2, u, h),
                               bias=coef(l, 3, u, h)).then_inc(up_ev, 1)
            act.wait_ge(cv_ok, U * 4 + 2)
            act.activation(cv_u[:, 2:FW], cv_u[:, 2:FW], ACT.Silu).then_inc(silu_ok, 1)
            act.wait_ge(gate_ok, U + 1)
            if not first:
                act.wait_ge(dn_ev, U * 18 + (DC - 18))
            act.activation(g_hi[:, par, 0:SEQ], cv_u[:, 2:2 + SEQ], ACT.Copy).then_inc(gh_ok, 1)
            act.activation(g_hi[:, par, SEQ:NTOK].rearrange("p (b t) -> p b t", t=NQ), samp_cv(cv_u), ACT.Copy).then_inc(gh_ok, 1)

        def samp_cv(t):
            return t[:, SAMP0:SAMP0 + NB * EXT].rearrange("p (b t) -> p b t", t=EXT)[:, :, 2:EXT]

        def dve_taps(dve, l, u, h, first):
            U = u + NFT * l
            up, cv = ((up_u, cv_u), (up_g, cv_g))[h]
            ft = bass.ds(u + NFT * h, 1)
            ext = up[:, SAMP0:SAMP0 + NB * EXT].rearrange("p (b t) -> p b t", t=EXT)
            dve.wait_ge(up_ev, U * 2 + (h + 1))
            dve.tensor_copy(ext[:, :, 0:2], past_t[:, :, :, ft].rearrange("p b j a -> p b (j a)")).then_inc(ins_ok, 1)
            dve.tensor_copy(tail_p[:, :, ft].rearrange("p j a -> p (j a)"), up[:, SEQ:SEQ + 2]).then_inc(tail_ok, 1)
            dve.tensor_copy(tail_s[:, :, :, ft].rearrange("p b j a -> p b (j a)"), ext[:, :, EXT - 2:EXT]).then_inc(tail_ok, 1)
            dve.wait_ge(ins_ok, U * 2 + (h + 1))
            dve.scalar_tensor_tensor(out=cv[:, 2:FW], in0=up[:, 1:FW - 1], scalar=coef(l, 1, u, h), in1=cv[:, 2:FW],
                                     op0=ALU.mult, op1=ALU.add).then_inc(cv_ok, 1)
            dve.wait_ge(cv_ok, U * 4 + (2 * h + 1))
            dve.scalar_tensor_tensor(out=cv[:, 2:FW], in0=up[:, 0:FW - 2], scalar=coef(l, 0, u, h), in1=cv[:, 2:FW],
                                     op0=ALU.mult, op1=ALU.add).then_inc(cv_ok, 1)
            dve.wait_ge(cv_ok, U * 4 + (2 * h + 2))
            dve.sem_inc(tap_ok, 1)

        ins_ok, tail_ok = sem("ins_ok"), sem("tail_ok")

        def dve_adds(dve, l, v):
            V = v + NFT * l
            for t in range(NT):
                for c in range(2):
                    dve.wait_ge(dn_mm, V * 18 + (2 * t + c + 1))
                    xs = x[0:ROWS[t], t, c * 512:(c + 1) * 512]
                    dve.tensor_tensor(xs, xs, ps[0:ROWS[t], DN_BANK[(2 * t + c) % 4], :], ALU.add).then_inc(dn_ev, 1)

        def dve_unit(dve, l, u, par, first):
            U = u + NFT * l
            n = u + ffn0[l]
            if not first:
                split_d_lo(dve, l, u - 1)
            if not (isinstance(n, int) and n + 1 >= N_UNITS):
                split_lo(dve, n + 1, 1 - wpar(l, par))
            dve_taps(dve, l, u, 0, first)
            if not first:
                dve_adds(dve, l, u - 1)
            dve_taps(dve, l, u, 1, first)
            dve.wait_ge(silu_ok, U + 1)
            dve.tensor_tensor(cv_u[:, 2:FW], cv_u[:, 2:FW], cv_g[:, 2:FW], ALU.mult).then_inc(gate_ok, 1)
            dve.wait_ge(gh_ok, U * 2 + 2)
            dve.tensor_tensor(g_lo[:, par, 0:SEQ], cv_u[:, 2:2 + SEQ], g_hi[:, par, 0:SEQ].bitcast(F32),
                              ALU.subtract).then_inc(g_ok, 1)
            dve.tensor_tensor(g_lo[:, par, SEQ:NTOK].rearrange("p (b t) -> p b t", t=NQ), samp_cv(cv_u),
                              g_hi[:, par, SEQ:NTOK].rearrange("p (b t) -> p b t", t=NQ).bitcast(F32),
                              ALU.subtract).then_inc(g_ok, 1)

        def act_ffn(act, l):
            ffn_units(act, l, lambda: act_unit(act, l, 0, 0, True), lambda u, par: act_unit(act, l, u, par, False))
            split_d_hi(act, l, NFT - 1)

        def dve_ffn(dve, l):
            ffn_units(dve, l, lambda: dve_unit(dve, l, 0, 0, True), lambda u, par: dve_unit(dve, l, u, par, False))
            split_d_lo(dve, l, NFT - 1)
            dve_adds(dve, l, NFT - 1)

        def pool_ffn(pool, l):
            pool.wait_ge(ms_lo, 2 * (l + 1))
            def load(v):
                if not (isinstance(v, int) and v == 0):
                    pool.wait_ge(d_ok, v + NFT * l)
                pool.dma_start(d_raw[:, :], A["w_down"][l][bass.ds(v * P, P), :]).then_inc(dr_ld, 16)
            load(0)
            with pool.Fori(0, NFT - 1) as i:
                load(i + 1)

        TAILS = [("p", 0, 2 * 2 * NFT)] + [("s", r0, nr) for r0, nr in ROWCH]

        TL_BANK = [6, 2]

        def tail_src(kind, r0, nr):
            t = tail_p[:, :, :].rearrange("p j t -> p (j t)") if kind == "p" else tail_s[:, :, :, :].rearrange("p b j t -> p (b j t)")
            return t[:, r0:r0 + nr]

        def pe_tails(pe, l):
            pe.wait_ge(tail_ok, 4 * NFT * (l + 1))
            for c, (kind, r0, nr) in enumerate(TAILS):
                if c >= 2:
                    pe.wait_ge(tl_ev, 7 * l + c - 1)
                pe.transpose(ps[0:nr, TL_BANK[l] + c % 2, 0:P], tail_src(kind, r0, nr), ident[:, :]).then_inc(tl_mm, 1)

        def dve_tails(dve, l):
            for c, (kind, r0, nr) in enumerate(TAILS):
                dve.wait_ge(tl_mm, 7 * l + c + 1)
                dve.tensor_copy(rows_st[0:nr, c, :], ps[0:nr, TL_BANK[l] + c % 2, 0:P]).then_inc(tl_ev, 1)

        def pool_tails(pool, l):
            for c, (kind, r0, nr) in enumerate(TAILS):
                pool.wait_ge(tl_ev, 7 * l + c + 1)
                dst = (O["conv_p"][l, 0].rearrange("j (t f) -> (j t) f", f=P) if kind == "p"
                       else O["conv_s"][l].rearrange("b j (t f) -> (b j t) f", f=P))
                pool.dma_start(dst[r0:r0 + nr, :], rows_st[0:nr, c, :]).then_inc(tl_out, 16)

        def x_ready(act, t, l, ffn):
            if ffn:
                act.wait_ge(out_ev, CB + 9 * OUT_U * (l + 1) - (NT - 1 - t))
            elif l:
                act.wait_ge(dn_ev, DC + 18 * NFT - 2 * (NT - 1 - t))
            else:
                act.wait_ge(x_ld[t // 4], 16)

        block = es.enter_context(nc.Block())

        @block.sync
        def _(sp):
            load_mem(sp)
            sp.wait_ge(set_ld, 16 * 9)
            for g in range(2):
                sp.dma_start(x[:, 4 * g:4 * g + 4, :],
                             A["x_prompt"][0, 512 * g:512 * g + 512, :].rearrange("(t p) d -> p t d", p=P)).then_inc(x_ld[g], 16)
            sp.dma_start(x[0:NS, NPT, :], A["x_sample"].rearrange("b t d -> (b t) d")).then_inc(x_ld[2], 16)
            for l in (0, 1):
                for u in range(KV_U):
                    load_cols(sp, kv0[l] + u, A["w_mem_kv"][l], u * UW)
                if l:
                    sp.wait_ge(dn_ev, DC + 18 * NFT)
                    load_mem(sp)
                if l:
                    load_cols(sp, in0[1], win[1], (IN_U[1] - 1) * UW)
                    in_rest(sp, l, lambda u, n, par, un: load_cols(sp, n, win[1], (u - 1) * UW))
                else:
                    for n, u in enumerate(ORDER0):
                        load_cols(sp, in0[0] + n, win[0], u * UW)
                load_cols(sp, out0[l], A["w_out"][l], 0)
                sp_ms(sp, l)
                if l:
                    sp_bs(sp)
                    sp.wait_ge(bs_vl[0], NB * NGR + 1)
                    sp.wait_ge(bs_vl[1], NB * NGR + 1)
                if l == 0:
                    sp.wait_ge(gm_v, NT)
                    sp.wait_ge(gm_gelu, 5)
                for u in range(1, OUT_U):
                    load_cols(sp, out0[l] + u, A["w_out"][l], u * UW)

                def load_up(u, par):
                    def half(h):
                        return A["w_up"][l][:, bass.ds(u * P + DFF * h, P)].rearrange("(k p) f -> p k f", p=P)
                    load_unit(sp, u + ffn0[l], half(0), half(1), w_raw[:, :, 0:P], w_raw[:, :, P:UW])

                ffn_units(sp, l, lambda: load_up(0, 0), load_up)
            for t0, t1 in ((0, 3), (3, 6), (6, 8)):
                sp.wait_ge(dn_ev, DC + 18 * (2 * NFT - 1) + 2 * t1)
                sp.dma_start(O["y_p"][0, t0 * P:t1 * P, :].rearrange("(t p) d -> p t d", p=P), x[:, t0:t1, :]).then_inc(y_out, 16)
            sp.wait_ge(dn_ev, DC + 18 * NFT * 2)
            sp.dma_start(O["y_s"].rearrange("b t d -> (b t) d"), x[0:NS, NPT, :]).then_inc(y_out, 16)
            sp.wait_ge(y_out, 64)
            sp.wait_ge(tl_out, 16 * 14)
            sp.wait_ge(kv_out, 64)
            sp.wait_ge(gm_out, 16)
            sp.wait_ge(copied, 64)
            sp.wait_ge(in_st, IN_ST[1])

        @block.gpsimd
        def _(pool):
            for s, v in ((bs_vl[0], 1), (bs_vl[1], 1), (in_ev, CB), (stage_free, 2), (out_ev, CB), (dn_ev, DC), (bp_sig, 2),
                         (bp_lo, 2), (bp_av, 2),
                         (bs_av, 2), (mq_lo, 2)):
                pool.sem_inc(s, v)
            pool.memset(eps_ap[:, :], EPS).then_inc(filled, 1)
            pool_masks.filled = 1
            pool_setup(pool)
            for l in (0, 1):
                if l:
                    pool_tails(pool, 0)
                pool_kv(pool, l)
                pool_in(pool, l)
                if l == 0:
                    pool_gm(pool)
                if l:
                    pool_sb_out(pool)
                    pool_bp(pool)
                    pool_bs(pool)
                    pool.wait_ge(bs_lo, NB)
                pool_past(pool, l)
                pool_ffn(pool, l)
                if l:
                    pool_tails(pool, l)

        @block.scalar
        def _(act):
            c = Counts()
            act_setup(act)
            act.wait_ge(filled, 1)
            act.wait_ge(set_ev, 1)
            for l in (0, 1):
                if l == 0:
                    act_mem(act, c, l)
                    split_hi(act, 0, 0)
                act_norm_x(act, c, 8 * l, False, lambda e, t: x_ready(e, t, l, False))
                if l:
                    act_mem(act, c, l)
                act_kv(act, c, l)
                act_in(act, c, l)
                if l == 0:
                    act_gm(act, c)
                act_mq(act, l)
                act_ms(act, l)
                if l:
                    act_bp(act)
                    act_bs(act)
                out_units(act, l, lambda u, n, par, un: split_hi(act, n + 1, 1 - par))
                act_norm_x(act, c, 16 + 8 * l, True, lambda e, t: x_ready(e, t, l, True))
                act_ffn(act, l)

        @block.vector
        def _(dve):
            c = Counts()
            dve_setup(dve)
            for l in (0, 1):
                if l == 0:
                    dve_mem(dve, c, l)
                    split_lo(dve, 0, 0)
                dve_norm_x(dve, c, 8 * l, False)
                if l:
                    dve_tails(dve, 0)
                    dve_mem(dve, c, l)
                dve_kv(dve, c, l)
                in_units(dve, l, lambda u, n, par, un: split_lo(dve, n + 1, 1 - par), lambda: dve_first(dve, l))
                if l == 0:
                    dve_gm_v(dve, c)
                if l == 0:
                    dve_gm(dve, c)
                dve_mq(dve, l)
                dve_ms(dve, l)
                if l:
                    dve_bp(dve)
                    dve_bs(dve)
                out_units(dve, l, lambda u, n, par, un: dve_out_unit(dve, u, n, par, un))
                dve_past(dve, l)
                dve_norm_x(dve, c, 16 + 8 * l, True)
                dve_ffn(dve, l)
            dve_tails(dve, 1)

        @block.tensor
        def _(pe):
            c = Counts()
            pe_setup(pe)
            for l in (0, 1):
                if l == 0:
                    pe_mem(pe, c, l)
                else:
                    pe.wait_ge(dn_ev, DC + 18 * NFT)
                pe_norm_x(pe, c)
                if l:
                    pe_tails(pe, 0)
                    pe_mem(pe, c, l)
                pe_kv(pe, c, l)
                in_units(pe, l, lambda u, n, par, un: pe_in_unit(pe, l, u, n, par, un * 9), lambda: pe_kv_turn(pe, c, l))
                if l == 0:
                    pe_gm(pe, c)
                pe_mq(pe, l)
                pe_ms(pe, l)
                if l:
                    pe_bp(pe)
                    pe_bs(pe)
                pe.wait_ge(turn_lo, c.turn)
                pe.wait_ge(mq_lo, 2 + 8 * (l + 1))
                pe.wait_ge(ms_lo, 2 * (l + 1))
                out_units(pe, l, lambda u, n, par, un: pe_out_unit(pe, u, n, par, un))
                pe_past(pe, l)
                pe_norm_x(pe, c)
                pe.wait_ge(turn_lo, c.turn)
                pe_ffn(pe, l)
            pe_tails(pe, 1)


_INS = ["x_prompt", "x_sample", "cache_mem_k", "cache_mem_v", "cache_sb_k", "cache_sb_v", "state_ffn_conv",
        "page_table", "mem_prompt", "norm_mix", "norm_ffn", "norm_mem", "w_in_a", "gm_v_norm", "gm_ws", "gm_bs",
        "w_in_b", "sb_bias", "w_mem_kv", "mem_q_norm", "mem_k_norm", "w_out", "w_up", "conv_w", "conv_b", "w_down"]
_OUTS = [("y_p", (1, SEQ, D)), ("y_s", (NB, NQ, D)), ("mem_k", (2, 1, M, MH, HD)), ("mem_v", (2, 1, M, MH, HD)),
         ("sb_k_p", (1, 1, SEQ, SH, HD)), ("sb_v_p", (1, 1, SEQ, SH, HD)), ("sb_k_s", (1, NB, NQ, SH, HD)),
         ("sb_v_s", (1, NB, NQ, SH, HD)), ("gm_v", (1, NB, NQ, MIX)), ("conv_p", (2, 1, 2, 2 * DFF)),
         ("conv_s", (2, NB, 2, 2 * DFF))]


def kernel(**inputs):
    import numpy as _np
    import concourse.bacc as _bacc
    from concourse import mybir as _mybir
    from concourse.bass_utils import run_bass_kernel_spmd as _run

    nc = _bacc.Bacc("TRN2", target_bir_lowering=False, num_devices=1)
    arrays, A, O = {}, {}, {}
    for name in _INS:
        a = _np.ascontiguousarray(inputs[name])
        arrays[f"in_{name}_dram"] = a
        A[name] = nc.dram_tensor(f"in_{name}_dram", a.shape, _mybir.dt.from_np(a.dtype), kind="ExternalInput").ap()
    A["state"] = A["state_ffn_conv"]
    for name, shape in _OUTS:
        O[name] = nc.dram_tensor(f"out_{name}_dram", shape, _mybir.dt.float32, kind="ExternalOutput").ap()
    scratch = nc.dram_tensor("projected", (NTOK, 3 * MIX + MEMW), _mybir.dt.float32, kind="Internal").ap()
    build(nc, A, O, scratch)
    r = _run(nc, [arrays], core_ids=[0])
    return tuple(r.results[0][f"out_{name}_dram"] for name, _ in _OUTS)
```
